# Optimizing a Trainium2 kernel written in Bass

```python
import math
import jax, jax.numpy as jnp
from jax import lax
import numpy as np

D_MODEL = 2048
BATCH = 1
SEQ = 256
DEPTH = 1
DEC_BATCH = 8
DEC_SEQ = 1
PAST_LEN = 2048
PAGE_SIZE = 128

S5_WIDTH = D_MODEL // 2
S5_GROUP = 16
S5_GROUPS = S5_WIDTH // S5_GROUP
S5_STATE = 64
HG_WIDTH = D_MODEL // 2
HG_HEAD_DIM = 128
HG_HEADS = HG_WIDTH // HG_HEAD_DIM
HG_CHUNK = 64
SPLIT_SIZES = (S5_WIDTH, HG_WIDTH, HG_WIDTH, HG_WIDTH, HG_WIDTH, D_MODEL, D_MODEL)
IN_COLS = sum(SPLIT_SIZES)
SPLIT_POINTS = tuple(np.cumsum(SPLIT_SIZES)[:-1].tolist())
N_GROUPS = 4
EXPERTS_PER_GROUP = 8
N_EXPERTS = N_GROUPS * EXPERTS_PER_GROUP
TOP_K = 2
D_EXPERT = 256
PLE_DIM = 256
DEEPNORM_ALPHA = (2 * DEPTH) ** 0.25
DEEPNORM_BETA = (8 * DEPTH) ** -0.25
LN_EPS = 1e-5
RMS_EPS = 1e-6
DT_MIN = 1e-3
DT_MAX = 1e-1

kernel_name = "s5_hgrn2_gated_parallel_hiermoe_decoder_step"

F32 = jnp.float32

def layer_norm(x, gain, bias):
    xf = x.astype(F32)
    mu = jnp.mean(xf, axis=-1, keepdims=True)
    var = jnp.mean(jnp.square(xf - mu), axis=-1, keepdims=True)
    return ((xf - mu) * lax.rsqrt(var + LN_EPS) * gain.astype(F32) + bias.astype(F32)).astype(x.dtype)

def rms_norm(x, gain):
    xf = x.astype(F32)
    return xf * lax.rsqrt(jnp.mean(jnp.square(xf), axis=-1, keepdims=True) + RMS_EPS) * gain.astype(F32)

def s5_mixer(u, s_re, s_im, lam_re, lam_im, log_dt, b_re, b_im, c_re, c_im, d_skip, w_glu):
    bt, t, _ = u.shape
    uf = u.astype(F32)
    dt = jnp.exp(log_dt.astype(F32))[:, None]
    lr = lam_re.astype(F32)
    li = lam_im.astype(F32)
    mag = jnp.exp(lr * dt)
    ab_re = mag * jnp.cos(li * dt)
    ab_im = mag * jnp.sin(li * dt)
    den = lr * lr + li * li
    nr = ab_re - 1.0
    zr = (nr * lr + ab_im * li) / den
    zi = (ab_im * lr - nr * li) / den
    bre = b_re.astype(F32)
    bim = b_im.astype(F32)
    bb_re = zr[..., None] * bre - zi[..., None] * bim
    bb_im = zr[..., None] * bim + zi[..., None] * bre
    ug = uf.reshape(bt, t, S5_GROUPS, S5_GROUP)
    bu_re = jnp.einsum('gnc,btgc->btgn', bb_re, ug)
    bu_im = jnp.einsum('gnc,btgc->btgn', bb_im, ug)
    sr = s_re.astype(F32)
    si = s_im.astype(F32)
    bu_re = bu_re.at[:, 0].add(ab_re * sr - ab_im * si)
    bu_im = bu_im.at[:, 0].add(ab_re * si + ab_im * sr)
    a_re = jnp.broadcast_to(ab_re, bu_re.shape)
    a_im = jnp.broadcast_to(ab_im, bu_im.shape)

    def combine(e1, e2):
        a1r, a1i, b1r, b1i = e1
        a2r, a2i, b2r, b2i = e2
        return (a2r * a1r - a2i * a1i,
                a2r * a1i + a2i * a1r,
                a2r * b1r - a2i * b1i + b2r,
                a2r * b1i + a2i * b1r + b2i)

    _, _, x_re, x_im = lax.associative_scan(combine, (a_re, a_im, bu_re, bu_im), axis=1)
    y = (jnp.einsum('gcn,btgn->btgc', c_re.astype(F32), x_re)
         - jnp.einsum('gcn,btgn->btgc', c_im.astype(F32), x_im))
    y = y.reshape(bt, t, S5_WIDTH) + d_skip.astype(F32) * uf
    y = jax.nn.gelu(y)
    y = y * jax.nn.sigmoid(y @ w_glu.astype(F32))
    return y.astype(u.dtype), x_re[:, -1], x_im[:, -1]

def gated_recurrence_blocks(q, k, v, logf, s0):
    bt, t, h, dk = q.shape
    c = min(HG_CHUNK, t)
    n_blocks = -(-t // c)
    pad = n_blocks * c - t
    if pad:
        pw = ((0, 0), (0, pad), (0, 0), (0, 0))
        q, k, v, logf = [jnp.pad(a, pw) for a in (q, k, v, logf)]

    def to_blocks(a):
        return jnp.moveaxis(a.reshape(bt, n_blocks, c, h, a.shape[-1]), 1, 0)

    causal = jnp.tril(jnp.ones((c, c), dtype=bool))[None, :, :, None, None]

    def step(s, blk):
        qc, kc, vc, gc = blk
        g_cum = jnp.cumsum(gc, axis=1)
        inter = jnp.einsum('bthk,bhkv->bthv', qc * jnp.exp(g_cum), s)
        diff = g_cum[:, :, None] - g_cum[:, None, :]
        decay = jnp.exp(jnp.where(causal, diff, -jnp.inf))
        scores = jnp.einsum('bthk,btshk,bshk->btsh', qc, decay, kc)
        intra = jnp.einsum('btsh,bshv->bthv', scores, vc)
        g_last = g_cum[:, -1]
        k_dec = kc * jnp.exp(g_last[:, None] - g_cum)
        s_new = jnp.exp(g_last)[..., None] * s + jnp.einsum('bshk,bshv->bhkv', k_dec, vc)
        return s_new, inter + intra

    s_fin, o = lax.scan(step, s0, (to_blocks(q), to_blocks(k), to_blocks(v), to_blocks(logf)))
    o = jnp.moveaxis(o, 0, 1).reshape(bt, n_blocks * c, h, v.shape[-1])[:, :t]
    return o, s_fin

def hgrn2_mixer(q_pre, f_pre, i_pre, g_pre, lb, s0, gn_gain):
    bt, t, _ = q_pre.shape
    shp = (bt, t, HG_HEADS, HG_HEAD_DIM)
    q = jax.nn.silu(q_pre.astype(F32)).reshape(shp)
    f = lb + (1.0 - lb) * jax.nn.sigmoid(f_pre.astype(F32))
    logf = jnp.log(f).reshape(shp)
    k = (1.0 - f).reshape(shp)
    v = i_pre.astype(F32).reshape(shp)
    o, s_new = gated_recurrence_blocks(q, k, v, logf, s0.astype(F32))
    o = rms_norm(o, gn_gain) * jax.nn.silu(g_pre.astype(F32).reshape(shp))
    return o.reshape(bt, t, HG_WIDTH).astype(q_pre.dtype), s_new

def hierarchical_moe(h, w_gr, b_gr, w_er, b_er, w_g, w_u, w_d):
    lead = h.shape[:-1]
    tok = h.reshape(-1, D_MODEL)
    grp_logits = (tok @ w_gr).astype(F32) + b_gr.astype(F32)
    grp_prob = jax.nn.softmax(grp_logits, axis=-1)
    grp_p, grp_idx = lax.top_k(grp_prob, 1)
    exp_logits = ((tok @ w_er).astype(F32) + b_er.astype(F32)).reshape(-1, N_GROUPS, EXPERTS_PER_GROUP)
    in_grp = jnp.einsum('mge,mg->me', exp_logits, jax.nn.one_hot(grp_idx[:, 0], N_GROUPS, dtype=F32))
    top_logit, top_local = lax.top_k(in_grp, TOP_K)
    top_w = jax.nn.softmax(top_logit, axis=-1) * grp_p
    top_e = grp_idx * EXPERTS_PER_GROUP + top_local
    combine = jnp.sum(jax.nn.one_hot(top_e, N_EXPERTS, dtype=F32) * top_w[..., None], axis=1)
    hid = jax.nn.silu(jnp.einsum('md,edf->mef', tok, w_g)) * jnp.einsum('md,edf->mef', tok, w_u)
    hid = hid * combine[:, :, None].astype(hid.dtype)
    out = jnp.einsum('mef,efd->md', hid, w_d)
    return out.reshape(*lead, D_MODEL)

def trunk_layer(x, p, s5_re, s5_im, hg_s, lb,
                w_in, lam_re, lam_im, log_dt, b_re, b_im, c_re, c_im, d_skip, w_glu, gn_gain,
                w_ba, w_bb, w_o, ln1_g, ln1_b,
                w_gr, b_gr, w_er, b_er, w_g, w_u, w_d,
                w_pp, w_pg, ln2_g, ln2_b):
    z = x @ w_in
    u_a, q_b, f_b, i_b, g_b, gate_a, gate_b = jnp.split(z, SPLIT_POINTS, axis=-1)
    y_a, s5_re_new, s5_im_new = s5_mixer(u_a, s5_re, s5_im, lam_re, lam_im, log_dt,
                                         b_re, b_im, c_re, c_im, d_skip, w_glu)
    y_b, hg_new = hgrn2_mixer(q_b, f_b, i_b, g_b, lb, hg_s, gn_gain)
    merged = jax.nn.sigmoid(gate_a) * (y_a @ w_ba) + jax.nn.sigmoid(gate_b) * (y_b @ w_bb)
    h = layer_norm(DEEPNORM_ALPHA * x + merged @ w_o, ln1_g, ln1_b)
    moe = hierarchical_moe(h, w_gr, b_gr, w_er, b_er, w_g, w_u, w_d)
    ple = jax.nn.sigmoid(h @ w_pg) * (p @ w_pp)
    x_new = layer_norm(DEEPNORM_ALPHA * h + moe + ple, ln2_g, ln2_b)
    return x_new, s5_re_new, s5_im_new, hg_new

def setup_inputs(seed: int = 0) -> dict:
    key = jax.random.key(seed)
    ks = iter(jax.random.split(key, 48))

    def nrm(shape, scale):
        return scale * jax.random.normal(next(ks), shape, F32)

    lam_im_base = jnp.pi * jnp.arange(S5_STATE, dtype=F32)
    return {
        "x_prompt": nrm((BATCH, SEQ, D_MODEL), 1.0),
        "x_sample": nrm((DEC_BATCH, DEC_SEQ, D_MODEL), 1.0),
        "p_prompt": nrm((DEPTH, BATCH, SEQ, PLE_DIM), 1.0),
        "p_sample": nrm((DEPTH, DEC_BATCH, DEC_SEQ, PLE_DIM), 1.0),
        "state_s5_re": nrm((DEPTH, DEC_BATCH, S5_GROUPS, S5_STATE), 0.5),
        "state_s5_im": nrm((DEPTH, DEC_BATCH, S5_GROUPS, S5_STATE), 0.5),
        "state_hgrn": nrm((DEPTH, DEC_BATCH, HG_HEADS, HG_HEAD_DIM, HG_HEAD_DIM), 0.5),
        "w_in": nrm((DEPTH, D_MODEL, IN_COLS), D_MODEL ** -0.5),
        "s5_lambda_re": -0.5 + nrm((DEPTH, S5_GROUPS, S5_STATE), 0.01),
        "s5_lambda_im": lam_im_base + nrm((DEPTH, S5_GROUPS, S5_STATE), 0.01),
        "s5_log_dt": jax.random.uniform(next(ks), (DEPTH, S5_GROUPS), F32,
                                        minval=math.log(DT_MIN), maxval=math.log(DT_MAX)),
        "s5_b_re": nrm((DEPTH, S5_GROUPS, S5_STATE, S5_GROUP), (2 * S5_GROUP) ** -0.5),
        "s5_b_im": nrm((DEPTH, S5_GROUPS, S5_STATE, S5_GROUP), (2 * S5_GROUP) ** -0.5),
        "s5_c_re": nrm((DEPTH, S5_GROUPS, S5_GROUP, S5_STATE), (2 * S5_STATE) ** -0.5),
        "s5_c_im": nrm((DEPTH, S5_GROUPS, S5_GROUP, S5_STATE), (2 * S5_STATE) ** -0.5),
        "s5_d": nrm((DEPTH, S5_WIDTH), 1.0),
        "s5_w_glu": nrm((DEPTH, S5_WIDTH, S5_WIDTH), S5_WIDTH ** -0.5),
        "hg_lower_bounds": 1.0 + nrm((DEPTH, HG_WIDTH), 0.3),
        "hg_norm_gain": 1.0 + nrm((DEPTH, HG_HEAD_DIM), 0.02),
        "w_branch_a": nrm((DEPTH, S5_WIDTH, D_MODEL), S5_WIDTH ** -0.5),
        "w_branch_b": nrm((DEPTH, HG_WIDTH, D_MODEL), HG_WIDTH ** -0.5),
        "w_out": nrm((DEPTH, D_MODEL, D_MODEL), DEEPNORM_BETA * D_MODEL ** -0.5),
        "ln1_gain": 1.0 + nrm((DEPTH, D_MODEL), 0.02),
        "ln1_bias": nrm((DEPTH, D_MODEL), 0.02),
        "w_group_router": nrm((DEPTH, D_MODEL, N_GROUPS), D_MODEL ** -0.5),
        "b_group_router": nrm((DEPTH, N_GROUPS), 0.01),
        "w_expert_router": nrm((DEPTH, D_MODEL, N_EXPERTS), D_MODEL ** -0.5),
        "b_expert_router": nrm((DEPTH, N_EXPERTS), 0.01),
        "w_exp_gate": nrm((DEPTH, N_EXPERTS, D_MODEL, D_EXPERT), D_MODEL ** -0.5),
        "w_exp_up": nrm((DEPTH, N_EXPERTS, D_MODEL, D_EXPERT), D_MODEL ** -0.5),
        "w_exp_down": nrm((DEPTH, N_EXPERTS, D_EXPERT, D_MODEL), DEEPNORM_BETA * D_EXPERT ** -0.5),
        "w_ple_proj": nrm((DEPTH, PLE_DIM, D_MODEL), DEEPNORM_BETA * PLE_DIM ** -0.5),
        "w_ple_gate": nrm((DEPTH, D_MODEL, D_MODEL), D_MODEL ** -0.5),
        "ln2_gain": 1.0 + nrm((DEPTH, D_MODEL), 0.02),
        "ln2_bias": nrm((DEPTH, D_MODEL), 0.02),
    }

def reference(x_prompt, x_sample, p_prompt, p_sample, state_s5_re, state_s5_im, state_hgrn,
              w_in, s5_lambda_re, s5_lambda_im, s5_log_dt, s5_b_re, s5_b_im, s5_c_re, s5_c_im,
              s5_d, s5_w_glu, hg_lower_bounds, hg_norm_gain, w_branch_a, w_branch_b, w_out,
              ln1_gain, ln1_bias, w_group_router, b_group_router, w_expert_router, b_expert_router,
              w_exp_gate, w_exp_up, w_exp_down, w_ple_proj, w_ple_gate, ln2_gain, ln2_bias):
    lb_soft = jax.nn.softmax(hg_lower_bounds.astype(F32), axis=0)
    lb_all = jnp.cumsum(lb_soft, axis=0) - lb_soft[0]

    bp = x_prompt.shape[0]
    zero_re = jnp.zeros((bp, S5_GROUPS, S5_STATE), F32)
    zero_hg = jnp.zeros((bp, HG_HEADS, HG_HEAD_DIM, HG_HEAD_DIM), F32)

    xp, xs = x_prompt, x_sample
    pr_re, pr_im, pr_hg, sm_re, sm_im, sm_hg = [], [], [], [], [], []
    for i in range(DEPTH):
        layer_w = (w_in[i], s5_lambda_re[i], s5_lambda_im[i], s5_log_dt[i], s5_b_re[i], s5_b_im[i],
                   s5_c_re[i], s5_c_im[i], s5_d[i], s5_w_glu[i], hg_norm_gain[i],
                   w_branch_a[i], w_branch_b[i], w_out[i], ln1_gain[i], ln1_bias[i],
                   w_group_router[i], b_group_router[i], w_expert_router[i], b_expert_router[i],
                   w_exp_gate[i], w_exp_up[i], w_exp_down[i], w_ple_proj[i], w_ple_gate[i],
                   ln2_gain[i], ln2_bias[i])
        xp, a_re, a_im, a_hg = trunk_layer(xp, p_prompt[i], zero_re, zero_re, zero_hg, lb_all[i], *layer_w)
        xs, b_re, b_im, b_hg = trunk_layer(xs, p_sample[i], state_s5_re[i], state_s5_im[i],
                                           state_hgrn[i], lb_all[i], *layer_w)
        pr_re.append(a_re); pr_im.append(a_im); pr_hg.append(a_hg)
        sm_re.append(b_re); sm_im.append(b_im); sm_hg.append(b_hg)

    return (xp, xs,
            jnp.stack(pr_re), jnp.stack(pr_im), jnp.stack(pr_hg),
            jnp.stack(sm_re), jnp.stack(sm_im), jnp.stack(sm_hg))


_drawn_inputs = setup_inputs


def setup_inputs(seed=0):
    import zlib

    import numpy as np

    out = dict(_drawn_inputs(seed))
    spreads = {}
    factors = {'s5_lambda_re': 16.411,
     'hg_norm_gain': 6.066,
     'b_group_router': 17.475,
     'b_expert_router': 6.472,
     'ln2_gain': 8.065,
     'ln2_bias': 8.131}
    for name, (base, spread) in spreads.items():
        noise = np.random.default_rng([zlib.crc32(name.encode()), seed]).standard_normal(out[name].shape)
        drawn = base * np.exp(spread * noise) if base else spread * noise
        out[name] = __import__('jax').numpy.asarray(drawn.astype(out[name].dtype))
    for name, factor in factors.items():
        out[name] = (out[name] * factor).astype(out[name].dtype)
    return out
```

```python
from contextlib import ExitStack

import numpy as np
import concourse.bass as bass
from concourse import mybir

F32 = mybir.dt.float32
F32R = mybir.dt.float32r
I32 = mybir.dt.int32
U32 = mybir.dt.uint32
ALU = mybir.AluOpType
ACT = mybir.ActivationFunctionType
AX_X = mybir.AxisListType.X

P = 128
D = 2048
KD = D // P
T = 256
NB = 8
NT = T + NB
HALF = 128
W = 1024
KW = W // P
NST = 32
HEADS = 8
HG = 4
GROUPS, EPG, FE = 4, 8, 256
SLOTS = 128
ROUNDS = 3
ALPHA = 2.0 ** 0.25
LN_EPS, RMS_EPS = 1e-5, 1e-6
TOK = [(0, 128), (128, 128), (256, 8)]
LEVELS = [1, 2, 4, 8, 16, 32, 64]

C_ID, C_LT, C_IO, C_MJ, C_MC, C_MB, C_CS = 0, 128, 256, 384, 388, 390, 392
C_RS = 408
C_MASK = C_RS + 512
C_END = C_MASK + 8 * 128


def shape_constants():
    r = np.arange(128)
    c = np.zeros((128, C_END), np.float32)
    c[:, C_ID:C_ID + 128] = np.eye(128)
    c[:, C_LT:C_LT + 128] = r[:, None] < r[None, :]
    c[:, C_IO:C_IO + 128] = r[None, :]
    c[:, C_MJ:C_MJ + 4] = (r[:, None] // 32) == np.arange(4)
    c[:, C_MC:C_MC + 2] = ((r[:, None] // 16) % 2) == np.arange(2)
    c[:, C_MB:C_MB + 2] = (r[:, None] // 64) == np.arange(2)
    for h in range(HG):
        c[:, C_CS + h * HG + h] = 1.0 / 128
        c[h, C_RS + h * 128:C_RS + (h + 1) * 128] = 1.0
    c[:, C_MASK:C_MASK + 128] = np.eye(128)
    for n, w in enumerate(LEVELS):
        s, t = r[:, None], r[None, :]
        c[:, C_MASK + (n + 1) * 128:C_MASK + (n + 2) * 128] = (
            (s // (2 * w) == t // (2 * w)) & (s // w % 2 == 0) & (t // w % 2 == 1))
    return c


RD = 4
RH = 2
BLK_IN, BLK_GLU, BLK_BA, BLK_BB, BLK_O, BLK_PP, BLK_PG = 0, 18, 20, 24, 28, 32, 36
N_IN, N_GLU, N_BA, N_BB, N_O, N_PP, N_PG, N_END = 0, 72, 76, 84, 92, 108, 110, 126
SPLIT_IN = 8


def is_split(n):
    return n < 4 * SPLIT_IN or n >= N_GLU


def split_count(n):
    return n if n <= 4 * SPLIT_IN else (4 * SPLIT_IN if n <= N_GLU else n - N_GLU + 4 * SPLIT_IN)


def build(nc, t, outs):
    base = (nc.sbuf_base + 63) // 64 * 64
    end = nc.sbuf_usable_end

    R_CONST = base
    R_XT = R_CONST + 17920
    R_Z = R_XT + KD * NT * 4
    ZSZ = KW * NT * 4
    R_GAB = R_Z + 5 * ZSZ
    R_RAW = R_GAB + 2 * KD * NT * 4
    R_HI = R_RAW + RD * 8192
    R_AR = R_HI + RH * 8192
    assert R_AR + 59520 <= end

    used_const = [R_CONST]

    def at(name, off, shape, dt=F32):
        return nc.alloc_sbuf_tensor_at(name, shape, dt, offset=off)

    def const(name, shape, dt=F32):
        size = 4
        for s in shape[1:]:
            size *= s
        off = used_const[0]
        used_const[0] = off + (size + 31) // 32 * 32
        assert used_const[0] <= R_XT, name
        return at(name, off, shape, dt)

    ident = const("ident", [P, 128])
    lowtri = const("lowtri", [P, 128])
    iota = const("iota", [P, 128])
    ones = const("ones", [P, 128])
    small = const("small", [P, 24])
    maskJ, maskC, maskB = small[:, 0:4], small[:, 4:6], small[:, 6:8]
    colsel = small[:, 8:24].rearrange("p (h m) -> p h m", h=HG)
    rowsel = const("rowsel", [HG, HG, 128])
    masks = const("masks", [P, 8, 128])
    dskip = const("dskip", [P, KW])
    gnorm = const("gnorm", [P, 1])
    lbraw = const("lbraw", [P, KW])
    lb = const("lb", [P, KW])
    oml = const("oml", [P, KW])
    sigtmp = const("sigtmp", [P, 2, NT])
    xs = const("xs", [P, 2, 256])
    fin = const("fin", [P, 2, NST])
    finT = const("finT", [NST, 2, 128])
    ab = const("ab", [P, 2, NST])
    mag = const("mag", [P, NST])
    stats = const("stats", [P, 3, 4, 6])
    mv = const("mv", [P, 3, 2])
    rstd = const("rstd", [P, 3])
    nmr = const("nmr", [P, 3])

    XT = at("XT", R_XT, [P, KD, NT])
    U = at("U", R_Z, [P, KW, NT])
    Q = at("Q", R_Z + ZSZ, [P, KW, NT])
    FG = at("FG", R_Z + 2 * ZSZ, [P, KW, NT])
    IV = at("IV", R_Z + 3 * ZSZ, [P, KW, NT])
    G = at("G", R_Z + 4 * ZSZ, [P, KW, NT])
    GA = at("GA", R_GAB, [P, KD, NT])
    GB = at("GB", R_GAB + KD * NT * 4, [P, KD, NT])
    XH = at("XH", R_GAB, [P, KD, NT], F32R)
    XL = at("XL", R_GAB + KD * NT * 4, [P, KD, NT], F32R)
    raw = at("raw", R_RAW, [P, RD, 2048])
    lo = at("lo", R_RAW, [P, RD, 2048], F32R)
    hi = at("hi", R_HI, [P, RH, 2048], F32R)

    xtok = at("xtok", R_AR, [P, 3, D])
    Pr = at("Pr", R_AR, [P, NST, HALF])
    Pi = at("Pi", R_AR + 16384, [P, NST, HALF])
    BBT = at("BBT", R_AR + 32768, [P, 2, KW, 128])
    CT = at("CT", R_AR + 40960, [P, 2, KW, 128])
    wA = at("wA", R_AR + 49152, [P, 2, T])
    wB = at("wB", R_AR + 51200, [P, 2, T])
    ws = at("ws", R_AR + 53248, [P, 2, T])
    xst = at("xst", R_AR + 55296, [P, 2, 2, T])
    o = R_Z + 3 * ZSZ
    braw = at("braw", o, [P, 2, NST, 16])
    craw = at("craw", o + 4096, [P, 2, KW, 64])
    o = R_Z + 4 * ZSZ
    yblk = at("yblk", o, [P, 2, NST, 32])
    o = R_Z + ZSZ
    ptmp = at("ptmp", o, [P, NST, 64])
    o = R_Z + 2 * ZSZ
    bbz = at("bbz", o, [P, 2, NST, 16])
    btmp = at("btmp", o + 4096, [P, NST, 16])
    par = at("par", o + 6144, [P, 16, NST])

    o = R_AR + 49152
    parnat = at("parnat", o, [NST, 3, 128])
    snat = at("snat", o + 1536, [P, 2, 2, 128])
    dtn = at("dtn", o + 3584, [NST, 2])
    sT = at("sT", o + 3616, [P, 2, 256])
    ublk = at("ublk", o + 5664, [P, KW, 4, NB])
    st1 = at("st1", o + 6688, [P, 256])
    st2 = at("st2", o + 7712, [P, 256])
    assert o + 8736 <= R_AR + 59392
    PP = at("PP", R_AR, [P, HG, T])
    SS = at("SS", R_AR + 4096, [P, HG, T])
    kt = at("kt", R_AR + 8192, [P, 2, HG, T])
    qt = at("qt", R_AR + 16384, [P, 2, HG, T])
    Sc = at("Sc", R_AR + 24576, [P, HG, 2, 128])
    kk = at("kk", R_AR + 28672, [P, HG, NT])
    ktok = at("ktok", R_AR + 32896, [P, 2, HG, 128])
    vtok = at("vtok", R_AR + 36992, [P, 2, HG, 128])
    S0 = at("S0", R_AR + 41088, [P, HG, 128])
    stS = at("stS", R_AR + 43136, [P, 2, NB, 128])
    sktok = at("sktok", R_AR + 51328, [NB, HG * 128])
    svtok = at("svtok", R_AR + 53376, [NB, HG * 128])
    svblk = at("svblk", R_AR + 55424, [NB, NB, 128])
    Sf = at("Sf", R_AR + 4096, [P, HG, 128])
    O4 = at("O4", R_AR + 8192, [P, HG, NT])
    sq = at("sq", R_AR + 12448, [P, HG, NT])
    rr = at("rr", R_AR + 24576, [HG, 2, NT])
    YGH = at("YGH", R_AR, [P, KW, NT], F32R)
    YGL = at("YGL", R_AR + ZSZ, [P, KW, NT], F32R)
    YAH = at("YAH", R_AR + 2 * ZSZ, [P, KW, NT], F32R)
    YAL = at("YAL", R_AR + 3 * ZSZ, [P, KW, NT], F32R)
    YBH = at("YBH", R_AR + 4 * ZSZ, [P, KW, NT], F32R)
    YBL = at("YBL", R_AR + 5 * ZSZ, [P, KW, NT], F32R)
    MH = at("MH", R_Z + ZSZ, [P, KD, NT], F32R)
    ML = at("ML", R_Z + 3 * ZSZ, [P, KD, NT], F32R)
    htok = at("htok", R_AR, [P, 3, D])
    ln1 = at("ln1", R_AR + 24576, [P, 2, D])
    wrr = at("wrr", R_AR + 40960, [P, KD, 36])
    wrh = at("wrh", R_AR + 43264, [P, KD, 36], F32R)
    wrl = at("wrl", R_AR + 45568, [P, KD, 36], F32R)
    rbias = at("rbias", R_AR + 47872, [P, 36])
    ptok = at("ptok", R_AR + 51200, [P, 3, 256])
    pTh = at("pTh", R_AR + 54272, [P, 2, NT], F32R)
    pTl = at("pTl", R_AR + 56384, [P, 2, NT], F32R)
    HTH = at("HTH", R_GAB, [P, KD, NT], F32R)
    HTL = at("HTL", R_GAB + KD * NT * 4, [P, KD, NT], F32R)
    PPT = at("PPT", R_Z + 3 * ZSZ, [P, KD, NT])
    atok = at("atok", R_Z, [P, 3, D])
    outg = at("outg", R_XT, [P, D])
    Sel = at("Sel", R_XT + 8192, [P, 3, GROUPS, SLOTS])
    SelT = at("SelT", R_XT + 14336, [P, 2, NT])
    hgh = at("hgh", R_AR + 24576, [P, 2, KD, SLOTS], F32R)
    hgl = at("hgl", R_AR + 40960, [P, 2, KD, SLOTS], F32R)
    XR = R_GAB
    mraw = [raw[:, 0], raw[:, 1], raw[:, 2], raw[:, 3],
            at("raw4", XR, [P, 2048])[:, :], at("raw5", XR + 8192, [P, 2048])[:, :]]
    mlo = [lo[:, 0], lo[:, 1], lo[:, 2], lo[:, 3],
           at("lo4", XR, [P, 2048], F32R)[:, :], at("lo5", XR + 8192, [P, 2048], F32R)[:, :]]
    mhi = [hi[:, 0], hi[:, 1], at("hi2", XR + 16384, [P, 2048], F32R)[:, :]]
    gsil = at("gsil", XR + 24576, [P, FE])
    hid = at("hid", XR + 25600, [P, FE])
    hidH = at("hidH", XR + 26624, [P, 2, SLOTS], F32R)
    hidL = at("hidL", XR + 27648, [P, 2, SLOTS], F32R)
    combg = at("combg", XR + 28672, [P, 2, EPG])
    ln2 = at("ln2", R_Z + 3 * ZSZ, [P, 2, D])
    logit = at("logit", R_AR + 48032, [P, 3, 36])
    lg8 = at("lg8", R_AR + 48480, [P, 3, 8])
    gmx = at("gmx", R_AR + 48576, [P, 3, 8])
    gix = at("gix", R_AR + 48672, [P, 3, 8], U32)
    gif = at("gif", R_AR + 48768, [P, 3, 8])
    ing = at("ing", R_AR + 48864, [P, 3, 8])
    emx = at("emx", R_AR + 48960, [P, 3, 8])
    eix = at("eix", R_AR + 49056, [P, 3, 8], U32)
    eif = at("eif", R_AR + 49152, [P, 3, 8])
    gex = at("gex", R_AR + 49248, [P, 3, 4])
    rsm = at("rsm", R_AR + 49312, [P, 3, 8])
    ctmp = at("ctmp", R_AR + 49408, [P, 3, 8])
    oh = const("oh", [P, 3, GROUPS])
    comb8 = const("comb8", [P, 3, EPG])
    rank = const("rank", [P, 3, GROUPS])
    flagf = const("flagf", [P, 2])
    flag = const("flag", [P, 1], I32)

    with ExitStack() as ctx:
        def sem(name):
            return ctx.enter_context(nc.semaphore(name))

        bank = [ctx.enter_context(nc.psum_tensor(f"bank{n}", [P, 512], F32)) for n in range(8)]

        s_const = sem("const_loaded")
        s_par = sem("s5_params_loaded")
        s_bc = sem("s5_bc_loaded")
        s_x = sem("x_loaded")
        s_vec = sem("vectors_loaded")
        s_ones = sem("ones_set")
        xh_done, xt_done = sem("x_high_done"), sem("x_split_done")
        landed = [sem(f"chunk_landed{s}") for s in range(RD)]
        hi_done, lo_done, chunk_used = sem("high_done"), sem("low_done"), sem("chunk_used")
        acc_ready = sem("tile_summed")
        acc_read = [sem(f"bank{m}_read") for m in range(4)]
        sig_ready, sig_used = sem("sigmoid_ready"), sem("sigmoid_used")
        misc_ready = sem("side_bank_ready")
        misc_read = [sem("side_bank6_read"), sem("side_bank7_read")]
        chain = sem("vector_chain")
        achain = sem("scalar_chain")
        dt_exp, dt_wide = sem("dt_exp"), sem("dt_wide")
        ang_ready, trig_done = sem("angle_ready"), sem("trig_done")
        abs_done = sem("abs_done")
        blk_ready = sem("block_forms_ready")
        bct_done = sem("bc_transposed_stored")
        ublk_ready = sem("sample_u_ready")
        xs_ready = sem("sample_state_ready")
        bu_ready, bu_read = sem("bu_ready"), sem("bu_read")
        xt_ready, xt_used = sem("s5_x_ready"), sem("s5_x_used")
        yt_ready, gelu_done = sem("y_ready"), sem("gelu_done")
        outT = sem("states_transposed")
        st_out = sem("stores_done")
        h_k, h_q, h_sc, h_scread = sem("hg_k_ready"), sem("hg_level_ready"), sem("hg_scores"), sem("hg_scores_read")
        h_tok, h_kts = sem("hg_tokens_stored"), sem("hg_k_decayed")
        h_s0, h_blk, h_st, h_new, h_o = (sem("hg_state0"), sem("hg_v_spread"), sem("hg_state_loaded"),
                                         sem("hg_state_new"), sem("hg_o_stored"))
        h_stq = [sem("hg_state_in0"), sem("hg_state_in1")]
        h_sto = [sem("hg_state_out0"), sem("hg_state_out1")]
        h_ms, h_sqrt, h_rstd, h_fin, h_outer = (sem("hg_ms"), sem("hg_sqrt"), sem("hg_rstd"), sem("hg_final"),
                                                sem("hg_o_used"))
        h_done = sem("hg_done")
        a_hi, a_lo = sem("act_high"), sem("act_low")
        a_raw = sem("act_raw")
        ln_ld, p_ld, r_ld, ln2_ld = sem("ln1_loaded"), sem("p_loaded"), sem("router_loaded"), sem("ln2_loaded")
        hpre, stat_done = sem("h_pre_ready"), sem("stats_taken")
        ln_var, ln_sq, ln_nmr, ln_norm, h_ready = (sem("variance"), sem("deviation"), sem("ln_scalars"),
                                                   sem("normalized"), sem("h_ready"))
        pt_hi, pt_lo = sem("p_high"), sem("p_low")
        ht_hi, ht_lo = sem("h_high"), sem("h_low")
        wr_hi, wr_lo = sem("router_high"), sem("router_low")
        r_log, r_exp, r_exp2 = sem("router_logits"), sem("group_exp"), sem("expert_exp")
        gm_neg, e_diff = sem("group_max"), sem("expert_diff")
        oh_ready = sem("groups_chosen")
        sel_ready = sem("selection_ready")
        flag_ready = sem("flag_ready")
        ple_ready = sem("ple_ready")
        selT_done, hg_hi, hg_lo, comb_done = (sem("selection_transposed"), sem("gathered_high"),
                                              sem("gathered_low"), sem("combine_gathered"))
        g_land = [sem(f"gate_up_landed{s}") for s in range(4)]
        d_land = [sem(f"down_landed{s}") for s in range(2)]
        g_hi, g_lo, g_used = sem("gate_up_high"), sem("gate_up_low"), sem("gate_up_used")
        d_hi, d_lo, d_used = sem("down_high"), sem("down_low"), sem("down_used")
        gu_ready, silu_done, hid_done = sem("gate_up_summed"), sem("silu_done"), sem("hidden_done")
        hidT_ready, hidT_hi, hidT_lo = sem("hidden_transposed"), sem("hidden_high"), sem("hidden_low")
        out_ready, outg_done, scat_done = sem("group_summed"), sem("group_stored"), sem("group_scattered")
        rounds_over = sem("rounds_over")
        f_var, f_sq, f_nmr, f_norm, f_out = (sem("final_variance"), sem("final_deviation"), sem("final_scalars"),
                                             sem("final_normalized"), sem("final_ready"))
        y_out = sem("y_stored")

        def chunk(n):
            def view(w, kq, cb, nk, nc_):
                return w[0, kq * nk * 128:(kq + 1) * nk * 128, cb * nc_:(cb + 1) * nc_].rearrange(
                    "(k p) n -> p k n", p=P)
            if n < N_GLU:
                return view(t["w_in"], n % 4, n // 4, 4, 512)
            if n < N_BA:
                return view(t["s5_w_glu"], (n - N_GLU) % 2, (n - N_GLU) // 2, 4, 512)
            if n < N_BB:
                return view(t["w_branch_a"], (n - N_BA) % 2, (n - N_BA) // 2, 4, 512)
            if n < N_O:
                return view(t["w_branch_b"], (n - N_BB) % 2, (n - N_BB) // 2, 4, 512)
            if n < N_PP:
                return view(t["w_out"], (n - N_O) % 4, (n - N_O) // 4, 4, 512)
            if n < N_PG:
                return view(t["w_ple_proj"], 0, n - N_PP, 2, 1024)
            return view(t["w_ple_gate"], (n - N_PG) % 4, (n - N_PG) // 4, 4, 512)

        def ahead_of(n):
            return {N_PP - 1: (N_PP, N_PP + 1), N_PP: (), N_END - 1: ()}.get(n, (n + 1,))

        s5_at = {}
        for tau in range(NST):
            c = 9 + 2 * tau if tau < 12 else 32 + (tau - 12) * 4 // 5
            s5_at.setdefault(c, []).append(tau)
        S5_END = 32 + 19 * 4 // 5 + 1
        hg_at = {}
        for n in range(32):
            hg_at.setdefault(S5_END + 1 + n * 22 // 32, []).append((n // 16, n % 16))
        misc = {}

        def side_read(eng, name):
            n = misc[name]
            eng.wait_ge(misc_read[n % 2], n // 2 + 1)

        def summed(eng, blk, m):
            if BLK_PP <= blk < BLK_PG:
                i, half = divmod(blk - BLK_PP, 2)
                if (half, m) == (1, 3):
                    eng.wait_ge(chunk_used, N_PP + i + 1)
                else:
                    eng.wait_ge(acc_ready, 3 * BLK_PP + 7 * i + 4 * half + m + 1)
                return
            if m < 3:
                eng.wait_ge(acc_ready, (3 * blk if blk < BLK_PP else 3 * BLK_PP + 14 + 3 * (blk - BLK_PG)) + m + 1)
                return
            for b0, n0, kqs in ((BLK_PG, N_PG, 4), (BLK_O, N_O, 4), (BLK_BB, N_BB, 2), (BLK_BA, N_BA, 2),
                                (BLK_GLU, N_GLU, 2), (BLK_IN, N_IN, 4)):
                if blk >= b0:
                    eng.wait_ge(chunk_used, n0 + kqs * (blk - b0 + 1))
                    return

        block = ctx.enter_context(nc.Block())

        @block.tensor
        def _(pe):
            def side(name):
                n = misc[name] = len(misc)
                if n >= 2:
                    pe.wait_ge(misc_read[n % 2], n // 2)
                return bank[6 + n % 2]

            def stored(name):
                side_read(pe, name)

            def mm(out, w, x, start, stop):
                return nc.tensor.matmul(out, w, x, start=start, stop=stop)

            def mm3(out, wh, wl, xh, xl, start, stop):
                mm(out, wh, xh, start, False)
                mm(out, wh, xl, False, False)
                return mm(out, wl, xh, False, stop)

            pe.wait_ge(s_const, 16 * 6)
            pe.wait_ge(s_x, 48)
            for k in range(KD):
                b = side(("x", k))
                for tt, (t0, tn) in enumerate(TOK):
                    last = nc.tensor.transpose(b[:, t0:t0 + tn], xtok[0:tn, tt, k * 128:(k + 1) * 128],
                                               ident[0:tn, 0:tn])
                last.then_inc(misc_ready, 1)

            def dense_chunk(n, blk, nk, kq, last_kq, xh, xl, xraw, slot, hslot):
                for m in range(4):
                    if kq == 0 and blk >= 1:
                        pe.wait_ge(acc_read[m], blk)
                    for k in range(nk):
                        cols = slice(k * 512 + m * 128, k * 512 + (m + 1) * 128)
                        first, stop = kq == 0 and k == 0, last_kq and k == nk - 1
                        kx = kq * nk + k
                        if xh is None:
                            ins = mm(bank[m][:, 0:NT], raw[:, slot, cols], xraw[:, kx], first, stop)
                        else:
                            ins = mm3(bank[m][:, 0:NT], hi[:, hslot, cols], lo[:, slot, cols],
                                      xh[:, kx], xl[:, kx], first, stop)
                    if last_kq and m < 3:
                        ins.then_inc(acc_ready, 1)
                ins.then_inc(chunk_used, 1)

            def s5_b(tau):
                k, j = divmod(tau, 4)
                rows = slice(32 * j, 32 * j + 32)
                if tau >= 2:
                    pe.wait_ge(bu_read, tau - 1)
                for ri in range(2):
                    last = mm(bank[4 + tau % 2][:, ri * T:(ri + 1) * T], BBT[rows, ri, k, :],
                              U[rows, k, 0:T], True, True)
                last.then_inc(bu_ready, 1)

            ybank = {}

            def s5_c(tau):
                k, j = divmod(tau, 4)
                if j == 0:
                    ybank[k] = side(("y", k))
                y = ybank[k][32 * j:32 * j + 32, :]
                pe.wait_ge(xt_ready, tau + 1)
                for ri in range(2):
                    last = mm(y[:, 0:T], CT[:, ri, k, 32 * j:32 * j + 32], xst[:, tau % 2, ri, :],
                              ri == 0, ri == 1)
                last.then_inc(xt_used, 1)
                for ri in range(2):
                    xv = xs[:, ri, :].rearrange("p (b t) -> p b t", b=NB)[:, :, tau]
                    last = mm(y[:, T:NT], CT[:, ri, k, 32 * j:32 * j + 32], xv, ri == 0, ri == 1)
                if j == 3:
                    last.then_inc(misc_ready, 1)

            def hgrn(hg, p):
                H0 = hg * HG
                if p == 0:
                    for c in range(2):
                        b = side(("v", hg, c))
                        for hh in range(HG):
                            last = nc.tensor.transpose(b[:, hh * 128:(hh + 1) * 128],
                                                       IV[:, H0 + hh, c * 128:(c + 1) * 128], ident[:, :])
                        last.then_inc(misc_ready, 1)
                    pe.wait_ge(h_k, hg + 1)
                    for name, src, h0 in (("sv", IV, H0), ("sk", kk, 0)):
                        b = side((name, hg))
                        for hh in range(HG):
                            last = nc.tensor.transpose(b[0:NB, hh * 128:(hh + 1) * 128],
                                                       src[:, h0 + hh, T:NT], ident[:, :])
                        last.then_inc(misc_ready, 1)
                if p <= 7:
                    if p:
                        pe.wait_ge(h_q, 7 * hg + p)
                    else:
                        pe.wait_ge(bu_read, NST)
                    for hp in range(2):
                        n = 16 * hg + 2 * p + hp
                        if n >= 2:
                            pe.wait_ge(h_scread, n - 1)
                        for q in range(4):
                            hh, c = 2 * hp + q // 2, q % 2
                            cs = slice(c * 128, (c + 1) * 128)
                            kl = kk[:, hh, cs] if p <= 1 else kt[:, p % 2, hh, cs]
                            ql = Q[:, H0 + hh, cs] if p == 0 else qt[:, p % 2, hh, cs]
                            last = mm(bank[4 + n % 2][:, q * 128:(q + 1) * 128], kl, ql, True, True)
                        last.then_inc(h_sc, 1)
                if p == 8:
                    pe.wait_ge(h_kts, hg + 1)
                    for c in range(2):
                        b = side(("k", hg, c))
                        for hh in range(HG):
                            last = nc.tensor.transpose(b[:, hh * 128:(hh + 1) * 128],
                                                       kt[:, 0, hh, c * 128:(c + 1) * 128], ident[:, :])
                        last.then_inc(misc_ready, 1)
                if p == 9:
                    for c in range(2):
                        stored(("v", hg, c))
                        stored(("k", hg, c))
                    for c in range(2):
                        b = side(("S", hg, c))
                        for hh in range(HG):
                            last = mm(b[:, hh * 128:(hh + 1) * 128], ktok[:, c, hh, :], vtok[:, c, hh, :],
                                      True, True)
                        last.then_inc(misc_ready, 1)
                if 10 <= p <= 13:
                    hh = p - 10
                    stored(("sk", hg))
                    pe.wait_ge(h_blk, H0 + hh + 1)
                    for half in range(2):
                        b = side(("ou", hg, hh, half))
                        mm(b[:, :], sktok[:, hh * 128:(hh + 1) * 128],
                           svblk[:, half * 4:(half + 1) * 4, :].rearrange("p b v -> p (b v)"),
                           True, True).then_inc(misc_ready, 1)
                if 11 <= p <= 14:
                    hh = p - 11
                    b = side(("o", hg, hh))
                    pe.wait_ge(h_scread, 16 * hg + 16)
                    mm(b[:, 0:128], vtok[:, 0, hh, :], Sc[:, hh, 0, :], True, True)
                    mm(b[:, 128:256], vtok[:, 1, hh, :], Sc[:, hh, 1, :], True, False)
                    stored(("S", hg, 0))
                    mm(b[:, 128:256], S0[:, hh, :], qt[:, 0, hh, 128:256], False, True)
                    pe.wait_ge(h_new, H0 + hh + 1)
                    for s in range(NB):
                        last = mm(b[:, T + s:T + s + 1], stS[:, hh % 2, s, :], Q[:, H0 + hh, T + s:T + s + 1],
                                  True, True)
                    last.then_inc(misc_ready, 1)
                if p == 14:
                    b = side(("ms", hg))
                    for hh in range(2, HG):
                        stored(("o", hg, hh))
                    for hh in range(HG):
                        last = mm(b[0:HG, 0:NT], colsel[:, hh, :], sq[:, hh, :], hh == 0, hh == HG - 1)
                    last.then_inc(misc_ready, 1)
                if p == 15:
                    pe.wait_ge(h_rstd, hg + 1)
                    for hh in range(HG):
                        b = side(("rb", hg, hh))
                        mm(b[:, 0:NT], rowsel[:, hh, :], rr[:, 1, :], True, True).then_inc(misc_ready, 1)

            for c in range(N_GLU):
                if c == 1:
                    pe.wait_ge(dt_wide, 1)
                    b = side("par")
                    for i in range(3):
                        last = nc.tensor.transpose(b[:, 32 * i:32 * i + 32], parnat[:, i, :],
                                                   ident[0:32, 0:32])
                    last.then_inc(misc_ready, 1)
                if c == 5 or c == 6:
                    pe.wait_ge(blk_ready, c - 4)
                    for ri in range(2):
                        for half in range(2):
                            b = side((c, ri, half))
                            for q in range(4):
                                k = half * 4 + q
                                last = nc.tensor.transpose(
                                    b[:, q * 128:(q + 1) * 128],
                                    yblk[:, ri].rearrange("p t c -> p (t c)")[:, k * 128:(k + 1) * 128],
                                    ident[:, :])
                            last.then_inc(misc_ready, 1)
                if c == 7:
                    b = side("s")
                    for q in range(4):
                        last = nc.tensor.transpose(b[:, q * 128:(q + 1) * 128], snat[:, q // 2, q % 2, :],
                                                   ident[:, :])
                    last.then_inc(misc_ready, 1)
                if c == 9:
                    b = side("bus")
                    pe.wait_ge(ublk_ready, 1)
                    for ri in range(2):
                        stored((5, ri, 1))
                    stored((5, 0, 0))
                    for ri in range(2):
                        for k in range(KW):
                            last = mm(b[:, ri * 256 + k * 32:ri * 256 + (k + 1) * 32], BBT[:, ri, k, :],
                                      ublk[:, k].rearrange("p j b -> p (j b)"), True, True)
                    last.then_inc(misc_ready, 1)
                    for ri in range(2):
                        stored((6, ri, 0))
                        stored((6, ri, 1))
                for tau in s5_at.get(c, []):
                    s5_b(tau)
                    if tau >= 2:
                        s5_c(tau - 2)
                if c == S5_END:
                    s5_c(NST - 2)
                    s5_c(NST - 1)
                    pe.wait_ge(yt_ready, KW)
                    b = side("fin")
                    for ri in range(2):
                        last = nc.tensor.transpose(b[0:NST, ri * 128:(ri + 1) * 128], fin[:, ri, :],
                                                   ident[:, :])
                    last.then_inc(misc_ready, 1)
                    b = side("xso")
                    for q in range(4):
                        last = nc.tensor.transpose(b[:, q * 128:(q + 1) * 128],
                                                   xs[:, q // 2, (q % 2) * 128:(q % 2 + 1) * 128], ident[:, :])
                    last.then_inc(misc_ready, 1)
                for hg, p in hg_at.get(c, []):
                    hgrn(hg, p)
                if is_split(c):
                    pe.wait_ge(lo_done, split_count(c) + 1)
                    dense_chunk(c, c // 4, 4, c % 4, c % 4 == 3, XH, XL, None, c % RD, split_count(c) % RH)
                else:
                    pe.wait_ge(landed[c % RD], 16 * (c // RD + 1))
                    dense_chunk(c, c // 4, 4, c % 4, c % 4 == 3, None, None, XT, c % RD, 0)

            def dense(n0, n1, blk0, kqs, xh, xl, after=None):
                for n in range(n0, n1):
                    kq, blk = (n - n0) % kqs, blk0 + (n - n0) // kqs
                    pe.wait_ge(lo_done, split_count(n) + 1)
                    dense_chunk(n, blk, 4, kq, kq == kqs - 1, xh, xl, None, n % RD, split_count(n) % RH)
                    if after is not None and kq == 1 and blk > blk0:
                        after(blk - blk0 - 1)
                if after is not None:
                    after((n1 - n0) // kqs - 1)

            pe.wait_ge(a_lo, 1)
            dense(N_GLU, N_BA, BLK_GLU, 2, YGH, YGL)
            pe.wait_ge(a_lo, 4)
            dense(N_BA, N_BB, BLK_BA, 2, YAH, YAL)
            dense(N_BB, N_O, BLK_BB, 2, YBH, YBL)
            pe.wait_ge(p_ld, 48)
            b2 = [side("p0"), side("p1")]
            for k in range(2):
                for tt, (t0, tn) in enumerate(TOK):
                    last = nc.tensor.transpose(b2[k][:, t0:t0 + tn], ptok[0:tn, tt, k * 128:(k + 1) * 128],
                                               ident[0:tn, 0:tn])
                last.then_inc(misc_ready, 1)

            def to_tokens(name, src, ready, per):
                def go(j):
                    pe.wait_ge(ready, j + 1)
                    for tt, (t0, tn) in enumerate(TOK):
                        b = side((name, j, tt))
                        for q in range(4):
                            last = nc.tensor.transpose(b[0:tn, q * 128:(q + 1) * 128],
                                                       src[:, 4 * j + q, t0:t0 + tn], ident[:, :])
                        last.then_inc(misc_ready, 1)
                return go

            pe.wait_ge(a_lo, 8)
            dense(N_O, N_PP, BLK_O, 4, MH, ML, to_tokens("h", XT, hpre, 0))
            stored("p0")
            stored("p1")
            for n in range(N_PP, N_PG):
                pe.wait_ge(lo_done, split_count(n) + 1)
                for half in range(2):
                    blk = BLK_PP + 2 * (n - N_PP) + half
                    for m in range(4):
                        pe.wait_ge(acc_read[m], blk)
                        for k in range(2):
                            cols = slice(k * 1024 + half * 512 + m * 128, k * 1024 + half * 512 + (m + 1) * 128)
                            last = mm3(bank[m][:, 0:NT], hi[:, split_count(n) % RH, cols], lo[:, n % RD, cols],
                                       pTh[:, k], pTl[:, k], k == 0, k == 1)
                        if (half, m) != (1, 3):
                            last.then_inc(acc_ready, 1)
                last.then_inc(chunk_used, 1)
            for k in range(KD):
                b = side(("ht", k))
                for tt, (t0, tn) in enumerate(TOK):
                    if k == 0:
                        pe.wait_ge(h_ready, tt + 1)
                    last = nc.tensor.transpose(b[:, t0:t0 + tn], htok[0:tn, tt, k * 128:(k + 1) * 128],
                                               ident[0:tn, 0:tn])
                last.then_inc(misc_ready, 1)
            b = side("log")
            pe.wait_ge(wr_lo, 1)
            stored(("ht", KD - 2))
            stored(("ht", KD - 1))
            for tt, (t0, tn) in enumerate(TOK):
                for k in range(KD):
                    last = mm3(b[0:tn, tt * 36:(tt + 1) * 36], HTH[:, k, t0:t0 + tn], HTL[:, k, t0:t0 + tn],
                               wrh[:, k], wrl[:, k], k == 0, k == KD - 1)
            last.then_inc(misc_ready, 1)

            def counts():
                b = side("rank")
                pe.wait_ge(oh_ready, 1)
                for tt, (t0, tn) in enumerate(TOK):
                    for s in range(tt):
                        mm(b[0:tn, tt * 4:(tt + 1) * 4], ones[:, 0:tn], oh[:, s], s == 0, False)
                    mm(b[0:tn, tt * 4:(tt + 1) * 4], lowtri[0:tn, 0:tn], oh[0:tn, tt], tt == 0, True)
                for tt, (t0, tn) in enumerate(TOK):
                    last = mm(b[:, 16:20], ones[0:tn, :], oh[0:tn, tt], tt == 0, tt == 2)
                last.then_inc(misc_ready, 1)

            def pg_after():
                go = to_tokens("ple", PPT, ple_ready, 0)
                def run(j):
                    if j == 2:
                        counts()
                    go(j)
                return run

            dense(N_PG, N_END, BLK_PG, 4, HTH, HTL, pg_after())

            def gather(rnd, g):
                gg = rnd * GROUPS + g
                pe.wait_ge(sel_ready, rnd + 1)
                b = side(("st", rnd, g))
                for tt, (t0, tn) in enumerate(TOK):
                    last = nc.tensor.transpose(b[:, t0:t0 + tn], Sel[0:tn, tt, g, :], ident[0:tn, 0:tn])
                last.then_inc(misc_ready, 1)
                b = side(("cg", rnd, g))
                for tt, (t0, tn) in enumerate(TOK):
                    last = mm(b[:, 0:EPG], Sel[0:tn, tt, g, :], comb8[0:tn, tt, :], tt == 0, tt == 2)
                last.then_inc(misc_ready, 1)
                for kq in range(4):
                    b = side(("ga", rnd, g, kq))
                    for q in range(4):
                        k = kq * 4 + q
                        for tt, (t0, tn) in enumerate(TOK):
                            hv = htok[0:tn, tt, :].rearrange("p (f k) -> p k f", k=KD)[:, k, :]
                            last = mm(b[:, q * 128:(q + 1) * 128], hv, Sel[0:tn, tt, g, :], tt == 0, tt == 2)
                    last.then_inc(misc_ready, 1)

            def scatter(rnd, g):
                gg = rnd * GROUPS + g
                pe.wait_ge(outg_done, 4 * (gg + 1))
                stored(("st", rnd, g))
                for tt, (t0, tn) in enumerate(TOK):
                    for nb in range(4):
                        b = side(("sc", rnd, g, tt, nb))
                        last = mm(b[0:tn, :], SelT[:, g % 2, t0:t0 + tn], outg[:, nb * 512:(nb + 1) * 512],
                                  True, True)
                        last.then_inc(misc_ready, 1)

            def gate_up(n, buf):
                for s in range(4):
                    pe.wait_ge(g_lo, 4 * n + s + 1)
                    for k in range(4):
                        kx = s * 4 + k
                        hs = mhi[s % 3][:, k * 512:(k + 1) * 512]
                        ls = mlo[s][:, k * 512:(k + 1) * 512]
                        mm(bank[4][:, :], hgh[:, buf, kx], hs, kx == 0, False)
                        mm(bank[4][:, :], hgl[:, buf, kx], hs, False, False)
                        last = mm(bank[4][:, :], hgh[:, buf, kx], ls, False, kx == 15)
                    last.then_inc(g_used, 1)

            def down(n, first, final):
                pe.wait_ge(hidT_lo, n + 1)
                for j in range(2):
                    pe.wait_ge(d_lo, 2 * n + j + 1)
                    for nb in range(4):
                        hs = mhi[(4 + j) % 3][:, nb * 512:(nb + 1) * 512]
                        ls = mlo[4 + j][:, nb * 512:(nb + 1) * 512]
                        st = first and j == 0
                        mm(bank[nb][:, :], hidH[:, j], hs, st, False)
                        mm(bank[nb][:, :], hidL[:, j], hs, False, False)
                        last = mm(bank[nb][:, :], hidH[:, j], ls, False, final and j == 1)
                    last.then_inc(d_used, 1)

            def turn(n):
                pe.wait_ge(hid_done, n + 1)
                for j in range(2):
                    last = nc.tensor.transpose(bank[5][:, j * 128:(j + 1) * 128],
                                               hid[:, :].rearrange("p (f j) -> p j f", j=2)[:, j, :],
                                               ident[:, :])
                last.then_inc(hidT_ready, 1)

            def expert_round(rnd):
                gather(rnd, 0)
                for g in range(GROUPS):
                    gg = rnd * GROUPS + g
                    n0 = EPG * gg
                    stored(("ga", rnd, g, 2))
                    stored(("ga", rnd, g, 3))
                    if n0:
                        pe.wait_ge(hid_done, n0)
                    gate_up(n0, gg % 2)
                    if g:
                        down(n0 - 1, False, True)
                    turn(n0)
                    pe.wait_ge(hid_done, n0 + 1)
                    gate_up(n0 + 1, gg % 2)
                    if gg:
                        pe.wait_ge(outg_done, 4 * gg)
                    else:
                        for m in range(4):
                            pe.wait_ge(acc_read[m], BLK_PG + 4)
                    down(n0, True, False)
                    if g:
                        scatter(rnd, g - 1)
                    if g + 1 < GROUPS:
                        gather(rnd, g + 1)
                    turn(n0 + 1)
                    with pe.Fori(n0 + 2, n0 + EPG) as n:
                        pe.wait_ge(hid_done, n)
                        gate_up(n, gg % 2)
                        down(n - 1, False, False)
                        turn(n)
                down(EPG * GROUPS * (rnd + 1) - 1, False, True)
                scatter(rnd, GROUPS - 1)

            expert_round(0)
            pe.wait_ge(flag_ready, 1)
            more = pe.value_load(flag[0:1, 0:1], min_val=0, max_val=1)
            with pe.If(more > 0):
                for rnd in range(1, ROUNDS):
                    expert_round(rnd)

        @block.sync
        def _(sp):
            for n in range(N_END):
                if n >= RD:
                    sp.wait_ge(chunk_used, n - RD + 1)
                c = chunk(n)
                sp.dma_start(raw[:, n % RD, :].rearrange("p (k n) -> p k n", k=c.shape[1]), c).then_inc(
                    landed[n % RD], 16)

            def gate_up_chunk(e, s):
                for i, w in enumerate((t["w_exp_gate"], t["w_exp_up"])):
                    src = w[0, bass.ds(e, 1)].rearrange("a (p k) f -> p (a k) f", p=P)[:, 4 * s:4 * s + 4, :]
                    dst = mraw[s].rearrange("p (k i f) -> p k i f", k=4, i=2)[:, :, i, :]
                    sp.dma_start(dst, src).then_inc(g_land[s], 16)

            def down_chunk(e, j):
                src = t["w_exp_down"][0, bass.ds(e, 1)].rearrange("a (p j) d -> p (a j) d", p=P)[:, j, :]
                sp.dma_start(mraw[4 + j], src).then_inc(d_land[j], 16)

            def expert_round(rnd):
                n0 = EPG * GROUPS * rnd
                for s in range(4):
                    if rnd:
                        sp.wait_ge(g_used, 4 * n0 - 3 + s)
                    else:
                        sp.wait_ge(chunk_used, max(n for n in range(N_END) if n % RD == s) + 1)
                    gate_up_chunk(0, s)
                for j in range(2):
                    if rnd:
                        sp.wait_ge(d_used, 2 * n0 - 1 + j)
                    else:
                        sp.wait_ge(chunk_used, N_END)
                    down_chunk(0, j)
                for s in range(4):
                    sp.wait_ge(g_used, 4 * n0 + s + 1)
                    gate_up_chunk(1, s)
                with sp.Fori(1, EPG * GROUPS - 1) as e:
                    for s in range(4):
                        sp.wait_ge(g_used, 4 * n0 + 4 * e + s + 1)
                        gate_up_chunk(e + 1, s)
                    for j in range(2):
                        sp.wait_ge(d_used, 2 * n0 + 2 * e + j - 1)
                        down_chunk(e, j)
                for j in range(2):
                    sp.wait_ge(d_used, 2 * n0 + 2 * (EPG * GROUPS - 1) + j - 1)
                    down_chunk(EPG * GROUPS - 1, j)

            expert_round(0)
            sp.wait_ge(flag_ready, 1)
            more = sp.value_load(flag[0:1, 0:1], min_val=0, max_val=1)
            with sp.If(more > 0):
                for rnd in range(1, ROUNDS):
                    expert_round(rnd)
            y = outs
            for tt, (t0, tn) in enumerate(TOK):
                sp.wait_ge(f_out, tt + 1)
                dst = y[0][0, t0:t0 + tn, :] if tt < 2 else y[1].rearrange("b a d -> (b a) d")
                sp.dma_start(dst, atok[0:tn, tt, :]).then_inc(y_out, 16)
            sp.wait_ge(y_out, 48)

        @block.gpsimd
        def _(pool):
            def state_view(x, h):
                return x[0, :, h].rearrange("b k v -> k b v")

            pool.wait_ge(outT, 1)
            for ri in range(2):
                pool.dma_start(outs[2 + ri].rearrange("a b (t g) n -> (a b t) (g n)", g=2),
                               finT[:, ri, :]).then_inc(st_out, 16)
            pool.wait_ge(outT, 2)
            for ri in range(2):
                pool.dma_start(outs[5 + ri][0].rearrange("(r b) (t g) n -> (b t) r (g n)", r=2, g=2),
                               xs[:, ri, :].rearrange("p (r n) -> p r n", r=2)).then_inc(st_out, 16)
            pool.wait_ge(xt_used, NST)
            for h in range(2):
                pool.dma_start(stS[:, h % 2], state_view(t["state_hgrn"], h)).then_inc(h_stq[h % 2], 16)
            for h in range(HEADS):
                hg, hh = divmod(h, HG)
                side_read(pool, ("sv", hg))
                if h:
                    last = misc[("ou", (h - 1) // HG, (h - 1) % HG, 1)]
                    pool.wait_ge(misc_ready, last + 1)
                nc.gpsimd.tensor_tensor(
                    svblk[:, :, :],
                    svtok[:, hh * 128:(hh + 1) * 128].unsqueeze(1).to_broadcast([NB, NB, 128]),
                    ident[0:NB, 0:NB].unsqueeze(2).to_broadcast([NB, NB, 128]), ALU.mult).then_inc(h_blk, 1)
                if 0 < h < HEADS - 1:
                    o = h - 1
                    pool.wait_ge(misc_ready, misc[("o", o // HG, o % HG)] + 1)
                    pool.wait_ge(h_sto[o % 2], 16 * (o // 2 + 1))
                    pool.dma_start(stS[:, o % 2], state_view(t["state_hgrn"], o + 2)).then_inc(h_stq[o % 2], 16)
                pool.wait_ge(h_new, h + 1)
                pool.dma_start(state_view(outs[7], h), stS[:, h % 2]).then_inc(h_sto[h % 2], 16)
                if hh == HG - 1:
                    pool.wait_ge(h_fin, hg + 1)
                    pool.dma_start(outs[4][0, 0, hg * HG:(hg + 1) * HG].rearrange("h k v -> k h v"),
                                   Sf[:, :, :]).then_inc(st_out, 16)
            pool.wait_ge(a_lo, 2)
            pool.dma_start(ptok[:, 0:2, :], t["p_prompt"][0, 0].rearrange("(t p) c -> p t c", p=P)).then_inc(
                p_ld, 16)
            pool.dma_start(ptok[0:NB, 2, :], t["p_sample"][0].rearrange("b a c -> (b a) c")).then_inc(p_ld, 32)
            pool.wait_ge(chunk_used, N_O)
            for i, n in enumerate(("ln1_gain", "ln1_bias")):
                pool.dma_start(ln1[:, i, :], t[n].to_broadcast([P, D])).then_inc(ln_ld, 16)
            pool.dma_start(wrr[:, :, 0:4], t["w_group_router"][0].rearrange("(k p) g -> p k g", p=P)).then_inc(
                r_ld, 16)
            pool.dma_start(wrr[:, :, 4:36], t["w_expert_router"][0].rearrange("(k p) g -> p k g", p=P)).then_inc(
                r_ld, 16)
            pool.dma_start(rbias[:, 0:4], t["b_group_router"].to_broadcast([P, 4])).then_inc(r_ld, 16)
            pool.dma_start(rbias[:, 4:36], t["b_expert_router"].to_broadcast([P, 32])).then_inc(r_ld, 16)
            pool.wait_ge(misc_ready, misc[("ple", 3, 2)] + 1)
            for i, n in enumerate(("ln2_gain", "ln2_bias")):
                pool.dma_start(ln2[:, i, :], t[n].to_broadcast([P, D])).then_inc(ln2_ld, 16)
            pool.wait_ge(st_out, 16 * 6)
            for i in range(2):
                pool.wait_ge(h_sto[i], 16 * 4)

        @block.scalar
        def _(act):
            def side(name):
                n = misc[name]
                act.wait_ge(misc_ready, n + 1)
                return bank[6 + n % 2], misc_read[n % 2]

            cc = t["consts"]
            act.dma_start(xtok[:, 0:2, :], t["x_prompt"][0].rearrange("(t p) d -> p t d", p=P)).then_inc(s_x, 32)
            act.dma_start(xtok[0:NB, 2, :], t["x_sample"].rearrange("b a d -> (b a) d")).then_inc(s_x, 16)
            act.dma_start(ident[:, :], cc[:, C_ID:C_ID + 128]).then_inc(s_const, 16)
            act.dma_start(lowtri[:, :], cc[:, C_LT:C_LT + 128]).then_inc(s_const, 16)
            act.dma_start(iota[:, :], cc[:, C_IO:C_IO + 128]).then_inc(s_const, 16)
            act.dma_start(small[:, :], cc[:, C_MJ:C_MJ + 24]).then_inc(s_const, 16)
            act.dma_start(rowsel[:, :, :], cc[0:HG, C_RS:C_RS + 512].rearrange("p (h n) -> p h n", h=HG)).then_inc(
                s_const, 16)
            act.dma_start(masks[:, :, :], cc[:, C_MASK:C_END].rearrange("p (h n) -> p h n", h=8)).then_inc(
                s_const, 16)
            act.dma_start(dtn[:, :], t["s5_log_dt"][0].rearrange("(t g) -> t g", g=2)).then_inc(s_par, 16)
            for i, n in enumerate(("s5_lambda_re", "s5_lambda_im")):
                act.dma_start(parnat[:, i, :], t[n][0].rearrange("(t g) n -> t (g n)", g=2)).then_inc(s_par, 16)
            for i, n in enumerate(("s5_b_re", "s5_b_im")):
                act.dma_start(braw[:, i], t[n][0].rearrange("(t g) n c -> (g n) t c", g=2)).then_inc(s_bc, 16)
            for i, n in enumerate(("s5_c_re", "s5_c_im")):
                act.dma_start(craw[:, i], t[n][0].rearrange("(k g) c n -> (g c) k n", g=8)).then_inc(s_bc, 16)
            for i, n in enumerate(("state_s5_re", "state_s5_im")):
                act.dma_start(snat[:, i], t[n][0].rearrange("(r b) (t g) n -> (b t) r (g n)", r=2, g=2)).then_inc(
                    s_bc, 16)
            with nc.allow_non_contiguous_dma(reason="three short vectors, a feature on each partition"):
                act.dma_start(dskip[:, :], t["s5_d"][0].rearrange("(k p) -> p k", p=P)).then_inc(s_vec, 16)
                act.dma_start(lbraw[:, :], t["hg_lower_bounds"][0].rearrange("(k p) -> p k", p=P)).then_inc(
                    s_vec, 16)
                act.dma_start(gnorm[:, :], t["hg_norm_gain"][0].rearrange("(k p) -> p k", p=P)).then_inc(s_vec, 16)

            act.wait_ge(s_par, 48)
            nc.scalar.activation(dtn[:, :], dtn[:, :], ACT.Exp).then_inc(dt_exp, 1)
            for k in range(KD):
                b, read = side(("x", k))
                nc.scalar.activation(XH[:, k, :], b[:, 0:NT], ACT.Copy).then_inc(xh_done, 1)

            def high(n):
                s = split_count(n)
                act.wait_ge(landed[n % RD], 16 * (n // RD + 1))
                if s >= RH:
                    prev = n - RH if n - RH >= N_GLU or n < N_GLU else 4 * SPLIT_IN - RH + (n - N_GLU)
                    act.wait_ge(chunk_used, prev + 1)
                nc.scalar.activation(hi[:, s % RH, :], raw[:, n % RD, :], ACT.Copy).then_inc(hi_done, 1)

            def hgrn(hg, p):
                if p == 0:
                    for n, name in enumerate((("v", hg, 0), ("v", hg, 1), ("sv", hg), ("sk", hg))):
                        b, read = side(name)
                        if n < 2:
                            nc.scalar.activation(vtok[:, n].rearrange("p h v -> p (h v)"), b[:, :],
                                                 ACT.Copy).then_inc(read, 1)
                        else:
                            nc.scalar.activation((svtok, sktok)[n - 2][:, :], b[0:NB, :], ACT.Copy).then_inc(
                                read, 1)
                if p == 8:
                    for c in range(2):
                        b, read = side(("k", hg, c))
                        nc.scalar.activation(ktok[:, c].rearrange("p h v -> p (h v)"), b[:, :],
                                             ACT.Copy).then_inc(read, 1)
                if p == 9:
                    b, read = side(("S", hg, 0))
                    nc.scalar.activation(S0[:, :, :].rearrange("p h v -> p (h v)"), b[:, :],
                                         ACT.Copy).then_inc(read, 1)
                if 11 <= p <= 14:
                    hh = p - 11
                    b, read = side(("o", hg, hh))
                    nc.scalar.activation(O4[:, hh, :], b[:, 0:NT], ACT.Copy)
                    nc.scalar.activation(sq[:, hh, :], b[:, 0:NT], ACT.Square).then_inc(read, 1)
                if p == 15:
                    act.wait_ge(h_ms, hg + 1)
                    nc.scalar.activation(rr[:, 1, :], rr[:, 0, :], ACT.Sqrt).then_inc(h_sqrt, 1)

            high(0)
            for c in range(N_GLU):
                blk = c // 4
                if c + 1 < 4 * SPLIT_IN:
                    high(c + 1)
                if c == 1:
                    act.wait_ge(ang_ready, 1)
                    nc.scalar.activation(par[:, 5], par[:, 4], ACT.Abs).then_inc(abs_done, 1)
                    nc.scalar.activation(par[:, 3], par[:, 3], ACT.Exp).then_inc(trig_done, 1)
                if c == 2:
                    act.wait_ge(ang_ready, 2)
                    nc.scalar.activation(Pi[:, :, 0], par[:, 4], ACT.Sin).then_inc(trig_done, 1)
                    nc.scalar.activation(Pr[:, :, 0], par[:, 5], ACT.Sin).then_inc(trig_done, 1)
                if c == 5 or c == 6:
                    for ri in range(2):
                        for half in range(2):
                            b, read = side((c, ri, half))
                            dst = (BBT, CT)[c - 5][:, ri, half * 4:half * 4 + 4, :].rearrange("p k n -> p (k n)")
                            nc.scalar.activation(dst, b[:, :], ACT.Copy,
                                                 scale=-1.0 if c == 6 and ri else 1.0).then_inc(read, 1)
                if c == 7:
                    b, read = side("s")
                    nc.scalar.activation(sT[:, :, :].rearrange("p r n -> p (r n)"), b[:, :], ACT.Copy).then_inc(
                        read, 1)
                if c == S5_END + 1:
                    act.wait_ge(yt_ready, KW)
                    nc.scalar.activation(U[:, :, :], U[:, :, :], ACT.Gelu_apprx_tanh).then_inc(gelu_done, 1)
                for hg, p in hg_at.get(c, []):
                    hgrn(hg, p)
                if c % 4 == 3:
                    for m in range(4):
                        J = blk * 4 + m
                        summed(act, blk, m)
                        src = bank[m][:, 0:NT]
                        z, j = J // KW, J % KW
                        if z in (1, 4):
                            n = (z == 4) * KW + j
                            act.wait_ge(acc_read[(m + 2) % 4], blk + (m >= 2))
                            nc.scalar.activation(sigtmp[:, n % 2, :], src, ACT.Sigmoid).then_inc(sig_ready, 1)
                            continue
                        if z == 3 and m == 0:
                            act.wait_ge(blk_ready, 2)
                        if z == 5 and j == 0:
                            act.wait_ge(chunk_used, 4 * SPLIT_IN)
                        dst = (U, Q, FG, IV, G)[z][:, j] if z < 5 else (
                            GA[:, J - 5 * KW] if J < 5 * KW + KD else GB[:, J - 5 * KW - KD])
                        nc.scalar.activation(dst, src, ACT.Copy if z in (0, 3) else ACT.Sigmoid).then_inc(
                            acc_read[m], 1)

            def bulk(xh, xraw, ready, n):
                act.wait_ge(*ready)
                nc.scalar.activation(xh, xraw, ACT.Copy).then_inc(a_hi, 1)

            high(N_GLU)
            act.wait_ge(h_done, 1)
            act.wait_ge(st_out, 16 * 6)
            bulk(YGH[:, :, :], U[:, :, :], (gelu_done, 1), 0)
            bulk(YBH[:, :, :], G[:, :, :], (h_done, 1), 0)
            for n in range(N_GLU, N_END):
                for ahead in ahead_of(n):
                    high(ahead)
                if n < N_BA and n % 2 == 1:
                    blk, b0 = (n - N_GLU) // 2, BLK_GLU
                    for m in range(4):
                        summed(act, BLK_GLU + blk, m)
                        k = 2 * KW + 4 * blk + m
                        act.wait_ge(acc_read[(m + 2) % 4], b0 + blk + (m >= 2))
                        nc.scalar.activation(sigtmp[:, k % 2, :], bank[m][:, 0:NT], ACT.Sigmoid).then_inc(
                            sig_ready, 1)
                    js = slice(4 * blk, 4 * blk + 4)
                    bulk(YAH[:, js, :], U[:, js, :], (a_raw, blk + 1), 0)
                if N_BB <= n < N_O and n % 2 == 1:
                    blk = (n - N_BB) // 2
                    js = slice(4 * blk, 4 * blk + 4)
                    bulk(MH[:, js, :], GA[:, js, :], (a_raw, 2 + blk + 1), 0)
                if n == N_O:
                    for k in range(2):
                        b, read = side(f"p{k}")
                        nc.scalar.activation(pTh[:, k, :], b[:, 0:NT], ACT.Copy).then_inc(pt_hi, 1)
                    act.wait_ge(r_ld, 64)
                    nc.scalar.activation(wrh[:, :, :], wrr[:, :, :], ACT.Copy).then_inc(wr_hi, 1)

                def to_htok(j):
                    for tt, (t0, tn) in enumerate(TOK):
                        b, read = side(("h", j, tt))
                        act.wait_ge(stat_done, 3 * j + tt + 1)
                        nc.scalar.activation(htok[0:tn, tt, j * 512:(j + 1) * 512], b[0:tn, :],
                                             ACT.Copy).then_inc(read, 1)
                if N_O + 4 < n < N_PP and (n - N_O) % 4 == 2:
                    to_htok((n - N_O) // 4 - 1)
                if n == N_PP - 1:
                    to_htok(3)
                    for tt, (t0, tn) in enumerate(TOK):
                        if tt == 0:
                            act.wait_ge(ln_var, 1)
                            nc.scalar.activation(rstd[:, :], rstd[:, :], ACT.Sqrt).then_inc(ln_sq, 1)
                        act.wait_ge(ln_nmr, 1)
                        nc.scalar.activation(htok[0:tn, tt, :], htok[0:tn, tt, :], ACT.Identity,
                                             bias=nmr[0:tn, tt:tt + 1], scale=rstd[0:tn, tt:tt + 1]).then_inc(
                            ln_norm, 1)
                if N_PP <= n < N_PG:
                    for J in range(8 * (n - N_PP), 8 * (n - N_PP) + 8):
                        summed(act, BLK_PP + J // 4, J % 4)
                        nc.scalar.activation(PPT[:, J, :], bank[J % 4][:, 0:NT], ACT.Copy).then_inc(
                            acc_read[J % 4], 1)
                if n == N_PG - 1:
                    for k in range(KD):
                        b, read = side(("ht", k))
                        nc.scalar.activation(HTH[:, k, :], b[:, 0:NT], ACT.Copy).then_inc(ht_hi, 1)
                if n >= N_PG and (n - N_PG) % 4 == 3:
                    blk, b0 = (n - N_PG) // 4, BLK_PG
                    for m in range(4):
                        summed(act, BLK_PG + blk, m)
                        k = 3 * KW + 4 * blk + m
                        act.wait_ge(acc_read[(m + 2) % 4], b0 + blk + (m >= 2))
                        nc.scalar.activation(sigtmp[:, k % 2, :], bank[m][:, 0:NT], ACT.Sigmoid).then_inc(
                            sig_ready, 1)
                if n == N_PG + 6:
                    act.wait_ge(gm_neg, 1)
                    nc.scalar.activation(gex[:, :, :], gex[:, :, :], ACT.Exp).then_inc(r_exp, 1)
                if n == N_PG + 10:
                    act.wait_ge(e_diff, 1)
                    nc.scalar.activation(rsm[:, :, 1], rsm[:, :, 0], ACT.Exp).then_inc(r_exp2, 1)

            def gather(rnd, g):
                gg = rnd * GROUPS + g
                b, read = side(("st", rnd, g))
                nc.scalar.activation(SelT[:, g % 2, :], b[:, 0:NT], ACT.Copy).then_inc(read, 1)
                b, read = side(("cg", rnd, g))
                nc.scalar.activation(combg[:, g % 2, :], b[:, 0:EPG], ACT.Copy).then_inc(read, 1)
                for kq in range(4):
                    b, read = side(("ga", rnd, g, kq))
                    nc.scalar.activation(hgh[:, gg % 2, 4 * kq:4 * kq + 4, :].rearrange("p k s -> p (k s)"),
                                         b[:, :], ACT.Copy).then_inc(hg_hi, 1)

            def highs(n, which):
                for s in which:
                    if s < 4:
                        act.wait_ge(g_land[s], 32 * n + 32)
                        if s == 3:
                            act.wait_ge(g_used, 4 * n + 1)
                        elif s == 0 and not (isinstance(n, int) and n == 0):
                            act.wait_ge(g_used, 4 * n)
                        elif s in (1, 2) and not (isinstance(n, int) and n < 2):
                            act.wait_ge(d_used, 2 * n - 4 + s)
                        nc.scalar.activation(mhi[s % 3], mraw[s], ACT.Copy).then_inc(g_hi, 1)
                    else:
                        act.wait_ge(d_land[s - 4], 16 * n)
                        act.wait_ge(g_used, 4 * n + s - 2)
                        nc.scalar.activation(mhi[s % 3], mraw[s], ACT.Copy).then_inc(d_hi, 1)

            def silu(n):
                act.wait_ge(g_used, 4 * n)
                if not (isinstance(n, int) and n < 2):
                    act.wait_ge(hid_done, n - 1)
                nc.scalar.activation(gsil[:, :], bank[4][:, 0:FE], ACT.Silu).then_inc(silu_done, 1)

            def hidden(n):
                act.wait_ge(hidT_ready, n)
                nc.scalar.activation(hidH[:, :, :].rearrange("p j s -> p (j s)"), bank[5][:, 0:256],
                                     ACT.Copy).then_inc(hidT_hi, 1)

            def store(gg):
                for nb in range(4):
                    if nb == 0:
                        act.wait_ge(d_used, 2 * EPG * (gg + 1))
                        if gg:
                            last = misc[("sc", (gg - 1) // GROUPS, (gg - 1) % GROUPS, 2, 3)]
                            act.wait_ge(misc_ready, last + 1)
                    nc.scalar.activation(outg[:, nb * 512:(nb + 1) * 512], bank[nb][:, :],
                                         ACT.Copy).then_inc(outg_done, 1)

            def turn(n):
                silu(n)
                highs(n, (0, 1, 2))
                hidden(n)
                highs(n, (3, 4, 5))

            act.wait_ge(chunk_used, N_END)
            def expert_round(rnd):
                gather(rnd, 0)
                for g in range(GROUPS):
                    gg = rnd * GROUPS + g
                    n0 = EPG * gg
                    if n0 == 0:
                        highs(0, (0, 1, 2, 3))
                    elif g == 0:
                        act.wait_ge(d_used, 2 * n0)
                        highs(n0, (0, 1, 2, 3))
                    else:
                        turn(n0)
                        store(gg - 1)
                    silu(n0 + 1)
                    highs(n0 + 1, (0, 1, 2))
                    hidden(n0 + 1)
                    highs(n0 + 1, (3, 4, 5))
                    if g + 1 < GROUPS:
                        gather(rnd, g + 1)
                    with act.Fori(n0 + 2, n0 + EPG) as n:
                        turn(n)
                n1 = EPG * GROUPS * (rnd + 1)
                silu(n1)
                hidden(n1)
                for s in (4, 5):
                    act.wait_ge(d_land[s - 4], 16 * n1)
                    nc.scalar.activation(mhi[s % 3], mraw[s], ACT.Copy).then_inc(d_hi, 1)
                store(GROUPS * (rnd + 1) - 1)

            expert_round(0)
            act.wait_ge(flag_ready, 1)
            more = act.value_load(flag[0:1, 0:1], min_val=0, max_val=1)
            with act.If(more > 0):
                for rnd in range(1, ROUNDS):
                    expert_round(rnd)
            for tt, (t0, tn) in enumerate(TOK):
                act.wait_ge(f_var, tt + 1)
                nc.scalar.activation(rstd[0:tn, tt:tt + 1], rstd[0:tn, tt:tt + 1], ACT.Sqrt).then_inc(f_sq, 1)
                act.wait_ge(f_nmr, tt + 1)
                nc.scalar.activation(atok[0:tn, tt, :], atok[0:tn, tt, :], ACT.Identity,
                                     bias=nmr[0:tn, tt:tt + 1], scale=rstd[0:tn, tt:tt + 1]).then_inc(f_norm, 1)

        @block.vector
        def _(dve):
            v = nc.vector
            count = [0]
            told = flagf[:, 1:2]

            def link(ins):
                count[0] += 1
                ins.then_inc(chain, 1)

            def settle():
                dve.wait_ge(chain, count[0])

            def side(name):
                n = misc[name]
                dve.wait_ge(misc_ready, n + 1)
                return bank[6 + n % 2], misc_read[n % 2]

            def low(n):
                s = split_count(n)
                dve.wait_ge(hi_done, s + 1)
                v.tensor_tensor(lo[:, n % RD, :], raw[:, n % RD, :], hi[:, s % RH, :].bitcast(F32),
                                ALU.subtract).then_inc(lo_done, 1)

            v.memset(ones[:, :], 1.0).then_inc(s_ones, 1)
            for k in range(KD):
                b, read = side(("x", k))
                dve.wait_ge(xh_done, k + 1)
                v.tensor_copy(XT[:, k, :], b[:, 0:NT]).then_inc(read, 1)
                side_read(dve, ("x", k))
                v.tensor_tensor(XL[:, k, :], XT[:, k, :], XH[:, k, :].bitcast(F32), ALU.subtract).then_inc(
                    xt_done, 1)
            dve.wait_ge(s_vec, 48)
            link(v.tensor_tensor(lb[:, :], lbraw[:, :], lbraw[:, :], ALU.subtract))

            def lower_bounds():
                settle()
                link(v.tensor_scalar(oml[:, :], lb[:, :], -1.0, 1.0, ALU.mult, ALU.add))
                settle()

            def params_1():
                b, read = side("par")
                v.tensor_copy(par[:, 0:3, :].rearrange("p i t -> p (i t)"), b[:, 0:96]).then_inc(read, 1)
                side_read(dve, "par")
                lr, li, dt = par[:, 0], par[:, 1], par[:, 2]
                link(v.tensor_tensor(par[:, 3], lr, dt, ALU.mult))
                link(v.tensor_tensor(par[:, 4], li, dt, ALU.mult))
                settle()
                magic = 12582912.0
                link(v.tensor_scalar(par[:, 6], par[:, 4], 1.0 / (2 * np.pi), magic, ALU.mult, ALU.add))
                settle()
                link(v.tensor_scalar(par[:, 6], par[:, 6], magic, None, ALU.subtract))
                settle()
                for c in (6.28125, 0.0019350051879882812, 3.0199159819567e-07):
                    link(v.scalar_tensor_tensor(out=par[:, 4], in0=par[:, 6], scalar=-c, in1=par[:, 4],
                                                op0=ALU.mult, op1=ALU.add))
                    settle()
                v.tensor_scalar(par[:, 4], par[:, 4], float(np.float32(np.pi) * 0.9999999),
                                -float(np.float32(np.pi) * 0.9999999), ALU.min, ALU.max).then_inc(ang_ready, 1)

            def params_2():
                dve.wait_ge(abs_done, 1)
                v.tensor_scalar(par[:, 5], par[:, 5], -1.0, float(np.pi / 2), ALU.mult, ALU.add).then_inc(
                    ang_ready, 1)
                dve.wait_ge(trig_done, 3)
                link(v.tensor_copy(mag[:, :], par[:, 3]))
                link(v.tensor_tensor(ab[:, 0], par[:, 3], Pr[:, :, 0], ALU.mult))
                link(v.tensor_tensor(ab[:, 1], par[:, 3], Pi[:, :, 0], ALU.mult))
                lr, li = par[:, 0], par[:, 1]
                link(v.tensor_tensor(par[:, 7], lr, lr, ALU.mult))
                link(v.tensor_tensor(par[:, 8], li, li, ALU.mult))
                settle()
                link(v.tensor_tensor(par[:, 7], par[:, 7], par[:, 8], ALU.add))
                link(v.tensor_scalar(par[:, 9], ab[:, 0], -1.0, None, ALU.add))
                settle()
                link(v.reciprocal(par[:, 7], par[:, 7]))
                link(v.tensor_tensor(par[:, 10], par[:, 9], lr, ALU.mult))
                link(v.tensor_tensor(par[:, 11], ab[:, 1], li, ALU.mult))
                link(v.tensor_tensor(par[:, 12], ab[:, 1], lr, ALU.mult))
                link(v.tensor_tensor(par[:, 13], par[:, 9], li, ALU.mult))
                settle()
                link(v.tensor_tensor(par[:, 10], par[:, 10], par[:, 11], ALU.add))
                link(v.tensor_tensor(par[:, 12], par[:, 12], par[:, 13], ALU.subtract))
                settle()
                link(v.tensor_tensor(par[:, 10], par[:, 10], par[:, 7], ALU.mult))
                link(v.tensor_tensor(par[:, 12], par[:, 12], par[:, 7], ALU.mult))
                settle()

            def input_matrix():
                zr = par[:, 10].unsqueeze(2).to_broadcast([P, NST, 16])
                zi = par[:, 12].unsqueeze(2).to_broadcast([P, NST, 16])
                dve.wait_ge(s_bc, 16 * 6)
                for ri, (x, y, op) in enumerate(((0, 1, ALU.subtract), (1, 0, ALU.add))):
                    link(v.tensor_tensor(bbz[:, ri], braw[:, x], zr, ALU.mult))
                    link(v.tensor_tensor(btmp[:, :, :], braw[:, y], zi, ALU.mult))
                    settle()
                    link(v.tensor_tensor(bbz[:, ri], bbz[:, ri], btmp[:, :, :], op))
                    settle()
                    for g in range(2):
                        last = v.tensor_scalar(yblk[:, ri, :, 16 * g:16 * g + 16], bbz[:, ri],
                                               maskB[:, g:g + 1], None, ALU.mult)
                last.then_inc(blk_ready, 1)

            def output_matrix():
                for ri in range(2):
                    for half in range(2):
                        side_read(dve, (5, ri, half))
                for ri in range(2):
                    dst = yblk[:, ri].rearrange("p t c -> p (t c)").rearrange("p (k g n) -> p k g n", g=2, n=64)
                    for g in range(2):
                        last = v.tensor_scalar(dst[:, :, g, :], craw[:, ri], maskC[:, g:g + 1], None, ALU.mult)
                last.then_inc(blk_ready, 1)

            def powers(w):
                cr = Pr[:, :, w - 1:w].to_broadcast([P, NST, w])
                ci = Pi[:, :, w - 1:w].to_broadcast([P, NST, w])
                tmp = ptmp[:, :, 0:w]
                for dst, x, y, op in ((Pr, cr, ci, ALU.subtract), (Pi, ci, cr, ALU.add)):
                    new = dst[:, :, w:2 * w]
                    link(v.tensor_tensor(tmp, Pr[:, :, 0:w], x, ALU.mult))
                    link(v.tensor_tensor(new, Pi[:, :, 0:w], y, ALU.mult))
                    settle()
                    link(v.tensor_tensor(new, tmp, new, op))
                    settle()

            def sample_states():
                for m in range(4):
                    dve.wait_ge(acc_read[m], 2)
                for j in range(4):
                    last = v.tensor_scalar(ublk[:, :, j, :], U[:, :, T:NT], maskJ[:, j:j + 1], None, ALU.mult)
                last.then_inc(ublk_ready, 1)
                side_read(dve, "s")
                b, read = side("bus")

                def bt(x):
                    return x.rearrange("p (b t) -> p b t", b=NB)
                ar = ab[:, 0].unsqueeze(1).to_broadcast([P, NB, NST])
                ai = ab[:, 1].unsqueeze(1).to_broadcast([P, NB, NST])
                for ri, (x, y, op) in enumerate(((ar, ai, ALU.subtract), (ai, ar, ALU.add))):
                    link(v.tensor_tensor(bt(st1[:, :]), bt(sT[:, 0]), x, ALU.mult))
                    link(v.tensor_tensor(bt(st2[:, :]), bt(sT[:, 1]), y, ALU.mult))
                    settle()
                    link(v.tensor_tensor(st1[:, :], st1[:, :], st2[:, :], op))
                    settle()
                    link(v.tensor_tensor(xs[:, ri].rearrange("p (b t) -> p t b", b=NB),
                                         st1[:, :].rearrange("p (b t) -> p t b", b=NB),
                                         b[:, ri * 256:(ri + 1) * 256].rearrange("p (t b) -> p t b", b=NB),
                                         ALU.add))
                    settle()
                v.memset(told, 0.0).then_inc(read, 1)

            def s5(tau):
                dve.wait_ge(bu_ready, tau + 1)
                bu = bank[4 + tau % 2][:, :].rearrange("p (r h t) -> p r h t", r=2, h=2)
                x = xst[:, tau % 2]

                def tab(tb, h):
                    if h:
                        return tb[:, tau, :].unsqueeze(1).unsqueeze(1).to_broadcast([P, 2, 2, HALF])
                    return tb[:, tau, :].unsqueeze(1).to_broadcast([P, 2, HALF])
                for ri in range(2):
                    pa = Pr[:, tau, :].unsqueeze(1).to_broadcast([P, 2, HALF])
                    pb = Pi[:, tau, :].unsqueeze(1).to_broadcast([P, 2, HALF])
                    link(v.tensor_tensor(wA[:, ri].rearrange("p (h t) -> p h t", h=2), bu[:, ri], pa, ALU.mult))
                    last = v.tensor_tensor(wB[:, ri].rearrange("p (h t) -> p h t", h=2), bu[:, ri], pb, ALU.mult)
                    if ri == 0:
                        link(last)
                last.then_inc(bu_read, 1)
                dve.wait_ge(bu_read, tau + 1)
                link(v.tensor_tensor(wA[:, 0], wA[:, 0], wB[:, 1], ALU.add))
                link(v.tensor_tensor(wA[:, 1], wA[:, 1], wB[:, 0], ALU.subtract))
                settle()
                if tau >= 2:
                    dve.wait_ge(xt_used, tau - 1)
                m = mag[:, tau:tau + 1].to_broadcast([P, HALF])
                for h in range(2):
                    hs = slice(h * HALF, (h + 1) * HALF)
                    for ri in range(2):
                        init = 0.0 if h == 0 else x[:, ri, HALF - 1:HALF]
                        link(v.tensor_tensor_scan(ws[:, ri, hs], m, wA[:, ri, hs], init, ALU.mult, ALU.add))
                    settle()
                    link(v.tensor_tensor(x[:, :, hs], ws[:, :, hs], tab(Pr, 0), ALU.mult))
                    link(v.tensor_tensor(wB[:, :, hs], ws[:, :, hs], tab(Pi, 0), ALU.mult))
                    settle()
                    link(v.tensor_tensor(x[:, 0, hs], x[:, 0, hs], wB[:, 1, hs], ALU.subtract))
                    last = v.tensor_tensor(x[:, 1, hs], x[:, 1, hs], wB[:, 0, hs], ALU.add)
                    if h == 0:
                        link(last)
                        settle()
                last.then_inc(xt_ready, 1)
                dve.wait_ge(xt_ready, tau + 1)
                settle()
                link(v.tensor_copy(fin[:, :, tau], x[:, :, T - 1]))

            def s5_y(k):
                b, read = side(("y", k))
                v.scalar_tensor_tensor(out=U[:, k, :], in0=U[:, k, :], scalar=dskip[:, k:k + 1],
                                       in1=b[:, 0:NT], op0=ALU.mult, op1=ALU.add).then_inc(read, 1)
                if k == KW - 1:
                    side_read(dve, ("y", k - 1))
                    side_read(dve, ("y", k))
                    settle()
                    v.memset(told, 0.0).then_inc(yt_ready, KW)

            def level(hg, i):
                H0, w = hg * HG, LEVELS[i - 1]
                if i >= 2:
                    dve.wait_ge(h_sc, 16 * hg + 2 * (i - 2) + 2)
                qv = Q[:, H0:H0 + HG, 0:T]
                kv = kk[:, :, 0:T]
                blocks = "p h (b u w) -> p h b u w"

                def half(x, u):
                    return x.rearrange(blocks, u=2, w=w)[:, :, :, u, :]
                if i <= 2:
                    last = v.tensor_tensor(qt[:, i % 2], qv, PP[:, :, :], ALU.mult)
                    if i == 2:
                        link(last)
                        last = v.tensor_tensor(kt[:, 0], kv, SS[:, :, :], ALU.mult)
                    last.then_inc(h_q, 1)
                else:
                    for h in range(HG):
                        link(v.tensor_tensor(
                            qt[:, i % 2, h].rearrange("p (b u w) -> p b u w", u=2, w=w)[:, :, 1, :],
                            Q[:, H0 + h, 0:T].rearrange("p (b u w) -> p b u w", u=2, w=w)[:, :, 1, :],
                            PP[:, h].rearrange("p (b u w) -> p b u w", u=2, w=w)[:, :, 1, :], ALU.mult))
                    if i == 3:
                        last = v.tensor_tensor(kt[:, 1], kv, SS[:, :, :], ALU.mult)
                    else:
                        for h in range(HG):
                            last = v.tensor_tensor(
                                kt[:, i % 2, h].rearrange("p (b u w) -> p b u w", u=2, w=w)[:, :, 0, :],
                                kk[:, h, 0:T].rearrange("p (b u w) -> p b u w", u=2, w=w)[:, :, 0, :],
                                SS[:, h].rearrange("p (b u w) -> p b u w", u=2, w=w)[:, :, 0, :], ALU.mult)
                            if h < HG - 1:
                                link(last)
                    last.then_inc(h_q, 1)
                dve.wait_ge(h_q, 7 * hg + i)
                pv = PP[:, :, :].rearrange("p h (b u w) -> p (h b) u w", u=2, w=w)
                sv = SS[:, :, :].rearrange("p h (b u w) -> p (h b) u w", u=2, w=w)
                nb_ = HG * T // (2 * w)
                link(v.tensor_tensor(sv[:, :, 0, :], sv[:, :, 0, :],
                                     pv[:, :, 1, w - 1:w].to_broadcast([P, nb_, w]), ALU.mult))
                settle()
                link(v.tensor_tensor(pv[:, :, 1, :], pv[:, :, 1, :],
                                     pv[:, :, 0, w - 1:w].to_broadcast([P, nb_, w]), ALU.mult))
                settle()

            def scores(hg, i):
                for hp in range(2):
                    n = 16 * hg + 2 * i + hp
                    dve.wait_ge(h_sc, n + 1)
                    if n % 16 >= 2:
                        dve.wait_ge(h_scread, n - 1)
                    v.copy_predicated(
                        Sc[:, 2 * hp:2 * hp + 2].rearrange("p h c t -> p (h c) t"),
                        masks[:, i, :].bitcast(U32).unsqueeze(1).to_broadcast([P, 4, 128]),
                        bank[4 + n % 2][:, :].rearrange("p (q t) -> p q t", q=4)).then_inc(h_scread, 1)

            def hgrn(hg, p):
                H0 = hg * HG
                if p == 0:
                    for m in range(4):
                        dve.wait_ge(acc_read[m], 6)
                    if hg == 0:
                        lower_bounds()
                        dve.wait_ge(xt_used, NST)
                    else:
                        dve.wait_ge(st_out, 16 * 5)
                    for h in range(H0, H0 + HG):
                        link(v.tensor_scalar(FG[:, h, :], FG[:, h, :], oml[:, h:h + 1], lb[:, h:h + 1],
                                             ALU.mult, ALU.add))
                    link(v.memset(SS[:, :, :], 1.0))
                    link(v.memset(Sc[:, :, :, :], 0.0))
                    settle()
                    v.tensor_scalar(kk[:, :, :], FG[:, H0:H0 + HG, :], -1.0, 1.0, ALU.mult, ALU.add).then_inc(
                        h_k, 1)
                    link(v.tensor_copy(PP[:, :, :], FG[:, H0:H0 + HG, 0:T]))
                    settle()
                    dve.wait_ge(h_k, hg + 1)
                    level(hg, 1)
                    scores(hg, 0)
                if 1 <= p <= 7:
                    if p < 7:
                        level(hg, p + 1)
                    else:
                        dve.wait_ge(h_sc, 16 * hg + 14)
                        v.tensor_tensor(kt[:, 0], kk[:, :, 0:T], SS[:, :, :], ALU.mult).then_inc(h_kts, 1)
                        link(v.tensor_tensor(qt[:, 0], Q[:, H0:H0 + HG, 0:T], PP[:, :, :], ALU.mult))
                        settle()
                    scores(hg, p)
                if p == 9:
                    side_read(dve, ("S", hg, 0))
                    b, read = side(("S", hg, 1))
                    side_read(dve, ("k", hg, 1))
                    for h in range(HG):
                        last = v.scalar_tensor_tensor(out=Sf[:, h, :], in0=S0[:, h, :],
                                                      scalar=PP[:, h, T - 1:T], in1=b[:, h * 128:(h + 1) * 128],
                                                      op0=ALU.mult, op1=ALU.add)
                        if h < HG - 1:
                            link(last)
                    last.then_inc(read, 1)
                    side_read(dve, ("S", hg, 1))
                    v.memset(told, 0.0).then_inc(h_fin, 1)
                if 10 <= p <= 13:
                    hh = p - 10
                    h = H0 + hh
                    dve.wait_ge(h_stq[h % 2], 16 * (h // 2 + 1))
                    for half in range(2):
                        b, read = side(("ou", hg, hh, half))
                        for s in range(4):
                            bs = half * 4 + s
                            last = v.scalar_tensor_tensor(out=stS[:, h % 2, bs, :], in0=stS[:, h % 2, bs, :],
                                                          scalar=FG[:, h, T + bs:T + bs + 1],
                                                          in1=b[:, s * 128:(s + 1) * 128],
                                                          op0=ALU.mult, op1=ALU.add)
                            if s < 3:
                                link(last)
                        last.then_inc(read, 1)
                    side_read(dve, ("ou", hg, hh, 0))
                    side_read(dve, ("ou", hg, hh, 1))
                    v.memset(told, 0.0).then_inc(h_new, 1)
                if p == 14:
                    b, read = side(("ms", hg))
                    v.tensor_scalar(rr[:, 0, :], b[0:HG, 0:NT], RMS_EPS, None, ALU.add).then_inc(read, 1)
                    side_read(dve, ("ms", hg))
                    v.memset(told, 0.0).then_inc(h_ms, 1)
                if p == 15:
                    dve.wait_ge(h_sqrt, hg + 1)
                    v.reciprocal(rr[:, 1, :], rr[:, 1, :]).then_inc(h_rstd, 1)
                    for hh in range(HG):
                        b, read = side(("rb", hg, hh))
                        h = H0 + hh
                        v.scalar_tensor_tensor(out=O4[:, hh, :], in0=O4[:, hh, :], scalar=gnorm[:, 0:1],
                                               in1=b[:, 0:NT], op0=ALU.mult, op1=ALU.mult).then_inc(read, 1)
                        side_read(dve, ("rb", hg, hh))
                        link(v.tensor_tensor(G[:, h, :], G[:, h, :], O4[:, hh, :], ALU.mult))
                    settle()
                    if hg == 1:
                        v.memset(told, 0.0).then_inc(h_done, 1)

            dve.wait_ge(xt_done, KD)
            low(0)
            for c in range(N_GLU):
                if c + 1 < 4 * SPLIT_IN:
                    low(c + 1)
                if c == 0:
                    dve.wait_ge(dt_exp, 1)
                    v.tensor_copy(parnat[:, 2, :].rearrange("t (g n) -> t g n", g=2),
                                  dtn[:, :].unsqueeze(2).to_broadcast([NST, 2, 64])).then_inc(dt_wide, 1)
                if c == 1:
                    params_1()
                if c == 2:
                    params_2()
                if c == 3:
                    input_matrix()
                if c == 4:
                    for w in (1, 2, 4, 8, 16):
                        powers(w)
                if c == 5:
                    output_matrix()
                if c == 6:
                    powers(32)
                if c == 7:
                    powers(64)
                if c == 9:
                    sample_states()
                for tau in s5_at.get(c, []):
                    s5(tau)
                    if tau % 4 == 1 and tau > 4:
                        s5_y(tau // 4 - 1)
                if c == S5_END:
                    s5_y(KW - 1)
                    b, read = side("fin")
                    v.tensor_copy(finT[:, :, :].rearrange("p r n -> p (r n)"), b[0:NST, 0:256]).then_inc(read, 1)
                    side_read(dve, "fin")
                    v.memset(told, 0.0).then_inc(outT, 1)
                    b, read = side("xso")
                    v.tensor_copy(xs[:, :, :].rearrange("p r n -> p (r n)"), b[:, :]).then_inc(read, 1)
                    side_read(dve, "xso")
                    v.memset(told, 0.0).then_inc(outT, 1)
                for hg, p in hg_at.get(c, []):
                    hgrn(hg, p)
                blk = c // 4
                if c % 4 == 3 and blk in (2, 3, 8, 9):
                    for m in range(4):
                        J = 4 * blk + m
                        n = (blk >= 8) * KW + J % KW
                        dve.wait_ge(sig_ready, n + 1)
                        v.tensor_tensor((Q, G)[blk >= 8][:, J % KW, :], bank[m][:, 0:NT], sigtmp[:, n % 2, :],
                                        ALU.mult).then_inc(acc_read[m], 1)

            low(N_GLU)
            dve.wait_ge(a_hi, 1)
            v.tensor_tensor(YGL[:, :, :], U[:, :, :], YGH[:, :, :].bitcast(F32), ALU.subtract).then_inc(a_lo, 1)
            dve.wait_ge(a_hi, 2)
            v.tensor_tensor(YBL[:, :, :], G[:, :, :], YBH[:, :, :].bitcast(F32), ALU.subtract).then_inc(a_lo, 1)

            def router(piece):
                if piece == 0:
                    b, read = side("log")
                    dve.wait_ge(r_ld, 64)
                    link(v.memset(lg8[:, :, :], -3.0e38))
                    link(v.memset(logit[:, :, :], 0.0))
                    settle()
                    for tt, (t0, tn) in enumerate(TOK):
                        last = v.tensor_tensor(logit[0:tn, tt, :], b[0:tn, tt * 36:(tt + 1) * 36],
                                               rbias[0:tn, :], ALU.add)
                        if tt < 2:
                            link(last)
                    last.then_inc(read, 1)
                    side_read(dve, "log")
                    settle()
                    link(v.tensor_copy(lg8[:, :, 0:4], logit[:, :, 0:4]))
                    settle()
                    for tt in range(3):
                        link(v.max(gmx[:, tt, :], lg8[:, tt, :]))
                    settle()
                    for tt in range(3):
                        link(v.max_index(gix[:, tt, :], gmx[:, tt, :], lg8[:, tt, :]))
                    v.tensor_tensor(gex[:, :, :], logit[:, :, 0:4], gmx[:, :, 0:1].to_broadcast([P, 3, 4]),
                                    ALU.subtract).then_inc(gm_neg, 1)
                    settle()
                    link(v.tensor_copy(gif[:, :, :], gix[:, :, :]))
                    settle()
                    last = v.tensor_tensor(oh[:, :, :], iota[:, 0:4].unsqueeze(1).to_broadcast([P, 3, 4]),
                                           gif[:, :, 0:1].to_broadcast([P, 3, 4]), ALU.is_equal)
                    last.then_inc(oh_ready, 1)
                    dve.wait_ge(oh_ready, 1)
                if piece == 1:
                    for g in range(GROUPS):
                        le = logit[:, :, 4 + 8 * g:12 + 8 * g]
                        w = oh[:, :, g:g + 1].to_broadcast([P, 3, 8])
                        dst = ing if g == 0 else ctmp
                        link(v.tensor_tensor(dst[:, :, :], le, w, ALU.mult))
                        settle()
                        if g:
                            link(v.tensor_tensor(ing[:, :, :], ing[:, :, :], ctmp[:, :, :], ALU.add))
                            settle()
                    for tt in range(3):
                        link(v.max(emx[:, tt, :], ing[:, tt, :]))
                    settle()
                    for tt in range(3):
                        link(v.max_index(eix[:, tt, :], emx[:, tt, :], ing[:, tt, :]))
                    v.tensor_tensor(rsm[:, :, 0], emx[:, :, 1], emx[:, :, 0], ALU.subtract).then_inc(e_diff, 1)
                    settle()
                    link(v.tensor_copy(eif[:, :, :], eix[:, :, :]))
                    settle()
                if piece == 2:
                    dve.wait_ge(r_exp, 1)
                    dve.wait_ge(r_exp2, 1)
                    link(v.tensor_reduce(rsm[:, :, 2:3], gex[:, :, :], AX_X, ALU.add))
                    link(v.tensor_scalar(rsm[:, :, 3], rsm[:, :, 1], 1.0, None, ALU.add))
                    settle()
                    link(v.tensor_tensor(rsm[:, :, 3], rsm[:, :, 3], rsm[:, :, 2], ALU.mult))
                    settle()
                    link(v.reciprocal(rsm[:, :, 3:4], rsm[:, :, 3:4]))
                    settle()
                    link(v.tensor_tensor(rsm[:, :, 4], rsm[:, :, 3], rsm[:, :, 1], ALU.mult))
                    settle()
                    for i in range(2):
                        dst = comb8 if i == 0 else ctmp
                        link(v.tensor_tensor(dst[:, :, :], iota[:, 0:8].unsqueeze(1).to_broadcast([P, 3, 8]),
                                             eif[:, :, i:i + 1].to_broadcast([P, 3, 8]), ALU.is_equal))
                        settle()
                        link(v.tensor_tensor(dst[:, :, :], dst[:, :, :],
                                             rsm[:, :, 3 + i:4 + i].to_broadcast([P, 3, 8]), ALU.mult))
                        settle()
                    link(v.tensor_tensor(comb8[:, :, :], comb8[:, :, :], ctmp[:, :, :], ALU.add))
                    settle()
                if piece == 3:
                    b, read = side("rank")
                    for tt, (t0, tn) in enumerate(TOK):
                        link(v.scalar_tensor_tensor(out=rank[0:tn, tt, :], in0=b[0:tn, 4 * tt:4 * tt + 4],
                                                    scalar=1.0, in1=oh[0:tn, tt, :], op0=ALU.add,
                                                    op1=ALU.mult))
                    link(v.tensor_reduce(flagf[:, 0:1], b[:, 16:20], AX_X, ALU.max))
                    settle()
                    v.memset(told, 0.0).then_inc(read, 1)
                    for tt, (t0, tn) in enumerate(TOK):
                        link(v.tensor_scalar(rank[0:tn, tt, :], rank[0:tn, tt, :], -1.0, None, ALU.add))
                    v.tensor_scalar(flag[:, :], flagf[:, 0:1], float(SLOTS), None, ALU.is_gt).then_inc(
                        flag_ready, 1)
                    settle()
                    select(0)

            def select(rnd):
                for g in range(GROUPS):
                    for tt, (t0, tn) in enumerate(TOK):
                        last = v.tensor_scalar(Sel[0:tn, tt, g, :], iota[0:tn, :], rank[0:tn, tt, g:g + 1],
                                               None, ALU.is_equal)
                        if (g, tt) != (GROUPS - 1, 2):
                            link(last)
                last.then_inc(sel_ready, 1)

            def statistics(j):
                for tt, (t0, tn) in enumerate(TOK):
                    b, read = side(("h", j, tt))
                    v.bn_stats(stats[0:tn, tt, j, :], b[0:tn, :]).then_inc(stat_done, 1)

            def deviations(tt, n, ready):
                v.bn_aggr(mv[0:n, tt, :], stats[0:n, tt, :, :].rearrange("p a b -> p (a b)")).then_inc(chain, 1)
                count[0] += 1
                settle()
                ready(v.tensor_scalar(rstd[0:n, tt:tt + 1], mv[0:n, tt, 1:2], LN_EPS, None, ALU.add))

            for n in range(N_GLU, N_END):
                for ahead in ahead_of(n):
                    low(ahead)
                if n < N_BA and n % 2 == 1:
                    blk = (n - N_GLU) // 2
                    for m in range(4):
                        J = 4 * blk + m
                        k = 2 * KW + J
                        dve.wait_ge(sig_ready, k + 1)
                        last = v.tensor_tensor(U[:, J, :], U[:, J, :], sigtmp[:, k % 2, :], ALU.mult)
                        last.then_inc(acc_read[m], 1)
                    dve.wait_ge(acc_read[3], BLK_GLU + blk + 1)
                    v.memset(told, 0.0).then_inc(a_raw, 1)
                    js = slice(4 * blk, 4 * blk + 4)
                    dve.wait_ge(a_hi, 3 + blk)
                    v.tensor_tensor(YAL[:, js, :], U[:, js, :], YAH[:, js, :].bitcast(F32),
                                    ALU.subtract).then_inc(a_lo, 1)
                if N_BA <= n < N_BB and n % 2 == 1:
                    for m in range(4):
                        J = 4 * ((n - N_BA) // 2) + m
                        summed(dve, BLK_BA + J // 4, m)
                        v.tensor_tensor(GA[:, J, :], bank[m][:, 0:NT], GA[:, J, :], ALU.mult).then_inc(
                            acc_read[m], 1)
                if N_BB <= n < N_O and n % 2 == 1:
                    blk = (n - N_BB) // 2
                    for m in range(4):
                        J = 4 * blk + m
                        summed(dve, BLK_BB + blk, m)
                        v.tensor_tensor(GB[:, J, :], bank[m][:, 0:NT], GB[:, J, :], ALU.mult).then_inc(
                            acc_read[m], 1)
                    js = slice(4 * blk, 4 * blk + 4)
                    for m in range(4):
                        dve.wait_ge(acc_read[m], BLK_BB + blk + 1)
                    v.tensor_tensor(GA[:, js, :], GA[:, js, :], GB[:, js, :], ALU.add).then_inc(a_raw, 1)
                    dve.wait_ge(a_hi, 5 + blk)
                    v.tensor_tensor(ML[:, js, :], GA[:, js, :], MH[:, js, :].bitcast(F32),
                                    ALU.subtract).then_inc(a_lo, 1)
                if n == N_O:
                    for k in range(2):
                        b, read = side(f"p{k}")
                        dve.wait_ge(pt_hi, k + 1)
                        v.tensor_tensor(pTl[:, k, :], b[:, 0:NT], pTh[:, k, :].bitcast(F32),
                                        ALU.subtract).then_inc(read, 1)
                    dve.wait_ge(wr_hi, 1)
                    v.tensor_tensor(wrl[:, :, :], wrr[:, :, :], wrh[:, :, :].bitcast(F32),
                                    ALU.subtract).then_inc(wr_lo, 1)
                if N_O + 4 < n < N_PP and (n - N_O) % 4 == 2:
                    statistics((n - N_O) // 4 - 1)
                if N_O <= n < N_PP and (n - N_O) % 4 == 3:
                    for m in range(4):
                        J = n - N_O - 3 + m
                        summed(dve, BLK_O + J // 4, m)
                        v.scalar_tensor_tensor(out=XT[:, J, :], in0=XT[:, J, :], scalar=ALPHA,
                                               in1=bank[m][:, 0:NT], op0=ALU.mult, op1=ALU.add).then_inc(
                            acc_read[m], 1)
                    for m in range(4):
                        dve.wait_ge(acc_read[m], BLK_O + (n - N_O) // 4 + 1)
                    v.memset(told, 0.0).then_inc(hpre, 1)
                if n == N_PP - 1:
                    statistics(3)
                    dve.wait_ge(stat_done, 12)
                    link(v.memset(mv[:, :, :], 0.0))
                    link(v.memset(rstd[:, :], 1.0))
                    settle()
                    for tt, (t0, tn) in enumerate(TOK):
                        deviations(tt, tn, link)
                    settle()
                    v.memset(told, 0.0).then_inc(ln_var, 1)
                    dve.wait_ge(ln_sq, 1)
                    link(v.reciprocal(rstd[:, :], rstd[:, :]))
                    settle()
                    v.scalar_tensor_tensor(out=nmr[:, :], in0=mv[:, :, 0], scalar=-1.0, in1=rstd[:, :],
                                           op0=ALU.mult, op1=ALU.mult).then_inc(ln_nmr, 1)
                    dve.wait_ge(ln_ld, 32)
                    for tt, (t0, tn) in enumerate(TOK):
                        dve.wait_ge(ln_norm, tt + 1)
                        link(v.tensor_tensor(htok[0:tn, tt, :], htok[0:tn, tt, :], ln1[0:tn, 0, :], ALU.mult))
                        settle()
                        v.tensor_tensor(htok[0:tn, tt, :], htok[0:tn, tt, :], ln1[0:tn, 1, :],
                                        ALU.add).then_inc(h_ready, 1)
                if n == N_PG - 1:
                    for k in range(KD):
                        b, read = side(("ht", k))
                        dve.wait_ge(ht_hi, k + 1)
                        v.tensor_tensor(HTL[:, k, :], b[:, 0:NT], HTH[:, k, :].bitcast(F32),
                                        ALU.subtract).then_inc(read, 1)
                if n >= N_PG:
                    i = n - N_PG
                    if i % 4 == 3:
                        for m in range(4):
                            J = i - 3 + m
                            k = 3 * KW + J
                            dve.wait_ge(sig_ready, k + 1)
                            v.tensor_tensor(PPT[:, J, :], PPT[:, J, :], sigtmp[:, k % 2, :], ALU.mult).then_inc(
                                acc_read[m], 1)
                        for m in range(4):
                            dve.wait_ge(acc_read[m], BLK_PG + i // 4 + 1)
                        v.memset(told, 0.0).then_inc(ple_ready, 1)
                    if i in (4, 6, 12, 14):
                        router((4, 6, 12, 14).index(i))
                    if (i % 4 == 2 and i > 4) or i == 15:
                        j = 3 if i == 15 else i // 4 - 1
                        for tt, (t0, tn) in enumerate(TOK):
                            b, read = side(("ple", j, tt))
                            cs = slice(j * 512, (j + 1) * 512)
                            v.scalar_tensor_tensor(out=atok[0:tn, tt, cs], in0=htok[0:tn, tt, cs],
                                                   scalar=ALPHA, in1=b[0:tn, :], op0=ALU.mult,
                                                   op1=ALU.add).then_inc(read, 1)

            def gather(rnd, g):
                gg = rnd * GROUPS + g
                for kq in range(4):
                    b, read = side(("ga", rnd, g, kq))
                    dve.wait_ge(hg_hi, 4 * gg + kq + 1)
                    ks = slice(4 * kq, 4 * kq + 4)
                    v.tensor_tensor(hgl[:, gg % 2, ks, :].rearrange("p k s -> p (k s)"), b[:, :],
                                    hgh[:, gg % 2, ks, :].rearrange("p k s -> p (k s)").bitcast(F32),
                                    ALU.subtract).then_inc(read, 1)

            def scatter(rnd, g):
                for tt, (t0, tn) in enumerate(TOK):
                    for nb in range(4):
                        b, read = side(("sc", rnd, g, tt, nb))
                        cs = slice(nb * 512, (nb + 1) * 512)
                        v.tensor_tensor(atok[0:tn, tt, cs], atok[0:tn, tt, cs], b[0:tn, :],
                                        ALU.add).then_inc(read, 1)
                side_read(dve, ("sc", rnd, g, 2, 2))
                side_read(dve, ("sc", rnd, g, 2, 3))

            def lows(n, which):
                for s in which:
                    if s < 4:
                        dve.wait_ge(g_hi, 4 * n + s + 1)
                        v.tensor_tensor(mlo[s], mraw[s], mhi[s % 3].bitcast(F32), ALU.subtract).then_inc(g_lo, 1)
                    else:
                        dve.wait_ge(d_hi, 2 * n + s - 5)
                        v.tensor_tensor(mlo[s], mraw[s], mhi[s % 3].bitcast(F32), ALU.subtract).then_inc(d_lo, 1)

            def hidden(n, g, e):
                dve.wait_ge(silu_done, n)
                v.scalar_tensor_tensor(out=hid[:, :], in0=bank[4][:, FE:2 * FE], scalar=combg[:, g % 2, e],
                                       in1=gsil[:, :], op0=ALU.mult, op1=ALU.mult).then_inc(hid_done, 1)

            def hidden_low(n):
                dve.wait_ge(hidT_hi, n)
                v.tensor_tensor(hidL[:, :, :].rearrange("p j s -> p (j s)"), bank[5][:, 0:256],
                                hidH[:, :, :].rearrange("p j s -> p (j s)").bitcast(F32),
                                ALU.subtract).then_inc(hidT_lo, 1)

            def turn(n, g, e):
                hidden(n, g, e)
                lows(n, (0, 1, 2))
                hidden_low(n)
                lows(n, (3, 4, 5))

            def expert_round(rnd):
                if rnd:
                    for tt, (t0, tn) in enumerate(TOK):
                        link(v.tensor_scalar(rank[0:tn, tt, :], rank[0:tn, tt, :], -float(SLOTS), None, ALU.add))
                    settle()
                    dve.wait_ge(misc_ready, misc[("ga", rnd - 1, GROUPS - 1, 3)] + 1)
                    select(rnd)
                gather(rnd, 0)
                for g in range(GROUPS):
                    gg = rnd * GROUPS + g
                    n0 = EPG * gg
                    if g == 0:
                        lows(n0, (0, 1, 2, 3))
                    else:
                        turn(n0, g - 1, slice(EPG - 1, EPG))
                    side_read(dve, ("cg", rnd, g))
                    turn(n0 + 1, g, slice(0, 1))
                    if g:
                        scatter(rnd, g - 1)
                    if g + 1 < GROUPS:
                        gather(rnd, g + 1)
                    with dve.Fori(n0 + 2, n0 + EPG) as n:
                        turn(n, g, bass.ds(n - (n0 + 1), 1))
                n1 = EPG * GROUPS * (rnd + 1)
                hidden(n1, GROUPS - 1, slice(EPG - 1, EPG))
                hidden_low(n1)
                for s in (4, 5):
                    dve.wait_ge(d_hi, 2 * n1 + s - 5)
                    v.tensor_tensor(mlo[s], mraw[s], mhi[s % 3].bitcast(F32), ALU.subtract).then_inc(d_lo, 1)
                scatter(rnd, GROUPS - 1)

            expert_round(0)
            dve.wait_ge(flag_ready, 1)
            more = dve.value_load(flag[0:1, 0:1], min_val=0, max_val=1)
            with dve.If(more > 0):
                for rnd in range(1, ROUNDS):
                    expert_round(rnd)
            tail = sem("final_chain")
            done = 0
            for tt, (t0, tn) in enumerate(TOK):
                for j in range(4):
                    v.bn_stats(stats[0:tn, tt, j, :], atok[0:tn, tt, j * 512:(j + 1) * 512]).then_inc(tail, 1)
                done += 4
                dve.wait_ge(tail, done)
                v.bn_aggr(mv[0:tn, tt, :], stats[0:tn, tt, :, :].rearrange("p a b -> p (a b)")).then_inc(tail, 1)
                done += 1
                dve.wait_ge(tail, done)
                v.tensor_scalar(rstd[0:tn, tt:tt + 1], mv[0:tn, tt, 1:2], LN_EPS, None, ALU.add).then_inc(f_var, 1)
                dve.wait_ge(f_sq, tt + 1)
                v.reciprocal(rstd[0:tn, tt:tt + 1], rstd[0:tn, tt:tt + 1]).then_inc(tail, 1)
                done += 1
                dve.wait_ge(tail, done)
                v.scalar_tensor_tensor(out=nmr[0:tn, tt:tt + 1], in0=mv[0:tn, tt, 0:1], scalar=-1.0,
                                       in1=rstd[0:tn, tt:tt + 1], op0=ALU.mult, op1=ALU.mult).then_inc(f_nmr, 1)
            dve.wait_ge(ln2_ld, 32)
            for tt, (t0, tn) in enumerate(TOK):
                dve.wait_ge(f_norm, tt + 1)
                v.tensor_tensor(atok[0:tn, tt, :], atok[0:tn, tt, :], ln2[0:tn, 0, :], ALU.mult).then_inc(tail, 1)
                done += 1
                dve.wait_ge(tail, done)
                v.tensor_tensor(atok[0:tn, tt, :], atok[0:tn, tt, :], ln2[0:tn, 1, :], ALU.add).then_inc(f_out, 1)


_INS = ["x_prompt", "x_sample", "p_prompt", "p_sample", "state_s5_re", "state_s5_im", "state_hgrn", "w_in",
        "s5_lambda_re", "s5_lambda_im", "s5_log_dt", "s5_b_re", "s5_b_im", "s5_c_re", "s5_c_im", "s5_d",
        "s5_w_glu", "hg_lower_bounds", "hg_norm_gain", "w_branch_a", "w_branch_b", "w_out", "ln1_gain",
        "ln1_bias", "w_group_router", "b_group_router", "w_expert_router", "b_expert_router", "w_exp_gate",
        "w_exp_up", "w_exp_down", "w_ple_proj", "w_ple_gate", "ln2_gain", "ln2_bias"]
_OUTS = [(1, T, D), (NB, 1, D), (1, 1, 64, 64), (1, 1, 64, 64), (1, 1, HEADS, 128, 128),
         (1, NB, 64, 64), (1, NB, 64, 64), (1, NB, HEADS, 128, 128)]


def kernel(**inputs):
    import concourse.bacc as _bacc
    from concourse.bass_utils import run_bass_kernel_spmd as _run

    nc = _bacc.Bacc("TRN2", target_bir_lowering=False, num_devices=1, dynamic_dma_scratch_size=8192)
    arrays, args = {}, {}
    for name in _INS + ["consts"]:
        a = shape_constants() if name == "consts" else np.ascontiguousarray(inputs[name])
        arrays[f"in_{name}"] = a
        args[name] = nc.dram_tensor(f"in_{name}", a.shape, mybir.dt.from_np(a.dtype), kind="ExternalInput").ap()
    outs = [nc.dram_tensor(f"out_{i}", shape, F32, kind="ExternalOutput").ap() for i, shape in enumerate(_OUTS)]
    build(nc, args, outs)
    r = _run(nc, [arrays], core_ids=[0])
    return tuple(r.results[0][f"out_{i}"] for i in range(len(_OUTS)))
```

```python
from contextlib import ExitStack

import numpy as np
import concourse.bass as bass
from concourse import mybir

F32 = mybir.dt.float32
F32R = mybir.dt.float32r
I32 = mybir.dt.int32
U32 = mybir.dt.uint32
ALU = mybir.AluOpType
ACT = mybir.ActivationFunctionType
AX_X = mybir.AxisListType.X

P = 128
D = 2048
KD = D // P
T = 256
NB = 8
NT = T + NB
HALF = 128
W = 1024
KW = W // P
NST = 32
HEADS = 8
HG = 4
GROUPS, EPG, FE = 4, 8, 256
SLOTS = 128
ROUNDS = 3
ALPHA = 2.0 ** 0.25
LN_EPS, RMS_EPS = 1e-5, 1e-6
TOK = [(0, 128), (128, 128), (256, 8)]
NORM_ORDER = (2, 0, 1)
LEVELS = [1, 2, 4, 8, 16, 32, 64]

C_ID, C_LT, C_IO, C_MJ, C_MC, C_MB, C_CS = 0, 128, 256, 384, 388, 390, 392
C_RS = 408
C_MASK = C_RS + 512
C_END = C_MASK + 8 * 128


def shape_constants():
    r = np.arange(128)
    c = np.zeros((128, C_END), np.float32)
    c[:, C_ID:C_ID + 128] = np.eye(128)
    c[:, C_LT:C_LT + 128] = r[:, None] < r[None, :]
    c[:, C_IO:C_IO + 128] = r[None, :]
    c[:, C_MJ:C_MJ + 4] = (r[:, None] // 32) == np.arange(4)
    c[:, C_MC:C_MC + 2] = ((r[:, None] // 16) % 2) == np.arange(2)
    c[:, C_MB:C_MB + 2] = (r[:, None] // 64) == np.arange(2)
    for h in range(HG):
        c[:, C_CS + h * HG + h] = 1.0 / 128
        c[h, C_RS + h * 128:C_RS + (h + 1) * 128] = 1.0
    c[:, C_MASK:C_MASK + 128] = np.eye(128)
    for n, w in enumerate(LEVELS):
        s, t = r[:, None], r[None, :]
        c[:, C_MASK + (n + 1) * 128:C_MASK + (n + 2) * 128] = (
            (s // (2 * w) == t // (2 * w)) & (s // w % 2 == 0) & (t // w % 2 == 1))
    return c


RD = 4
RH = 2
BLK_IN, BLK_GLU, BLK_BB, BLK_BA, BLK_O, BLK_PP, BLK_PG = 0, 18, 20, 24, 28, 32, 36
N_IN, N_GLU, N_BB, N_BA, N_O, N_PP, N_PG, N_END = 0, 72, 76, 84, 92, 108, 110, 126
SPLIT_IN = 8


def is_split(n):
    return n < 4 * SPLIT_IN or n >= N_GLU


def split_count(n):
    return n if n <= 4 * SPLIT_IN else (4 * SPLIT_IN if n <= N_GLU else n - N_GLU + 4 * SPLIT_IN)


def build(nc, t, outs):
    base = (nc.sbuf_base + 63) // 64 * 64
    end = nc.sbuf_usable_end

    R_CONST = base
    R_XT = R_CONST + 17920
    R_Z = R_XT + KD * NT * 4
    ZSZ = KW * NT * 4
    R_GAB = R_Z + 5 * ZSZ
    R_RAW = R_GAB + 2 * KD * NT * 4
    R_HI = R_RAW + RD * 8192
    R_AR = R_HI + RH * 8192
    assert R_AR + 59520 <= end

    used_const = [R_CONST]

    def at(name, off, shape, dt=F32):
        return nc.alloc_sbuf_tensor_at(name, shape, dt, offset=off)

    def const(name, shape, dt=F32):
        size = 4
        for s in shape[1:]:
            size *= s
        off = used_const[0]
        used_const[0] = off + (size + 31) // 32 * 32
        assert used_const[0] <= R_XT, name
        return at(name, off, shape, dt)

    ident = const("ident", [P, 128])
    lowtri = const("lowtri", [P, 128])
    iota = const("iota", [P, 128])
    ones = const("ones", [P, 128])
    small = const("small", [P, 24])
    maskJ, maskC, maskB = small[:, 0:4], small[:, 4:6], small[:, 6:8]
    colsel = small[:, 8:24].rearrange("p (h m) -> p h m", h=HG)
    rowsel = const("rowsel", [HG, HG, 128])
    masks = const("masks", [P, 8, 128])
    dskip = const("dskip", [P, KW])
    gnorm = const("gnorm", [P, 1])
    lbraw = const("lbraw", [P, KW])
    lb = const("lb", [P, KW])
    oml = const("oml", [P, KW])
    sigtmp = const("sigtmp", [P, 2, NT])
    xs = const("xs", [P, 2, 256])
    fin = const("fin", [P, 2, NST])
    finT = const("finT", [NST, 2, 128])
    ab = const("ab", [P, 2, NST])
    mag = const("mag", [P, NST])
    stats = const("stats", [P, 3, 4, 6])
    mv = const("mv", [P, 3, 2])
    rstd = const("rstd", [P, 3])
    nmr = const("nmr", [P, 3])

    XT = at("XT", R_XT, [P, KD, NT])
    U = at("U", R_Z, [P, KW, NT])
    Q = at("Q", R_Z + ZSZ, [P, KW, NT])
    FG = at("FG", R_Z + 2 * ZSZ, [P, KW, NT])
    IV = at("IV", R_Z + 3 * ZSZ, [P, KW, NT])
    G = at("G", R_Z + 4 * ZSZ, [P, KW, NT])
    GA = at("GA", R_GAB, [P, KD, NT])
    GB = at("GB", R_GAB + KD * NT * 4, [P, KD, NT])
    XH = at("XH", R_GAB, [P, KD, NT], F32R)
    XL = at("XL", R_GAB + KD * NT * 4, [P, KD, NT], F32R)
    raw = at("raw", R_RAW, [P, RD, 2048])
    lo = at("lo", R_RAW, [P, RD, 2048], F32R)
    hi = at("hi", R_HI, [P, RH, 2048], F32R)

    xtok = at("xtok", R_AR, [P, 3, D])
    Pr = at("Pr", R_AR, [P, NST, HALF])
    Pi = at("Pi", R_AR + 16384, [P, NST, HALF])
    BBT = at("BBT", R_AR + 32768, [P, 2, KW, 128])
    CT = at("CT", R_AR + 40960, [P, 2, KW, 128])
    wA = at("wA", R_AR + 49152, [P, 2, T])
    wB = at("wB", R_AR + 51200, [P, 2, T])
    ws = at("ws", R_AR + 53248, [P, 2, T])
    xst = at("xst", R_AR + 55296, [P, 2, 2, T])
    o = R_Z + 3 * ZSZ
    braw = at("braw", o, [P, 2, NST, 16])
    craw = at("craw", o + 4096, [P, 2, KW, 64])
    o = R_Z + 4 * ZSZ
    yblk = at("yblk", o, [P, 2, NST, 32])
    o = R_Z + ZSZ
    ptmp = at("ptmp", o, [P, NST, 64])
    o = R_Z + 2 * ZSZ
    bbz = at("bbz", o, [P, 2, NST, 16])
    btmp = at("btmp", o + 4096, [P, NST, 16])
    par = at("par", o + 6144, [P, 16, NST])

    o = R_AR + 49152
    parnat = at("parnat", o, [NST, 3, 128])
    snat = at("snat", o + 1536, [P, 2, 2, 128])
    dtn = at("dtn", o + 3584, [NST, 2])
    sT = at("sT", o + 3616, [P, 2, 256])
    ublk = at("ublk", o + 5664, [P, KW, 4, NB])
    st1 = at("st1", o + 6688, [P, 256])
    st2 = at("st2", o + 7712, [P, 256])
    assert o + 8736 <= R_AR + 59392
    PP = at("PP", R_AR, [P, HG, T])
    SS = at("SS", R_AR + 4096, [P, HG, T])
    kt = at("kt", R_AR + 8192, [P, 2, HG, T])
    qt = at("qt", R_AR + 16384, [P, 2, HG, T])
    Sc = at("Sc", R_AR + 24576, [P, HG, 2, 128])
    kk = at("kk", R_AR + 28672, [P, HG, NT])
    ktok = at("ktok", R_AR + 32896, [P, 2, HG, 128])
    vtok = at("vtok", R_AR + 36992, [P, 2, HG, 128])
    S0 = at("S0", R_AR + 41088, [P, HG, 128])
    stS = at("stS", R_AR + 43136, [P, 2, NB, 128])
    sktok = at("sktok", R_AR + 51328, [NB, HG * 128])
    svtok = at("svtok", R_AR + 53376, [NB, HG * 128])
    svblk = at("svblk", R_AR + 55424, [NB, NB, 128])
    Sf = at("Sf", R_AR + 4096, [P, HG, 128])
    O4 = at("O4", R_AR + 8192, [P, HG, NT])
    sq = at("sq", R_AR + 12448, [P, HG, NT])
    rr = at("rr", R_AR + 24576, [HG, 2, NT])
    YGH = at("YGH", R_AR, [P, KW, NT], F32R)
    YGL = at("YGL", R_AR + ZSZ, [P, KW, NT], F32R)
    YAH = at("YAH", R_AR + 2 * ZSZ, [P, KW, NT], F32R)
    YAL = at("YAL", R_AR + 3 * ZSZ, [P, KW, NT], F32R)
    YBH = at("YBH", R_AR + 4 * ZSZ, [P, KW, NT], F32R)
    YBL = at("YBL", R_AR + 5 * ZSZ, [P, KW, NT], F32R)
    MH = at("MH", R_Z + ZSZ, [P, KD, NT], F32R)
    ML = at("ML", R_Z + 3 * ZSZ, [P, KD, NT], F32R)
    htok = at("htok", R_AR, [P, 3, D])
    ln1 = at("ln1", R_AR + 24576, [P, 2, D])
    wrr = at("wrr", R_AR + 40960, [P, KD, 36])
    wrh = at("wrh", R_AR + 43264, [P, KD, 36], F32R)
    wrl = at("wrl", R_AR + 45568, [P, KD, 36], F32R)
    rbias = at("rbias", R_AR + 47872, [P, 36])
    ptok = at("ptok", R_AR + 51200, [P, 3, 256])
    pTh = at("pTh", R_AR + 54272, [P, 2, NT], F32R)
    pTl = at("pTl", R_AR + 56384, [P, 2, NT], F32R)
    HTH = at("HTH", R_GAB, [P, KD, NT], F32R)
    HTL = at("HTL", R_GAB + KD * NT * 4, [P, KD, NT], F32R)
    PPT = at("PPT", R_Z + 3 * ZSZ, [P, KD, NT])
    atok = at("atok", R_Z, [P, 3, D])
    outgh = at("outgh", R_XT, [P, D], F32R)
    outgl = at("outgl", R_Z + 3 * ZSZ, [P, D], F32R)
    Sel = at("Sel", R_XT + 8192, [P, 3, GROUPS, SLOTS])
    SelT = at("SelT", R_XT + 14336, [P, 2, NT], F32R)
    hgh = at("hgh", R_AR + 24576, [P, 2, KD, SLOTS], F32R)
    hgl = at("hgl", R_AR + 40960, [P, 2, KD, SLOTS], F32R)
    XR = R_GAB
    mraw = [raw[:, 0], raw[:, 1], raw[:, 2], raw[:, 3],
            at("raw4", XR, [P, 2048])[:, :], at("raw5", XR + 8192, [P, 2048])[:, :]]
    mlo = [lo[:, 0], lo[:, 1], lo[:, 2], lo[:, 3],
           at("lo4", XR, [P, 2048], F32R)[:, :], at("lo5", XR + 8192, [P, 2048], F32R)[:, :]]
    mhi = [hi[:, 0], hi[:, 1], at("hi2", XR + 16384, [P, 2048], F32R)[:, :]]
    gsil = at("gsil", XR + 24576, [P, FE])
    hid = at("hid", XR + 25600, [P, FE])
    hidH = at("hidH", XR + 26624, [P, 2, SLOTS], F32R)
    hidL = at("hidL", XR + 27648, [P, 2, SLOTS], F32R)
    combg = at("combg", XR + 28672, [P, 2, EPG])
    ln2 = at("ln2", R_RAW + 2 * 8192, [P, 2, D])
    logit = at("logit", R_AR + 48032, [P, 3, 36])
    logT = at("logT", R_AR + 50048, [36, NT])
    lg8 = at("lg8", R_AR + 48480, [P, 3, 8])
    gmx = at("gmx", R_AR + 48576, [P, 3, 8])
    gix = at("gix", R_AR + 48672, [P, 3, 8], U32)
    gif = at("gif", R_AR + 48768, [P, 3, 8])
    ing = at("ing", R_AR + 48864, [P, 3, 8])
    emx = at("emx", R_AR + 48960, [P, 3, 8])
    eix = at("eix", R_AR + 49056, [P, 3, 8], U32)
    eif = at("eif", R_AR + 49152, [P, 3, 8])
    gex = at("gex", R_AR + 49248, [P, 3, 4])
    rsm = at("rsm", R_AR + 49312, [P, 3, 8])
    ctmp = at("ctmp", R_AR + 49408, [P, 3, 8])
    oh = const("oh", [P, 3, GROUPS])
    comb8 = const("comb8", [P, 3, EPG])
    rank = const("rank", [P, 3, GROUPS])
    flagf = const("flagf", [P, 2])
    flag = const("flag", [P, 1], I32)

    with ExitStack() as ctx:
        def sem(name):
            return ctx.enter_context(nc.semaphore(name))

        bank = [ctx.enter_context(nc.psum_tensor(f"bank{n}", [P, 512], F32)) for n in range(8)]

        s_const, s_id, s_vec = sem("const_loaded"), sem("identity_loaded"), sem("vectors_loaded")
        s_x = [sem("x_left_loaded"), sem("x_right_loaded")]
        s_par, s_bc = sem("s5_params_loaded"), sem("s5_bc_loaded")
        ln_ld, p_ld, r_ld, ln2_ld = sem("ln1_loaded"), sem("p_loaded"), sem("router_loaded"), sem("ln2_loaded")
        landed = [sem(f"chunk_landed{s}") for s in range(RD)]
        g_land = [sem(f"gate_up_landed{s}") for s in range(4)]
        d_land = [sem(f"down_landed{s}") for s in range(2)]
        hi_done, lo_done, chunk_used = sem("high_done"), sem("low_done"), sem("chunk_used")
        acc_ready = sem("tile_summed")
        acc_read = [sem(f"bank{m}_read") for m in range(4)]
        sig_ready = sem("sigmoid_ready")
        misc_ready = sem("side_bank_ready")
        misc_read = {b: sem(f"side_bank{b}_read") for b in (4, 5, 6, 7)}
        chain = sem("vector_chain")
        xh_done, xt_done = sem("x_high_done"), sem("x_split_done")
        a_hi, a_lo, a_raw = sem("act_high"), sem("act_low"), sem("act_raw")
        s_ones = sem("ones_set")
        lb_diff, lb_exp = sem("lower_bound_diff"), sem("lower_bound_exp")
        dt_exp, dt_wide = sem("dt_exp"), sem("dt_wide")
        ang_ready, trig_done, abs_done = sem("angle_ready"), sem("trig_done"), sem("abs_done")
        tab_part, tab_done = sem("table_products"), sem("table_sums")
        blk_ready, ublk_ready = sem("block_forms_ready"), sem("sample_u_ready")
        bu_ready, bu_read = sem("bu_ready"), sem("bu_read")
        xt_ready, xt_used = sem("s5_x_ready"), sem("s5_x_used")
        yt_ready, gelu_done = sem("y_ready"), sem("gelu_done")
        outT, st_out = sem("states_transposed"), sem("stores_done")
        h_k, h_q, h_sc, h_scread = sem("hg_k_ready"), sem("hg_level_ready"), sem("hg_scores"), sem("hg_scores_read")
        h_kts, h_blk, h_new = sem("hg_k_decayed"), sem("hg_v_spread"), sem("hg_state_new")
        h_stq = [sem("hg_state_in0"), sem("hg_state_in1")]
        h_sto = [sem("hg_state_out0"), sem("hg_state_out1")]
        h_ms, h_sqrt, h_rstd = sem("hg_ms"), sem("hg_sqrt"), sem("hg_rstd")
        h_fin, h_done = sem("hg_final"), sem("hg_done")
        hpre, stat_done = sem("h_pre_ready"), sem("stats_taken")
        ln_var, ln_sq, ln_nmr, ln_norm = sem("variance"), sem("deviation"), sem("ln_scalars"), sem("normalized")
        gained, small_gain = sem("gained"), sem("small_tile_gain")
        h_ready, h_small = sem("h_ready"), sem("h_small_tile_ready")
        pt_hi, ht_hi = sem("p_high"), sem("h_high")
        wr_hi, wr_lo = sem("router_high"), sem("router_low")
        r_exp, r_exp2 = sem("group_exp"), sem("expert_exp")
        gm_neg, e_diff = sem("group_max"), sem("expert_diff")
        oh_ready, sel_ready, flag_ready = sem("groups_chosen"), sem("selection_ready"), sem("flag_ready")
        ple_ready = sem("ple_ready")
        hg_hi = sem("gathered_high")
        g_hi, g_lo, g_used = sem("gate_up_high"), sem("gate_up_low"), sem("gate_up_used")
        d_hi, d_lo, d_used = sem("down_high"), sem("down_low"), sem("down_used")
        silu_done, hid_done = sem("silu_done"), sem("hidden_done")
        hidT_ready, hidT_hi, hidT_lo = sem("hidden_transposed"), sem("hidden_high"), sem("hidden_low")
        outg_done, outg_low = sem("group_stored_high"), sem("group_stored_low")
        final_vectors = sem("final_vectors_there")
        f_var, f_sq, f_nmr, f_norm = (sem("final_variance"), sem("final_deviation"), sem("final_scalars"),
                                      sem("final_normalized"))
        f_small, f_out = sem("final_small_tile_ready"), sem("final_ready")
        y_out = sem("y_stored")

        def chunk(n):
            def view(w, kq, cb, nk, nc_):
                return w[0, kq * nk * 128:(kq + 1) * nk * 128, cb * nc_:(cb + 1) * nc_].rearrange(
                    "(k p) n -> p k n", p=P)
            if n < N_GLU:
                return view(t["w_in"], n % 4, n // 4, 4, 512)
            if n < N_BB:
                return view(t["s5_w_glu"], (n - N_GLU) % 2, (n - N_GLU) // 2, 4, 512)
            if n < N_BA:
                return view(t["w_branch_b"], (n - N_BB) % 2, (n - N_BB) // 2, 4, 512)
            if n < N_O:
                return view(t["w_branch_a"], (n - N_BA) % 2, (n - N_BA) // 2, 4, 512)
            if n < N_PP:
                return view(t["w_out"], (n - N_O) % 4, (n - N_O) // 4, 4, 512)
            if n < N_PG:
                return view(t["w_ple_proj"], 0, n - N_PP, 2, 1024)
            return view(t["w_ple_gate"], (n - N_PG) % 4, (n - N_PG) // 4, 4, 512)

        def ahead_of(n):
            return {N_PP - 1: (N_PP, N_PP + 1), N_PP: (), N_END - 1: ()}.get(n, (n + 1,))

        s5_at = {}
        for tau in range(NST):
            c = 12 + 2 * tau if tau < 10 else 32 + (tau - 10) * 4 // 5
            s5_at.setdefault(c, []).append(tau)
        S5_END = 32 + 21 * 4 // 5 + 1
        hg_at = {}
        steps = [0, 1, 1.7, 2.4, 3.1, 3.8, 4.5, 5.2, 6, 6, 6.8, 7.4, 8, 8.6, 9.2, 10]
        for hg in range(2):
            for p, at_ in enumerate(steps):
                hg_at.setdefault(S5_END + 1 + int(at_ + 11 * hg), []).append((hg, p))
        misc = {}
        uses = {4: 0, 5: 0, 6: 0, 7: 0}

        def side_read(eng, name):
            n, b, use = misc[name]
            eng.wait_ge(misc_read[b], use)

        def summed(eng, blk, m):
            if BLK_PP <= blk < BLK_PG:
                i, half = divmod(blk - BLK_PP, 2)
                if (half, m) == (1, 3):
                    eng.wait_ge(chunk_used, N_PP + i + 1)
                else:
                    eng.wait_ge(acc_ready, 3 * BLK_PP + 7 * i + 4 * half + m + 1)
                return
            if m < 3:
                eng.wait_ge(acc_ready, (3 * blk if blk < BLK_PP else 3 * BLK_PP + 14 + 3 * (blk - BLK_PG)) + m + 1)
                return
            for b0, n0, kqs in ((BLK_PG, N_PG, 4), (BLK_O, N_O, 4), (BLK_BA, N_BA, 2), (BLK_BB, N_BB, 2),
                                (BLK_GLU, N_GLU, 2), (BLK_IN, N_IN, 4)):
                if blk >= b0:
                    eng.wait_ge(chunk_used, n0 + kqs * (blk - b0 + 1))
                    return

        block = ctx.enter_context(nc.Block())

        @block.tensor
        def _(pe):
            ring = [4, 5, 6, 7]

            def side(name):
                b = ring[0]
                ring.append(ring.pop(0))
                uses[b] += 1
                misc[name] = (len(misc), b, uses[b])
                if uses[b] > 1:
                    pe.wait_ge(misc_read[b], uses[b] - 1)
                return bank[b]

            def stored(name):
                side_read(pe, name)

            def mm(out, w, x, start, stop):
                return nc.tensor.matmul(out, w, x, start=start, stop=stop)

            def mm3(out, wh, wl, xh, xl, start, stop):
                mm(out, wh, xh, start, False)
                mm(out, wh, xl, False, False)
                return mm(out, wl, xh, False, stop)

            pe.wait_ge(s_id, 16)
            for k in range(KD):
                if k % (KD // 2) == 0:
                    pe.wait_ge(s_x[k // (KD // 2)], 48)
                b = side(("x", k))
                for tt, (t0, tn) in enumerate(TOK):
                    last = nc.tensor.transpose(b[:, t0:t0 + tn], xtok[0:tn, tt, k * 128:(k + 1) * 128],
                                               ident[0:tn, 0:tn])
                last.then_inc(misc_ready, 1)

            def dense_chunk(n, blk, nk, kq, last_kq, xh, xl, xraw, slot, hslot):
                for m in range(4):
                    if kq == 0 and blk >= 1:
                        pe.wait_ge(acc_read[m], blk)
                    for k in range(nk):
                        cols = slice(k * 512 + m * 128, k * 512 + (m + 1) * 128)
                        first, stop = kq == 0 and k == 0, last_kq and k == nk - 1
                        kx = kq * nk + k
                        if xh is None:
                            ins = mm(bank[m][:, 0:NT], raw[:, slot, cols], xraw[:, kx], first, stop)
                        else:
                            ins = mm3(bank[m][:, 0:NT], hi[:, hslot, cols], lo[:, slot, cols],
                                      xh[:, kx], xl[:, kx], first, stop)
                    if last_kq and m < 3:
                        ins.then_inc(acc_ready, 1)
                ins.then_inc(chunk_used, 1)

            def s5_b(tau):
                k, j = divmod(tau, 4)
                rows = slice(32 * j, 32 * j + 32)
                if tau >= 2:
                    pe.wait_ge(bu_read, tau - 1)
                for ri in range(2):
                    last = mm(bank[4 + tau % 2][:, ri * T:(ri + 1) * T], BBT[rows, ri, k, :],
                              U[rows, k, 0:T], True, True)
                last.then_inc(bu_ready, 1)

            ybank = {}

            def s5_c(tau):
                k, j = divmod(tau, 4)
                if j == 0:
                    ybank[k] = side(("y", k))
                y = ybank[k][32 * j:32 * j + 32, :]
                pe.wait_ge(xt_ready, tau + 1)
                for ri in range(2):
                    last = mm(y[:, 0:T], CT[:, ri, k, 32 * j:32 * j + 32], xst[:, tau % 2, ri, :],
                              ri == 0, ri == 1)
                last.then_inc(xt_used, 1)
                for ri in range(2):
                    xv = xs[:, ri, :].rearrange("p (b t) -> p b t", b=NB)[:, :, tau]
                    last = mm(y[:, T:NT], CT[:, ri, k, 32 * j:32 * j + 32], xv, ri == 0, ri == 1)
                if j == 3:
                    last.then_inc(misc_ready, 1)

            def hgrn(hg, p):
                H0 = hg * HG
                if p == 0:
                    for c in range(2):
                        b = side(("v", hg, c))
                        for hh in range(HG):
                            last = nc.tensor.transpose(b[:, hh * 128:(hh + 1) * 128],
                                                       IV[:, H0 + hh, c * 128:(c + 1) * 128], ident[:, :])
                        last.then_inc(misc_ready, 1)
                    pe.wait_ge(h_k, hg + 1)
                    for name, src, h0 in (("sv", IV, H0), ("sk", kk, 0)):
                        b = side((name, hg))
                        for hh in range(HG):
                            last = nc.tensor.transpose(b[0:NB, hh * 128:(hh + 1) * 128],
                                                       src[:, h0 + hh, T:NT], ident[:, :])
                        last.then_inc(misc_ready, 1)
                if p <= 7:
                    if p:
                        pe.wait_ge(h_q, 7 * hg + p)
                    else:
                        pe.wait_ge(bu_read, NST)
                    for hp in range(2):
                        n = 16 * hg + 2 * p + hp
                        if n >= 2:
                            pe.wait_ge(h_scread, n - 1)
                        for q in range(4):
                            hh, c = 2 * hp + q // 2, q % 2
                            cs = slice(c * 128, (c + 1) * 128)
                            kl = kk[:, hh, cs] if p <= 1 else kt[:, p % 2, hh, cs]
                            ql = Q[:, H0 + hh, cs] if p == 0 else qt[:, p % 2, hh, cs]
                            last = mm(bank[4 + n % 2][:, q * 128:(q + 1) * 128], kl, ql, True, True)
                        last.then_inc(h_sc, 1)
                if p == 8:
                    pe.wait_ge(h_kts, hg + 1)
                    for c in range(2):
                        b = side(("k", hg, c))
                        for hh in range(HG):
                            last = nc.tensor.transpose(b[:, hh * 128:(hh + 1) * 128],
                                                       kt[:, 0, hh, c * 128:(c + 1) * 128], ident[:, :])
                        last.then_inc(misc_ready, 1)
                if p == 9:
                    for c in range(2):
                        stored(("v", hg, c))
                        stored(("k", hg, c))
                    for c in range(2):
                        b = side(("S", hg, c))
                        for hh in range(HG):
                            last = mm(b[:, hh * 128:(hh + 1) * 128], ktok[:, c, hh, :], vtok[:, c, hh, :],
                                      True, True)
                        last.then_inc(misc_ready, 1)
                if 10 <= p <= 13:
                    hh = p - 10
                    stored(("sk", hg))
                    pe.wait_ge(h_blk, H0 + hh + 1)
                    for half in range(2):
                        b = side(("ou", hg, hh, half))
                        mm(b[:, :], sktok[:, hh * 128:(hh + 1) * 128],
                           svblk[:, half * 4:(half + 1) * 4, :].rearrange("p b v -> p (b v)"),
                           True, True).then_inc(misc_ready, 1)
                if 11 <= p <= 14:
                    hh = p - 11
                    b = side(("o", hg, hh))
                    pe.wait_ge(h_scread, 16 * hg + 16)
                    mm(b[:, 0:128], vtok[:, 0, hh, :], Sc[:, hh, 0, :], True, True)
                    mm(b[:, 128:256], vtok[:, 1, hh, :], Sc[:, hh, 1, :], True, False)
                    stored(("S", hg, 0))
                    mm(b[:, 128:256], S0[:, hh, :], qt[:, 0, hh, 128:256], False, True)
                    pe.wait_ge(h_new, H0 + hh + 1)
                    for s in range(NB):
                        last = mm(b[:, T + s:T + s + 1], stS[:, hh % 2, s, :], Q[:, H0 + hh, T + s:T + s + 1],
                                  True, True)
                    last.then_inc(misc_ready, 1)
                if p == 14:
                    b = side(("ms", hg))
                    for hh in range(2, HG):
                        stored(("o", hg, hh))
                    for hh in range(HG):
                        last = mm(b[0:HG, 0:NT], colsel[:, hh, :], sq[:, hh, :], hh == 0, hh == HG - 1)
                    last.then_inc(misc_ready, 1)
                if p == 15:
                    pe.wait_ge(h_rstd, hg + 1)
                    for hh in range(HG):
                        b = side(("rb", hg, hh))
                        mm(b[:, 0:NT], rowsel[:, hh, :], rr[:, 1, :], True, True).then_inc(misc_ready, 1)

            for c in range(N_GLU):
                if c == 1:
                    pe.wait_ge(dt_wide, 1)
                    b = side("par")
                    for i in range(3):
                        last = nc.tensor.transpose(b[:, 32 * i:32 * i + 32], parnat[:, i, :],
                                                   ident[0:32, 0:32])
                    last.then_inc(misc_ready, 1)
                if c == 5 or c == 6:
                    pe.wait_ge(blk_ready, c - 4)
                    for ri in range(2):
                        for half in range(2):
                            b = side((c, ri, half))
                            for q in range(4):
                                k = half * 4 + q
                                last = nc.tensor.transpose(
                                    b[:, q * 128:(q + 1) * 128],
                                    yblk[:, ri].rearrange("p t c -> p (t c)")[:, k * 128:(k + 1) * 128],
                                    ident[:, :])
                            last.then_inc(misc_ready, 1)
                if c == 7:
                    b = side("s")
                    for q in range(4):
                        last = nc.tensor.transpose(b[:, q * 128:(q + 1) * 128], snat[:, q // 2, q % 2, :],
                                                   ident[:, :])
                    last.then_inc(misc_ready, 1)
                if c == 9:
                    pe.wait_ge(s_const, 16 * 5)
                    b = side("bus")
                    pe.wait_ge(ublk_ready, 1)
                    for ri in range(2):
                        stored((5, ri, 1))
                    stored((5, 0, 0))
                    for ri in range(2):
                        for k in range(KW):
                            last = mm(b[:, ri * 256 + k * 32:ri * 256 + (k + 1) * 32], BBT[:, ri, k, :],
                                      ublk[:, k].rearrange("p j b -> p (j b)"), True, True)
                    last.then_inc(misc_ready, 1)
                    for ri in range(2):
                        stored((6, ri, 0))
                        stored((6, ri, 1))
                if c == 10:
                    ring[:] = [6, 7]
                    for b in (4, 5):
                        pe.wait_ge(misc_read[b], uses[b])
                for tau in s5_at.get(c, []):
                    s5_b(tau)
                    if tau >= 2:
                        s5_c(tau - 2)
                if c == S5_END:
                    s5_c(NST - 2)
                    s5_c(NST - 1)
                    pe.wait_ge(yt_ready, KW)
                    b = side("fin")
                    for ri in range(2):
                        last = nc.tensor.transpose(b[0:NST, ri * 128:(ri + 1) * 128], fin[:, ri, :],
                                                   ident[:, :])
                    last.then_inc(misc_ready, 1)
                    b = side("xso")
                    for q in range(4):
                        last = nc.tensor.transpose(b[:, q * 128:(q + 1) * 128],
                                                   xs[:, q // 2, (q % 2) * 128:(q % 2 + 1) * 128], ident[:, :])
                    last.then_inc(misc_ready, 1)
                for hg, p in hg_at.get(c, []):
                    hgrn(hg, p)
                if c < 4:
                    pe.wait_ge(xt_done, 4 * c + 4)
                if is_split(c):
                    pe.wait_ge(lo_done, split_count(c) + 1)
                    dense_chunk(c, c // 4, 4, c % 4, c % 4 == 3, XH, XL, None, c % RD, split_count(c) % RH)
                else:
                    pe.wait_ge(landed[c % RD], 16 * (c // RD + 1))
                    dense_chunk(c, c // 4, 4, c % 4, c % 4 == 3, None, None, XT, c % RD, 0)

            def dense(n0, n1, blk0, kqs, xh, xl, after=None, parts=(0, 0)):
                for n in range(n0, n1):
                    kq, blk = (n - n0) % kqs, blk0 + (n - n0) // kqs
                    if n == N_PG + 2:
                        logits_by_token()
                    if n - n0 < parts[1]:
                        pe.wait_ge(a_lo, parts[0] + kq)
                    pe.wait_ge(lo_done, split_count(n) + 1)
                    dense_chunk(n, blk, 4, kq, kq == kqs - 1, xh, xl, None, n % RD, split_count(n) % RH)
                    if after is not None and kq == 1 and blk > blk0:
                        after(blk - blk0 - 1)
                if after is not None:
                    after((n1 - n0) // kqs - 1)

            ring[:] = [6, 7, 4, 5]
            dense(N_GLU, N_BB, BLK_GLU, 2, YGH, YGL, parts=(1, 2))
            pe.wait_ge(a_lo, 3)
            dense(N_BB, N_BA, BLK_BB, 2, YBH, YBL)
            dense(N_BA, N_O, BLK_BA, 2, YAH, YAL, parts=(4, 2))
            pe.wait_ge(p_ld, 48)
            b2 = [side("p0"), side("p1")]
            for k in range(2):
                for tt, (t0, tn) in enumerate(TOK):
                    last = nc.tensor.transpose(b2[k][:, t0:t0 + tn], ptok[0:tn, tt, k * 128:(k + 1) * 128],
                                               ident[0:tn, 0:tn])
                last.then_inc(misc_ready, 1)

            def to_tokens(name, src, ready):
                def go(j):
                    pe.wait_ge(ready, j + 1)
                    for tt, (t0, tn) in enumerate(TOK):
                        b = side((name, j, tt))
                        for q in range(4):
                            last = nc.tensor.transpose(b[0:tn, q * 128:(q + 1) * 128],
                                                       src[:, 4 * j + q, t0:t0 + tn], ident[:, :])
                        last.then_inc(misc_ready, 1)
                return go

            dense(N_O, N_PP, BLK_O, 4, MH, ML, to_tokens("h", XT, hpre), parts=(6, 4))
            stored("p0")
            stored("p1")
            for n in range(N_PP, N_PG):
                pe.wait_ge(lo_done, split_count(n) + 1)
                for half in range(2):
                    blk = BLK_PP + 2 * (n - N_PP) + half
                    for m in range(4):
                        pe.wait_ge(acc_read[m], blk)
                        for k in range(2):
                            cols = slice(k * 1024 + half * 512 + m * 128, k * 1024 + half * 512 + (m + 1) * 128)
                            last = mm3(bank[m][:, 0:NT], hi[:, split_count(n) % RH, cols], lo[:, n % RD, cols],
                                       pTh[:, k], pTl[:, k], k == 0, k == 1)
                        if (half, m) != (1, 3):
                            last.then_inc(acc_ready, 1)
                last.then_inc(chunk_used, 1)
            for k in range(KD):
                b = side(("ht", k))
                for tt, (t0, tn) in enumerate(TOK):
                    if k == 0:
                        pe.wait_ge(*((h_ready, tt + 1) if tt < 2 else (h_small, 1)))
                    last = nc.tensor.transpose(b[:, t0:t0 + tn], htok[0:tn, tt, k * 128:(k + 1) * 128],
                                               ident[0:tn, 0:tn])
                last.then_inc(misc_ready, 1)
            b = side("logT")
            pe.wait_ge(wr_lo, 1)
            for k in range(KD - 4, KD):
                stored(("ht", k))
            for k in range(KD):
                last = mm3(b[0:36, 0:NT], wrh[:, k], wrl[:, k], HTH[:, k], HTL[:, k], k == 0, k == KD - 1)
            last.then_inc(misc_ready, 1)

            def logits_by_token():
                b = side("log")
                stored("logT")
                for tt, (t0, tn) in enumerate(TOK):
                    last = nc.tensor.transpose(b[0:tn, tt * 36:(tt + 1) * 36], logT[:, t0:t0 + tn],
                                               ident[0:36, 0:36])
                last.then_inc(misc_ready, 1)

            def counts():
                b = side("rank")
                pe.wait_ge(oh_ready, 1)
                for tt, (t0, tn) in enumerate(TOK):
                    for s in range(tt):
                        mm(b[0:tn, tt * 4:(tt + 1) * 4], ones[:, 0:tn], oh[:, s], s == 0, False)
                    mm(b[0:tn, tt * 4:(tt + 1) * 4], lowtri[0:tn, 0:tn], oh[0:tn, tt], tt == 0, True)
                for tt, (t0, tn) in enumerate(TOK):
                    last = mm(b[:, 16:20], ones[0:tn, :], oh[0:tn, tt], tt == 0, tt == 2)
                last.then_inc(misc_ready, 1)

            def pg_after():
                go = to_tokens("ple", PPT, ple_ready)
                def run(j):
                    if j == 2:
                        counts()
                    go(j)
                return run

            dense(N_PG, N_END, BLK_PG, 4, HTH, HTL, pg_after())

            def gather(rnd, g):
                pe.wait_ge(sel_ready, rnd + 1)
                b = side(("st", rnd, g))
                for tt, (t0, tn) in enumerate(TOK):
                    last = nc.tensor.transpose(b[:, t0:t0 + tn], Sel[0:tn, tt, g, :], ident[0:tn, 0:tn])
                last.then_inc(misc_ready, 1)
                b = side(("cg", rnd, g))
                for tt, (t0, tn) in enumerate(TOK):
                    last = mm(b[:, 0:EPG], Sel[0:tn, tt, g, :], comb8[0:tn, tt, :], tt == 0, tt == 2)
                last.then_inc(misc_ready, 1)

            def gather_part(rnd, g, kq):
                b = side(("ga", rnd, g, kq))
                for q in range(4):
                    k = kq * 4 + q
                    for tt, (t0, tn) in enumerate(TOK):
                        hv = htok[0:tn, tt, :].rearrange("p (f k) -> p k f", k=KD)[:, k, :]
                        last = mm(b[:, q * 128:(q + 1) * 128], hv, Sel[0:tn, tt, g, :], tt == 0, tt == 2)
                last.then_inc(misc_ready, 1)

            def scatter(rnd, g):
                gg = rnd * GROUPS + g
                stored(("st", rnd, g))
                for tt, (t0, tn) in enumerate(TOK):
                    for nb in range(4):
                        b = side(("sc", rnd, g, tt, nb))
                        if tt == 0:
                            pe.wait_ge(outg_low, 4 * gg + nb + 1)
                        cs = slice(nb * 512, (nb + 1) * 512)
                        mm(b[0:tn, :], SelT[:, g % 2, t0:t0 + tn], outgh[:, cs], True, False)
                        last = mm(b[0:tn, :], SelT[:, g % 2, t0:t0 + tn], outgl[:, cs], False, True)
                        last.then_inc(misc_ready, 1)

            def gate_up(n, buf):
                for s in range(4):
                    pe.wait_ge(g_lo, 4 * n + s + 1)
                    for k in range(4):
                        kx = s * 4 + k
                        hs = mhi[s % 3][:, k * 512:(k + 1) * 512]
                        ls = mlo[s][:, k * 512:(k + 1) * 512]
                        mm(bank[4][:, :], hgh[:, buf, kx], hs, kx == 0, False)
                        mm(bank[4][:, :], hgl[:, buf, kx], hs, False, False)
                        last = mm(bank[4][:, :], hgh[:, buf, kx], ls, False, kx == 15)
                    last.then_inc(g_used, 1)

            def down(n, first, final, slots=(4, 5)):
                pe.wait_ge(hidT_lo, n + 1)
                for j in range(2):
                    pe.wait_ge(d_lo, 2 * n + j + 1)
                    for nb in range(4):
                        hs = mhi[(4 + j) % 3][:, nb * 512:(nb + 1) * 512]
                        ls = mlo[slots[j]][:, nb * 512:(nb + 1) * 512]
                        st = first and j == 0
                        mm(bank[nb][:, :], hidH[:, j], hs, st, False)
                        mm(bank[nb][:, :], hidL[:, j], hs, False, False)
                        last = mm(bank[nb][:, :], hidH[:, j], ls, False, final and j == 1)
                    last.then_inc(d_used, 1)

            def turn(n):
                pe.wait_ge(hid_done, n + 1)
                for j in range(2):
                    last = nc.tensor.transpose(bank[5][:, j * 128:(j + 1) * 128],
                                               hid[:, :].rearrange("p (f j) -> p j f", j=2)[:, j, :],
                                               ident[:, :])
                last.then_inc(hidT_ready, 1)

            def expert_round(rnd):
                if rnd == 0:
                    ring[:] = [6, 7]
                    for tt in range(3):
                        stored(("ple", 3, tt))
                    stored(("ple", 2, 2))
                gather(rnd, 0)
                for kq in range(4):
                    gather_part(rnd, 0, kq)
                for g in range(GROUPS):
                    gg = rnd * GROUPS + g
                    n0 = EPG * gg
                    stored(("ga", rnd, g, 2))
                    stored(("ga", rnd, g, 3))
                    if n0:
                        pe.wait_ge(hid_done, n0)
                    gate_up(n0, gg % 2)
                    if g:
                        down(n0 - 1, False, True)
                    turn(n0)
                    pe.wait_ge(hid_done, n0 + 1)
                    gate_up(n0 + 1, gg % 2)
                    if gg:
                        pe.wait_ge(outg_low, 4 * gg)
                    else:
                        for m in range(4):
                            pe.wait_ge(acc_read[m], BLK_PG + 4)
                    down(n0, True, False)
                    turn(n0 + 1)
                    if g:
                        scatter(rnd, g - 1)
                    def inner(n):
                        pe.wait_ge(hid_done, n)
                        gate_up(n, gg % 2)
                        down(n - 1, False, False)
                        turn(n)

                    n1 = n0 + 2
                    if g + 1 < GROUPS:
                        gather(rnd, g + 1)
                        for kq in range(4):
                            gather_part(rnd, g + 1, kq)
                            inner(n1 + kq)
                        n1 += 4
                    with pe.Fori(n1, n0 + EPG) as n:
                        inner(n)
                down(EPG * GROUPS * (rnd + 1) - 1, False, True, slots=(0, 1))
                scatter(rnd, GROUPS - 1)

            expert_round(0)
            pe.wait_ge(flag_ready, 1)
            more = pe.value_load(flag[0:1, 0:1], min_val=0, max_val=1)
            with pe.If(more > 0):
                for rnd in range(1, ROUNDS):
                    expert_round(rnd)

        @block.sync
        def _(sp):
            cc = t["consts"]

            def small_inputs():
                for i, n in enumerate(("s5_b_re", "s5_b_im")):
                    sp.dma_start(braw[:, i], t[n][0].rearrange("(t g) n c -> (g n) t c", g=2)).then_inc(s_bc, 16)
                for i, n in enumerate(("s5_c_re", "s5_c_im")):
                    sp.dma_start(craw[:, i], t[n][0].rearrange("(k g) c n -> (g c) k n", g=8)).then_inc(s_bc, 16)
                for i, n in enumerate(("state_s5_re", "state_s5_im")):
                    sp.dma_start(snat[:, i], t[n][0].rearrange("(r b) (t g) n -> (b t) r (g n)", r=2, g=2)).then_inc(
                        s_bc, 16)
                with nc.allow_non_contiguous_dma(reason="three short vectors, a feature on each partition"):
                    sp.dma_start(dskip[:, :], t["s5_d"][0].rearrange("(k p) -> p k", p=P)).then_inc(s_vec, 16)
                    sp.dma_start(lbraw[:, :], t["hg_lower_bounds"][0].rearrange("(k p) -> p k", p=P)).then_inc(
                        s_vec, 16)
                    sp.dma_start(gnorm[:, :], t["hg_norm_gain"][0].rearrange("(k p) -> p k", p=P)).then_inc(s_vec, 16)
                sp.dma_start(lowtri[:, :], cc[:, C_LT:C_LT + 128]).then_inc(s_const, 16)
                sp.dma_start(iota[:, :], cc[:, C_IO:C_IO + 128]).then_inc(s_const, 16)
                sp.dma_start(small[:, :], cc[:, C_MJ:C_MJ + 24]).then_inc(s_const, 16)
                sp.dma_start(rowsel[:, :, :], cc[0:HG, C_RS:C_RS + 512].rearrange("p (h n) -> p h n", h=HG)).then_inc(
                    s_const, 16)
                sp.dma_start(masks[:, :, :], cc[:, C_MASK:C_END].rearrange("p (h n) -> p h n", h=8)).then_inc(
                    s_const, 16)

            for i in range(2):
                cs = slice(i * D // 2, (i + 1) * D // 2)
                sp.dma_start(xtok[:, 0:2, cs], t["x_prompt"][0][:, cs].rearrange("(t p) d -> p t d", p=P)).then_inc(
                    s_x[i], 32)
                sp.dma_start(xtok[0:NB, 2, cs], t["x_sample"].rearrange("b a d -> (b a) d")[:, cs]).then_inc(
                    s_x[i], 16)
            sp.dma_start(ident[:, :], cc[:, C_ID:C_ID + 128]).then_inc(s_id, 16)
            sp.dma_start(dtn[:, :], t["s5_log_dt"][0].rearrange("(t g) -> t g", g=2)).then_inc(s_par, 16)
            for i, n in enumerate(("s5_lambda_re", "s5_lambda_im")):
                sp.dma_start(parnat[:, i, :], t[n][0].rearrange("(t g) n -> t (g n)", g=2)).then_inc(s_par, 16)
            sp.wait_ge(s_x[0], 48)
            for n in range(N_END):
                if n == 1:
                    small_inputs()
                    sp.wait_ge(s_x[1], 48)
                if n == 2:
                    sp.wait_ge(landed[0], 16)
                if n >= RD:
                    sp.wait_ge(chunk_used, n - RD + 1)
                c = chunk(n)
                sp.dma_start(raw[:, n % RD, :].rearrange("p (k n) -> p k n", k=c.shape[1]), c).then_inc(
                    landed[n % RD], 16)

            def gate_up_chunk(e, s):
                for i, w in enumerate((t["w_exp_gate"], t["w_exp_up"])):
                    src = w[0, bass.ds(e, 1)].rearrange("a (p k) f -> p (a k) f", p=P)[:, 4 * s:4 * s + 4, :]
                    dst = mraw[s].rearrange("p (k i f) -> p k i f", k=4, i=2)[:, :, i, :]
                    sp.dma_start(dst, src).then_inc(g_land[s], 16)

            def down_chunk(e, j, slot):
                src = t["w_exp_down"][0, bass.ds(e, 1)].rearrange("a (p j) d -> p (a j) d", p=P)[:, j, :]
                sp.dma_start(mraw[slot], src).then_inc(d_land[j], 16)

            def expert_round(rnd):
                n0 = EPG * GROUPS * rnd
                for s in range(4):
                    if rnd and s < 2:
                        sp.wait_ge(d_used, 2 * n0 - 1 + s)
                    elif rnd:
                        sp.wait_ge(ln2_ld, 32 * rnd)
                    else:
                        sp.wait_ge(chunk_used, max(n for n in range(N_END) if n % RD == s) + 1)
                    gate_up_chunk(0, s)
                for j in range(2):
                    if rnd:
                        sp.wait_ge(d_used, 2 * n0 - 3 + j)
                    else:
                        sp.wait_ge(chunk_used, N_END)
                    down_chunk(0, j, 4 + j)
                for s in range(4):
                    sp.wait_ge(g_used, 4 * n0 + s + 1)
                    gate_up_chunk(1, s)
                with sp.Fori(1, EPG * GROUPS - 1) as e:
                    for s in range(4):
                        sp.wait_ge(g_used, 4 * n0 + 4 * e + s + 1)
                        gate_up_chunk(e + 1, s)
                    for j in range(2):
                        sp.wait_ge(d_used, 2 * n0 + 2 * e + j - 1)
                        down_chunk(e, j, 4 + j)
                for j in range(2):
                    sp.wait_ge(g_used, 4 * n0 + 4 * (EPG * GROUPS - 1) + j + 1)
                    sp.wait_ge(d_land[j], 16 * (n0 + EPG * GROUPS - 1))
                    down_chunk(EPG * GROUPS - 1, j, j)
                sp.wait_ge(g_used, 4 * (n0 + EPG * GROUPS))
                for i, n in enumerate(("ln2_gain", "ln2_bias")):
                    sp.dma_start(ln2[:, i, :], t[n].to_broadcast([P, D])).then_inc(ln2_ld, 16)

            expert_round(0)
            sp.wait_ge(flag_ready, 1)
            more = sp.value_load(flag[0:1, 0:1], min_val=0, max_val=1)
            with sp.If(more > 0):
                for rnd in range(1, ROUNDS):
                    expert_round(rnd)
            y = outs
            for tt in NORM_ORDER:
                t0, tn = TOK[tt]
                sp.wait_ge(*((f_out, tt + 1) if tt < 2 else (f_small, 1)))
                dst = y[0][0, t0:t0 + tn, :] if tt < 2 else y[1].rearrange("b a d -> (b a) d")
                sp.dma_start(dst, atok[0:tn, tt, :]).then_inc(y_out, 16)
            sp.wait_ge(y_out, 48)

        @block.gpsimd
        def _(pool):
            def state_view(x, h):
                return x[0, :, h].rearrange("b k v -> k b v")

            for k in range(KD):
                side_read(pool, ("x", k))
                nc.gpsimd.tensor_tensor(XL[:, k, :], XT[:, k, :], XH[:, k, :].bitcast(F32),
                                        ALU.subtract).then_inc(xt_done, 1)
            pool.wait_ge(trig_done, 3)
            for n, w in enumerate(LEVELS[:-1]):
                cr = Pr[:, :, w - 1:w].to_broadcast([P, NST, w])
                ci = Pi[:, :, w - 1:w].to_broadcast([P, NST, w])
                for i, (dst, x, y, op) in enumerate(((Pr, cr, ci, ALU.subtract), (Pi, ci, cr, ALU.add))):
                    tmp = ptmp[:, :, 0:w]
                    new = dst[:, :, w:2 * w]
                    nc.gpsimd.tensor_tensor(tmp, Pr[:, :, 0:w], x, ALU.mult).then_inc(tab_part, 1)
                    nc.gpsimd.tensor_tensor(new, Pi[:, :, 0:w], y, ALU.mult).then_inc(tab_part, 1)
                    pool.wait_ge(tab_part, 4 * n + 2 * i + 2)
                    nc.gpsimd.tensor_tensor(new, tmp, new, op).then_inc(tab_done, 2)
                    pool.wait_ge(tab_done, 4 * n + 2 * i + 2)
            pool.wait_ge(outT, 1)
            for ri in range(2):
                pool.dma_start(outs[2 + ri].rearrange("a b (t g) n -> (a b t) (g n)", g=2),
                               finT[:, ri, :]).then_inc(st_out, 16)
            pool.wait_ge(outT, 2)
            for ri in range(2):
                pool.dma_start(outs[5 + ri][0].rearrange("(r b) (t g) n -> (b t) r (g n)", r=2, g=2),
                               xs[:, ri, :].rearrange("p (r n) -> p r n", r=2)).then_inc(st_out, 16)
            pool.wait_ge(xt_used, NST)
            for h in range(2):
                pool.dma_start(stS[:, h % 2], state_view(t["state_hgrn"], h)).then_inc(h_stq[h % 2], 16)

            for h in range(HEADS):
                hg, hh = divmod(h, HG)
                pool.wait_ge(h_new, h + 1)
                pool.dma_start(state_view(outs[7], h), stS[:, h % 2]).then_inc(h_sto[h % 2], 16)
                if h + 2 < HEADS:
                    pool.wait_ge(misc_ready, misc[("o", hg, hh)][0] + 1)
                    pool.wait_ge(h_sto[h % 2], 16 * (h // 2 + 1))
                    pool.dma_start(stS[:, h % 2], state_view(t["state_hgrn"], h + 2)).then_inc(h_stq[h % 2], 16)
                if hh == HG - 1:
                    pool.wait_ge(h_fin, hg + 1)
                    pool.dma_start(outs[4][0, 0, hg * HG:(hg + 1) * HG].rearrange("h k v -> k h v"),
                                   Sf[:, :, :]).then_inc(st_out, 16)
            pool.wait_ge(a_lo, 3)
            pool.dma_start(ptok[:, 0:2, :], t["p_prompt"][0, 0].rearrange("(t p) c -> p t c", p=P)).then_inc(
                p_ld, 16)
            pool.dma_start(ptok[0:NB, 2, :], t["p_sample"][0].rearrange("b a c -> (b a) c")).then_inc(p_ld, 32)
            pool.wait_ge(chunk_used, N_BA)
            pool.dma_start(wrr[:, :, 0:4], t["w_group_router"][0].rearrange("(k p) g -> p k g", p=P)).then_inc(
                r_ld, 16)
            pool.dma_start(wrr[:, :, 4:36], t["w_expert_router"][0].rearrange("(k p) g -> p k g", p=P)).then_inc(
                r_ld, 16)
            pool.dma_start(rbias[:, 0:4], t["b_group_router"].to_broadcast([P, 4])).then_inc(r_ld, 16)
            pool.dma_start(rbias[:, 4:36], t["b_expert_router"].to_broadcast([P, 32])).then_inc(r_ld, 16)
            pool.wait_ge(chunk_used, N_O)
            for i, n in enumerate(("ln1_gain", "ln1_bias")):
                pool.dma_start(ln1[:, i, :], t[n].to_broadcast([P, D])).then_inc(ln_ld, 16)
            pool.wait_ge(ln_ld, 32)
            pool.wait_ge(ln_norm, 1)
            small_h, small_y = htok[0:NB, 2, :], atok[0:NB, 2, :]
            nc.gpsimd.tensor_tensor(small_h, small_h, ln1[0:NB, 0, :], ALU.mult).then_inc(small_gain, 1)
            pool.wait_ge(small_gain, 1)
            nc.gpsimd.tensor_tensor(small_h, small_h, ln1[0:NB, 1, :], ALU.add).then_inc(h_small, 1)
            pool.wait_ge(st_out, 16 * 6)
            for i in range(2):
                pool.wait_ge(h_sto[i], 16 * 4)
            pool.wait_ge(final_vectors, 1)
            pool.wait_ge(f_norm, 1)
            nc.gpsimd.tensor_tensor(small_y, small_y, ln2[0:NB, 0, :], ALU.mult).then_inc(small_gain, 1)
            pool.wait_ge(small_gain, 2)
            nc.gpsimd.tensor_tensor(small_y, small_y, ln2[0:NB, 1, :], ALU.add).then_inc(f_small, 1)

        @block.scalar
        def _(act):
            def side(name):
                n, b, use = misc[name]
                act.wait_ge(misc_ready, n + 1)
                return bank[b], misc_read[b]

            for k in range(KD):
                b, read = side(("x", k))
                nc.scalar.activation(XH[:, k, :], b[:, 0:NT], ACT.Copy).then_inc(xh_done, 1)
            act.wait_ge(s_par, 48)
            nc.scalar.activation(dtn[:, :], dtn[:, :], ACT.Exp).then_inc(dt_exp, 1)

            def high(n):
                s = split_count(n)
                act.wait_ge(landed[n % RD], 16 * (n // RD + 1))
                if s >= RH:
                    prev = n - RH if n - RH >= N_GLU or n < N_GLU else 4 * SPLIT_IN - RH + (n - N_GLU)
                    act.wait_ge(chunk_used, prev + 1)
                nc.scalar.activation(hi[:, s % RH, :], raw[:, n % RD, :], ACT.Copy).then_inc(hi_done, 1)

            def hgrn(hg, p):
                if p == 0:
                    for n, name in enumerate((("v", hg, 0), ("v", hg, 1), ("sv", hg), ("sk", hg))):
                        b, read = side(name)
                        if n < 2:
                            nc.scalar.activation(vtok[:, n].rearrange("p h v -> p (h v)"), b[:, :],
                                                 ACT.Copy).then_inc(read, 1)
                        else:
                            nc.scalar.activation((svtok, sktok)[n - 2][:, :], b[0:NB, :], ACT.Copy).then_inc(
                                read, 1)
                if p == 8:
                    for c in range(2):
                        b, read = side(("k", hg, c))
                        nc.scalar.activation(ktok[:, c].rearrange("p h v -> p (h v)"), b[:, :],
                                             ACT.Copy).then_inc(read, 1)
                if p == 9:
                    b, read = side(("S", hg, 0))
                    nc.scalar.activation(S0[:, :, :].rearrange("p h v -> p (h v)"), b[:, :],
                                         ACT.Copy).then_inc(read, 1)
                if 11 <= p <= 14:
                    hh = p - 11
                    b, read = side(("o", hg, hh))
                    nc.scalar.activation(O4[:, hh, :], b[:, 0:NT], ACT.Copy)
                    nc.scalar.activation(sq[:, hh, :], b[:, 0:NT], ACT.Square).then_inc(read, 1)
                if p == 14:
                    act.wait_ge(h_ms, hg + 1)
                    nc.scalar.activation(rr[:, 1, :], rr[:, 0, :], ACT.Sqrt).then_inc(h_sqrt, 1)

            high(0)
            for c in range(N_GLU):
                blk = c // 4
                if c + 1 < 4 * SPLIT_IN:
                    high(c + 1)
                if c == 1:
                    act.wait_ge(ang_ready, 1)
                    nc.scalar.activation(par[:, 5], par[:, 4], ACT.Abs).then_inc(abs_done, 1)
                    nc.scalar.activation(par[:, 3], par[:, 3], ACT.Exp).then_inc(trig_done, 1)
                    act.wait_ge(lb_diff, 1)
                    nc.scalar.activation(lbraw[:, :], lbraw[:, :], ACT.Exp).then_inc(lb_exp, 1)
                if c == 2:
                    act.wait_ge(ang_ready, 2)
                    nc.scalar.activation(Pi[:, :, 0], par[:, 4], ACT.Sin).then_inc(trig_done, 1)
                    nc.scalar.activation(Pr[:, :, 0], par[:, 5], ACT.Sin).then_inc(trig_done, 1)
                if c == 5 or c == 6:
                    for ri in range(2):
                        for half in range(2):
                            b, read = side((c, ri, half))
                            dst = (BBT, CT)[c - 5][:, ri, half * 4:half * 4 + 4, :].rearrange("p k n -> p (k n)")
                            nc.scalar.activation(dst, b[:, :], ACT.Copy,
                                                 scale=-1.0 if c == 6 and ri else 1.0).then_inc(read, 1)
                if c == 7:
                    b, read = side("s")
                    nc.scalar.activation(sT[:, :, :].rearrange("p r n -> p (r n)"), b[:, :], ACT.Copy).then_inc(
                        read, 1)
                if c == S5_END + 1:
                    act.wait_ge(yt_ready, KW)
                    nc.scalar.activation(U[:, :, :], U[:, :, :], ACT.Gelu_apprx_tanh).then_inc(gelu_done, 1)
                for hg, p in hg_at.get(c, []):
                    hgrn(hg, p)
                if c % 4 == 3:
                    for m in range(4):
                        J = blk * 4 + m
                        summed(act, blk, m)
                        src = bank[m][:, 0:NT]
                        z, j = J // KW, J % KW
                        if z in (1, 4):
                            n = (z == 4) * KW + j
                            act.wait_ge(acc_read[(m + 2) % 4], blk + (m >= 2))
                            nc.scalar.activation(sigtmp[:, n % 2, :], src, ACT.Sigmoid).then_inc(sig_ready, 1)
                            continue
                        if z == 3 and m == 0:
                            act.wait_ge(blk_ready, 2)
                        if z == 5 and j == 0:
                            act.wait_ge(chunk_used, 4 * SPLIT_IN)
                        dst = (U, Q, FG, IV, G)[z][:, j] if z < 5 else (
                            GA[:, J - 5 * KW] if J < 5 * KW + KD else GB[:, J - 5 * KW - KD])
                        nc.scalar.activation(dst, src, ACT.Copy if z in (0, 3) else ACT.Sigmoid).then_inc(
                            acc_read[m], 1)

            def bulk(xh, xraw, ready):
                act.wait_ge(*ready)
                nc.scalar.activation(xh, xraw, ACT.Copy).then_inc(a_hi, 1)

            high(N_GLU)
            act.wait_ge(h_done, 1)
            act.wait_ge(st_out, 16 * 6)
            for i in range(2):
                bulk(YGH[:, 4 * i:4 * i + 4, :], U[:, 4 * i:4 * i + 4, :], (gelu_done, 1))
            bulk(YBH[:, :, :], G[:, :, :], (h_done, 1))
            for n in range(N_GLU, N_END):
                for ahead in ahead_of(n):
                    high(ahead)
                if N_GLU < n <= N_BB and n % 2 == 0:
                    js = slice(4 * ((n - N_GLU) // 2 - 1), 4 * ((n - N_GLU) // 2))
                    bulk(YAH[:, js, :], U[:, js, :], (a_raw, (n - N_GLU) // 2))
                if N_BA < n <= N_O and n % 2 == 0:
                    js = slice(4 * ((n - N_BA) // 2 - 1), 4 * ((n - N_BA) // 2))
                    bulk(MH[:, js, :], GA[:, js, :], (a_raw, 2 + (n - N_BA) // 2))
                if n < N_BB and n % 2 == 1:
                    blk, b0 = (n - N_GLU) // 2, BLK_GLU
                    for m in range(4):
                        summed(act, BLK_GLU + blk, m)
                        k = 2 * KW + 4 * blk + m
                        act.wait_ge(acc_read[(m + 2) % 4], b0 + blk + (m >= 2))
                        nc.scalar.activation(sigtmp[:, k % 2, :], bank[m][:, 0:NT], ACT.Sigmoid).then_inc(
                            sig_ready, 1)
                if n == N_O:
                    for k in range(2):
                        b, read = side(f"p{k}")
                        nc.scalar.activation(pTh[:, k, :], b[:, 0:NT], ACT.Copy).then_inc(pt_hi, 1)
                    act.wait_ge(r_ld, 64)
                    nc.scalar.activation(wrh[:, :, :], wrr[:, :, :], ACT.Copy).then_inc(wr_hi, 1)

                def to_htok(j):
                    for tt, (t0, tn) in enumerate(TOK):
                        b, read = side(("h", j, tt))
                        act.wait_ge(stat_done, 3 * j + tt + 1)
                        nc.scalar.activation(htok[0:tn, tt, j * 512:(j + 1) * 512], b[0:tn, :],
                                             ACT.Copy).then_inc(read, 1)
                if N_O + 4 < n < N_PP and (n - N_O) % 4 == 1:
                    to_htok((n - N_O) // 4 - 1)
                if n == N_PP - 1:
                    to_htok(3)
                    act.wait_ge(ln_var, 1)
                    nc.scalar.activation(rstd[:, :], rstd[:, :], ACT.Sqrt).then_inc(ln_sq, 1)
                    act.wait_ge(ln_nmr, 1)
                    for tt in NORM_ORDER:
                        tn = TOK[tt][1]
                        nc.scalar.activation(htok[0:tn, tt, :], htok[0:tn, tt, :], ACT.Identity,
                                             bias=nmr[0:tn, tt:tt + 1], scale=rstd[0:tn, tt:tt + 1]).then_inc(
                            ln_norm, 1)
                if N_PP <= n < N_PG:
                    for J in range(4 if n == N_PP else 8, 8 * (n - N_PP) + 8):
                        summed(act, BLK_PP + J // 4, J % 4)
                        nc.scalar.activation(PPT[:, J, :], bank[J % 4][:, 0:NT], ACT.Copy).then_inc(
                            acc_read[J % 4], 1)
                if n == N_PG - 1:
                    for k in range(KD):
                        b, read = side(("ht", k))
                        nc.scalar.activation(HTH[:, k, :], b[:, 0:NT], ACT.Copy).then_inc(ht_hi, 1)
                if n == N_PG:
                    b, read = side("logT")
                    nc.scalar.activation(logT[:, :], b[0:36, 0:NT], ACT.Copy).then_inc(read, 1)
                if n >= N_PG and (n - N_PG) % 4 == 3:
                    blk, b0 = (n - N_PG) // 4, BLK_PG
                    for m in range(4):
                        summed(act, BLK_PG + blk, m)
                        k = 3 * KW + 4 * blk + m
                        act.wait_ge(acc_read[(m + 2) % 4], b0 + blk + (m >= 2))
                        nc.scalar.activation(sigtmp[:, k % 2, :], bank[m][:, 0:NT], ACT.Sigmoid).then_inc(
                            sig_ready, 1)
                if n == N_PG + 6:
                    act.wait_ge(gm_neg, 1)
                    nc.scalar.activation(gex[:, :, :], gex[:, :, :], ACT.Exp).then_inc(r_exp, 1)
                if n == N_PG + 10:
                    act.wait_ge(e_diff, 1)
                    nc.scalar.activation(rsm[:, :, 1], rsm[:, :, 0], ACT.Exp).then_inc(r_exp2, 1)

            def gather(rnd, g):
                b, read = side(("st", rnd, g))
                nc.scalar.activation(SelT[:, g % 2, :], b[:, 0:NT], ACT.Copy).then_inc(read, 1)
                b, read = side(("cg", rnd, g))
                nc.scalar.activation(combg[:, g % 2, :], b[:, 0:EPG], ACT.Copy).then_inc(read, 1)

            def gather_part(rnd, g, kq):
                b, read = side(("ga", rnd, g, kq))
                nc.scalar.activation(hgh[:, g % 2, 4 * kq:4 * kq + 4, :].rearrange("p k s -> p (k s)"),
                                     b[:, :], ACT.Copy).then_inc(hg_hi, 1)

            def highs(n, which):
                for s in which:
                    if s < 4:
                        act.wait_ge(g_land[s], 32 * n + 32)
                        if s == 3:
                            act.wait_ge(g_used, 4 * n + 1)
                        elif s == 0 and not (isinstance(n, int) and n == 0):
                            act.wait_ge(g_used, 4 * n)
                        elif s in (1, 2) and not (isinstance(n, int) and n < 2):
                            act.wait_ge(d_used, 2 * n - 4 + s)
                        nc.scalar.activation(mhi[s % 3], mraw[s], ACT.Copy).then_inc(g_hi, 1)
                    else:
                        act.wait_ge(d_land[s - 4], 16 * n)
                        act.wait_ge(g_used, 4 * n + s - 2)
                        nc.scalar.activation(mhi[s % 3], mraw[s], ACT.Copy).then_inc(d_hi, 1)

            def silu(n):
                act.wait_ge(g_used, 4 * n)
                if not (isinstance(n, int) and n < 2):
                    act.wait_ge(hid_done, n - 1)
                nc.scalar.activation(gsil[:, :], bank[4][:, 0:FE], ACT.Silu).then_inc(silu_done, 1)

            def hidden(n):
                act.wait_ge(hidT_ready, n)
                nc.scalar.activation(hidH[:, :, :].rearrange("p j s -> p (j s)"), bank[5][:, 0:256],
                                     ACT.Copy).then_inc(hidT_hi, 1)

            def store(gg):
                for nb in range(4):
                    if nb == 0:
                        act.wait_ge(d_used, 2 * EPG * (gg + 1))
                        if gg:
                            last = misc[("sc", (gg - 1) // GROUPS, (gg - 1) % GROUPS, 2, 3)][0]
                            act.wait_ge(misc_ready, last + 1)
                    nc.scalar.activation(outgh[:, nb * 512:(nb + 1) * 512], bank[nb][:, :],
                                         ACT.Copy).then_inc(outg_done, 1)

            def turn(n):
                silu(n)
                highs(n, (0, 1, 2))
                hidden(n)
                highs(n, (3, 4, 5))

            act.wait_ge(chunk_used, N_END)
            def expert_round(rnd):
                if rnd:
                    act.wait_ge(d_used, 2 * EPG * GROUPS * rnd)
                n0 = EPG * GROUPS * rnd
                highs(n0, (0,))
                gather(rnd, 0)
                for kq in range(4):
                    gather_part(rnd, 0, kq)
                    if kq < 2:
                        highs(n0, (kq + 1,))
                for g in range(GROUPS):
                    gg = rnd * GROUPS + g
                    n0 = EPG * gg
                    if g == 0:
                        highs(n0, (3,))
                    else:
                        turn(n0)
                    silu(n0 + 1)
                    highs(n0 + 1, (0, 1))
                    if g:
                        store(gg - 1)
                    highs(n0 + 1, (2,))
                    hidden(n0 + 1)
                    highs(n0 + 1, (3, 4, 5))
                    silu(n0 + 2)
                    hidden(n0 + 2)
                    highs(n0 + 2, (0, 1))
                    if g + 1 < GROUPS:
                        gather(rnd, g + 1)
                        gather_part(rnd, g + 1, 0)
                    highs(n0 + 2, (2, 3, 4, 5))
                    n1 = n0 + 3
                    if g + 1 < GROUPS:
                        for kq in range(1, 4):
                            silu(n1)
                            highs(n1, (0, 1, 2))
                            hidden(n1)
                            gather_part(rnd, g + 1, kq)
                            highs(n1, (3, 4, 5))
                            n1 += 1
                    with act.Fori(n1, n0 + EPG) as n:
                        turn(n)
                n1 = EPG * GROUPS * (rnd + 1)
                silu(n1)
                for j in range(2):
                    act.wait_ge(d_land[j], 16 * n1)
                    act.wait_ge(d_used, 2 * n1 - 3 + j)
                    nc.scalar.activation(mhi[(4 + j) % 3], mraw[j], ACT.Copy).then_inc(d_hi, 1)
                    if j == 0:
                        hidden(n1)
                store(GROUPS * (rnd + 1) - 1)

            expert_round(0)
            act.wait_ge(flag_ready, 1)
            more = act.value_load(flag[0:1, 0:1], min_val=0, max_val=1)
            with act.If(more > 0):
                for rnd in range(1, ROUNDS):
                    expert_round(rnd)
            for i, tt in enumerate(NORM_ORDER):
                tn = TOK[tt][1]
                act.wait_ge(f_var, i + 1)
                nc.scalar.activation(rstd[0:tn, tt:tt + 1], rstd[0:tn, tt:tt + 1], ACT.Sqrt).then_inc(f_sq, 1)
                act.wait_ge(f_nmr, i + 1)
                nc.scalar.activation(atok[0:tn, tt, :], atok[0:tn, tt, :], ACT.Identity,
                                     bias=nmr[0:tn, tt:tt + 1], scale=rstd[0:tn, tt:tt + 1]).then_inc(f_norm, 1)

        @block.vector
        def _(dve):
            v = nc.vector
            count = [0]
            told = flagf[:, 1:2]

            def link(ins):
                count[0] += 1
                ins.then_inc(chain, 1)

            def settle():
                dve.wait_ge(chain, count[0])

            def side(name):
                n, b, use = misc[name]
                dve.wait_ge(misc_ready, n + 1)
                return bank[b], misc_read[b]

            def low(n):
                s = split_count(n)
                dve.wait_ge(hi_done, s + 1)
                v.tensor_tensor(lo[:, n % RD, :], raw[:, n % RD, :], hi[:, s % RH, :].bitcast(F32),
                                ALU.subtract).then_inc(lo_done, 1)

            v.memset(ones[:, :], 1.0).then_inc(s_ones, 1)
            for k in range(KD):
                b, read = side(("x", k))
                dve.wait_ge(xh_done, k + 1)
                v.tensor_copy(XT[:, k, :], b[:, 0:NT]).then_inc(read, 1)

            def lower_bounds():
                dve.wait_ge(lb_exp, 1)
                link(v.reciprocal(oml[:, :], lbraw[:, :]))
                settle()
                link(v.tensor_tensor(oml[:, :], oml[:, :], lbraw[:, :], ALU.mult))
                settle()
                link(v.tensor_tensor(lb[:, :], oml[:, :], oml[:, :], ALU.subtract))
                settle()
                link(v.tensor_scalar(oml[:, :], lb[:, :], -1.0, 1.0, ALU.mult, ALU.add))
                settle()

            def params_1():
                b, read = side("par")
                v.tensor_copy(par[:, 0:3, :].rearrange("p i t -> p (i t)"), b[:, 0:96]).then_inc(read, 1)
                side_read(dve, "par")
                lr, li, dt = par[:, 0], par[:, 1], par[:, 2]
                link(v.tensor_tensor(par[:, 3], lr, dt, ALU.mult))
                link(v.tensor_tensor(par[:, 4], li, dt, ALU.mult))
                settle()
                magic = 12582912.0
                link(v.tensor_scalar(par[:, 6], par[:, 4], 1.0 / (2 * np.pi), magic, ALU.mult, ALU.add))
                settle()
                link(v.tensor_scalar(par[:, 6], par[:, 6], magic, None, ALU.subtract))
                settle()
                for c in (6.28125, 0.0019350051879882812, 3.0199159819567e-07):
                    link(v.scalar_tensor_tensor(out=par[:, 4], in0=par[:, 6], scalar=-c, in1=par[:, 4],
                                                op0=ALU.mult, op1=ALU.add))
                    settle()
                v.tensor_scalar(par[:, 4], par[:, 4], float(np.float32(np.pi) * 0.9999999),
                                -float(np.float32(np.pi) * 0.9999999), ALU.min, ALU.max).then_inc(ang_ready, 1)

            def params_2():
                dve.wait_ge(abs_done, 1)
                v.tensor_scalar(par[:, 5], par[:, 5], -1.0, float(np.pi / 2), ALU.mult, ALU.add).then_inc(
                    ang_ready, 1)
                dve.wait_ge(trig_done, 3)
                link(v.tensor_copy(mag[:, :], par[:, 3]))
                link(v.tensor_tensor(ab[:, 0], par[:, 3], Pr[:, :, 0], ALU.mult))
                link(v.tensor_tensor(ab[:, 1], par[:, 3], Pi[:, :, 0], ALU.mult))
                lr, li = par[:, 0], par[:, 1]
                link(v.tensor_tensor(par[:, 7], lr, lr, ALU.mult))
                link(v.tensor_tensor(par[:, 8], li, li, ALU.mult))
                settle()
                link(v.tensor_tensor(par[:, 7], par[:, 7], par[:, 8], ALU.add))
                link(v.tensor_scalar(par[:, 9], ab[:, 0], -1.0, None, ALU.add))
                settle()
                link(v.reciprocal(par[:, 7], par[:, 7]))
                link(v.tensor_tensor(par[:, 10], par[:, 9], lr, ALU.mult))
                link(v.tensor_tensor(par[:, 11], ab[:, 1], li, ALU.mult))
                link(v.tensor_tensor(par[:, 12], ab[:, 1], lr, ALU.mult))
                link(v.tensor_tensor(par[:, 13], par[:, 9], li, ALU.mult))
                settle()
                link(v.tensor_tensor(par[:, 10], par[:, 10], par[:, 11], ALU.add))
                link(v.tensor_tensor(par[:, 12], par[:, 12], par[:, 13], ALU.subtract))
                settle()
                link(v.tensor_tensor(par[:, 10], par[:, 10], par[:, 7], ALU.mult))
                link(v.tensor_tensor(par[:, 12], par[:, 12], par[:, 7], ALU.mult))
                settle()

            def input_matrix():
                zr = par[:, 10].unsqueeze(2).to_broadcast([P, NST, 16])
                zi = par[:, 12].unsqueeze(2).to_broadcast([P, NST, 16])
                dve.wait_ge(s_bc, 16 * 6)
                for ri, (x, y, op) in enumerate(((0, 1, ALU.subtract), (1, 0, ALU.add))):
                    link(v.tensor_tensor(bbz[:, ri], braw[:, x], zr, ALU.mult))
                    link(v.tensor_tensor(btmp[:, :, :], braw[:, y], zi, ALU.mult))
                    settle()
                    link(v.tensor_tensor(bbz[:, ri], bbz[:, ri], btmp[:, :, :], op))
                    settle()
                    for g in range(2):
                        last = v.tensor_scalar(yblk[:, ri, :, 16 * g:16 * g + 16], bbz[:, ri],
                                               maskB[:, g:g + 1], None, ALU.mult)
                last.then_inc(blk_ready, 1)

            def output_matrix():
                for ri in range(2):
                    for half in range(2):
                        side_read(dve, (5, ri, half))
                for ri in range(2):
                    dst = yblk[:, ri].rearrange("p t c -> p (t c)").rearrange("p (k g n) -> p k g n", g=2, n=64)
                    for g in range(2):
                        last = v.tensor_scalar(dst[:, :, g, :], craw[:, ri], maskC[:, g:g + 1], None, ALU.mult)
                last.then_inc(blk_ready, 1)

            def last_powers(i):
                w = LEVELS[-1]
                if i == 0:
                    dve.wait_ge(tab_done, 4 * (len(LEVELS) - 1))
                cr = Pr[:, :, w - 1:w].to_broadcast([P, NST, w])
                ci = Pi[:, :, w - 1:w].to_broadcast([P, NST, w])
                dst, x, y, op = ((Pr, cr, ci, ALU.subtract), (Pi, ci, cr, ALU.add))[i]
                new = dst[:, :, w:2 * w]
                link(v.tensor_tensor(ptmp[:, :, :], Pr[:, :, 0:w], x, ALU.mult))
                link(v.tensor_tensor(new, Pi[:, :, 0:w], y, ALU.mult))
                settle()
                link(v.tensor_tensor(new, ptmp[:, :, :], new, op))
                settle()

            def spread_u():
                for m in range(4):
                    dve.wait_ge(acc_read[m], 2)
                for j in range(4):
                    last = v.tensor_scalar(ublk[:, :, j, :], U[:, :, T:NT], maskJ[:, j:j + 1], None, ALU.mult)
                last.then_inc(ublk_ready, 1)

            def sample_states():
                side_read(dve, "s")
                b, read = side("bus")

                def bt(x):
                    return x.rearrange("p (b t) -> p b t", b=NB)
                ar = ab[:, 0].unsqueeze(1).to_broadcast([P, NB, NST])
                ai = ab[:, 1].unsqueeze(1).to_broadcast([P, NB, NST])
                for ri, (x, y, op) in enumerate(((ar, ai, ALU.subtract), (ai, ar, ALU.add))):
                    link(v.tensor_tensor(bt(st1[:, :]), bt(sT[:, 0]), x, ALU.mult))
                    link(v.tensor_tensor(bt(st2[:, :]), bt(sT[:, 1]), y, ALU.mult))
                    settle()
                    link(v.tensor_tensor(st1[:, :], st1[:, :], st2[:, :], op))
                    settle()
                    link(v.tensor_tensor(xs[:, ri].rearrange("p (b t) -> p t b", b=NB),
                                         st1[:, :].rearrange("p (b t) -> p t b", b=NB),
                                         b[:, ri * 256:(ri + 1) * 256].rearrange("p (t b) -> p t b", b=NB),
                                         ALU.add))
                    settle()
                v.memset(told, 0.0).then_inc(read, 1)

            def s5(tau):
                dve.wait_ge(bu_ready, tau + 1)
                bu = bank[4 + tau % 2][:, :].rearrange("p (r h t) -> p r h t", r=2, h=2)
                x = xst[:, tau % 2]

                def tab(tb):
                    return tb[:, tau, :].unsqueeze(1).to_broadcast([P, 2, HALF])
                for ri in range(2):
                    pa, pb = tab(Pr), tab(Pi)
                    link(v.tensor_tensor(wA[:, ri].rearrange("p (h t) -> p h t", h=2), bu[:, ri], pa, ALU.mult))
                    last = v.tensor_tensor(wB[:, ri].rearrange("p (h t) -> p h t", h=2), bu[:, ri], pb, ALU.mult)
                    if ri == 0:
                        link(last)
                last.then_inc(bu_read, 1)
                dve.wait_ge(bu_read, tau + 1)
                link(v.tensor_tensor(wA[:, 0], wA[:, 0], wB[:, 1], ALU.add))
                link(v.tensor_tensor(wA[:, 1], wA[:, 1], wB[:, 0], ALU.subtract))
                settle()
                if tau >= 2:
                    dve.wait_ge(xt_used, tau - 1)
                m = mag[:, tau:tau + 1].to_broadcast([P, HALF])
                for h in range(2):
                    hs = slice(h * HALF, (h + 1) * HALF)
                    for ri in range(2):
                        init = 0.0 if h == 0 else x[:, ri, HALF - 1:HALF]
                        link(v.tensor_tensor_scan(ws[:, ri, hs], m, wA[:, ri, hs], init, ALU.mult, ALU.add))
                    settle()
                    link(v.tensor_tensor(x[:, :, hs], ws[:, :, hs], tab(Pr), ALU.mult))
                    link(v.tensor_tensor(wB[:, :, hs], ws[:, :, hs], tab(Pi), ALU.mult))
                    settle()
                    link(v.tensor_tensor(x[:, 0, hs], x[:, 0, hs], wB[:, 1, hs], ALU.subtract))
                    last = v.tensor_tensor(x[:, 1, hs], x[:, 1, hs], wB[:, 0, hs], ALU.add)
                    if h == 0:
                        link(last)
                        settle()
                last.then_inc(xt_ready, 1)
                dve.wait_ge(xt_ready, tau + 1)
                settle()
                link(v.tensor_copy(fin[:, :, tau], x[:, :, T - 1]))

            def s5_y(k):
                if k == 0:
                    dve.wait_ge(s_vec, 48)
                b, read = side(("y", k))
                v.scalar_tensor_tensor(out=U[:, k, :], in0=U[:, k, :], scalar=dskip[:, k:k + 1],
                                       in1=b[:, 0:NT], op0=ALU.mult, op1=ALU.add).then_inc(read, 1)
                if k == KW - 1:
                    side_read(dve, ("y", k - 1))
                    side_read(dve, ("y", k))
                    settle()
                    v.memset(told, 0.0).then_inc(yt_ready, KW)

            def level(hg, i):
                H0, w = hg * HG, LEVELS[i - 1]
                if i >= 2:
                    dve.wait_ge(h_sc, 16 * hg + 2 * (i - 2) + 2)
                qv = Q[:, H0:H0 + HG, 0:T]
                kv = kk[:, :, 0:T]
                blocks = "p h (b u w) -> p h b u w"

                def half(x, u):
                    return x.rearrange(blocks, u=2, w=w)[:, :, :, u, :]
                if i <= 2:
                    last = v.tensor_tensor(qt[:, i % 2], qv, PP[:, :, :], ALU.mult)
                    if i == 2:
                        link(last)
                        last = v.tensor_tensor(kt[:, 0], kv, SS[:, :, :], ALU.mult)
                    last.then_inc(h_q, 1)
                else:
                    for h in range(HG):
                        link(v.tensor_tensor(
                            qt[:, i % 2, h].rearrange("p (b u w) -> p b u w", u=2, w=w)[:, :, 1, :],
                            Q[:, H0 + h, 0:T].rearrange("p (b u w) -> p b u w", u=2, w=w)[:, :, 1, :],
                            PP[:, h].rearrange("p (b u w) -> p b u w", u=2, w=w)[:, :, 1, :], ALU.mult))
                    if i == 3:
                        last = v.tensor_tensor(kt[:, 1], kv, SS[:, :, :], ALU.mult)
                    else:
                        for h in range(HG):
                            last = v.tensor_tensor(
                                kt[:, i % 2, h].rearrange("p (b u w) -> p b u w", u=2, w=w)[:, :, 0, :],
                                kk[:, h, 0:T].rearrange("p (b u w) -> p b u w", u=2, w=w)[:, :, 0, :],
                                SS[:, h].rearrange("p (b u w) -> p b u w", u=2, w=w)[:, :, 0, :], ALU.mult)
                            if h < HG - 1:
                                link(last)
                    last.then_inc(h_q, 1)
                dve.wait_ge(h_q, 7 * hg + i)
                pv = PP[:, :, :].rearrange("p h (b u w) -> p (h b) u w", u=2, w=w)
                sv = SS[:, :, :].rearrange("p h (b u w) -> p (h b) u w", u=2, w=w)
                nb_ = HG * T // (2 * w)
                link(v.tensor_tensor(sv[:, :, 0, :], sv[:, :, 0, :],
                                     pv[:, :, 1, w - 1:w].to_broadcast([P, nb_, w]), ALU.mult))
                settle()
                link(v.tensor_tensor(pv[:, :, 1, :], pv[:, :, 1, :],
                                     pv[:, :, 0, w - 1:w].to_broadcast([P, nb_, w]), ALU.mult))
                settle()

            def scores(hg, i):
                for hp in range(2):
                    n = 16 * hg + 2 * i + hp
                    dve.wait_ge(h_sc, n + 1)
                    if n % 16 >= 2:
                        dve.wait_ge(h_scread, n - 1)
                    v.copy_predicated(
                        Sc[:, 2 * hp:2 * hp + 2].rearrange("p h c t -> p (h c) t"),
                        masks[:, i, :].bitcast(U32).unsqueeze(1).to_broadcast([P, 4, 128]),
                        bank[4 + n % 2][:, :].rearrange("p (q t) -> p q t", q=4)).then_inc(h_scread, 1)

            def spread(hg, hh):
                side_read(dve, ("sv", hg))
                v.tensor_tensor(svblk[:, :, :],
                                svtok[:, hh * 128:(hh + 1) * 128].unsqueeze(1).to_broadcast([NB, NB, 128]),
                                ident[0:NB, 0:NB].unsqueeze(2).to_broadcast([NB, NB, 128]),
                                ALU.mult).then_inc(h_blk, 1)

            def hgrn(hg, p):
                H0 = hg * HG
                if p == 0:
                    for m in range(4):
                        dve.wait_ge(acc_read[m], 6)
                    if hg == 0:
                        lower_bounds()
                        dve.wait_ge(xt_used, NST)
                    for h in range(H0, H0 + HG):
                        link(v.tensor_scalar(FG[:, h, :], FG[:, h, :], oml[:, h:h + 1], lb[:, h:h + 1],
                                             ALU.mult, ALU.add))
                    settle()
                    v.tensor_scalar(kk[:, :, :], FG[:, H0:H0 + HG, :], -1.0, 1.0, ALU.mult, ALU.add).then_inc(
                        h_k, 1)
                    link(v.memset(Sc[:, :, :, :], 0.0))
                    if hg:
                        dve.wait_ge(st_out, 16 * 5)
                    link(v.memset(SS[:, :, :], 1.0))
                    link(v.tensor_copy(PP[:, :, :], FG[:, H0:H0 + HG, 0:T]))
                    settle()
                    dve.wait_ge(h_k, hg + 1)
                    level(hg, 1)
                    scores(hg, 0)
                if 1 <= p <= 7:
                    if p < 7:
                        level(hg, p + 1)
                    else:
                        dve.wait_ge(h_sc, 16 * hg + 14)
                        v.tensor_tensor(kt[:, 0], kk[:, :, 0:T], SS[:, :, :], ALU.mult).then_inc(h_kts, 1)
                        link(v.tensor_tensor(qt[:, 0], Q[:, H0:H0 + HG, 0:T], PP[:, :, :], ALU.mult))
                        settle()
                    scores(hg, p)
                if p == 8:
                    spread(hg, 0)
                if p == 9:
                    side_read(dve, ("S", hg, 0))
                    b, read = side(("S", hg, 1))
                    side_read(dve, ("k", hg, 1))
                    for h in range(HG):
                        last = v.scalar_tensor_tensor(out=Sf[:, h, :], in0=S0[:, h, :],
                                                      scalar=PP[:, h, T - 1:T], in1=b[:, h * 128:(h + 1) * 128],
                                                      op0=ALU.mult, op1=ALU.add)
                        if h < HG - 1:
                            link(last)
                    last.then_inc(read, 1)
                    side_read(dve, ("S", hg, 1))
                    v.memset(told, 0.0).then_inc(h_fin, 1)
                if 10 <= p <= 13:
                    hh = p - 10
                    h = H0 + hh
                    dve.wait_ge(h_stq[h % 2], 16 * (h // 2 + 1))
                    for half in range(2):
                        b, read = side(("ou", hg, hh, half))
                        for s in range(4):
                            bs = half * 4 + s
                            last = v.scalar_tensor_tensor(out=stS[:, h % 2, bs, :], in0=stS[:, h % 2, bs, :],
                                                          scalar=FG[:, h, T + bs:T + bs + 1],
                                                          in1=b[:, s * 128:(s + 1) * 128],
                                                          op0=ALU.mult, op1=ALU.add)
                            if s < 3:
                                link(last)
                        last.then_inc(read, 1)
                    side_read(dve, ("ou", hg, hh, 0))
                    side_read(dve, ("ou", hg, hh, 1))
                    v.memset(told, 0.0).then_inc(h_new, 1)
                    if hh + 1 < HG:
                        spread(hg, hh + 1)
                if p == 14:
                    b, read = side(("ms", hg))
                    v.tensor_scalar(rr[:, 0, :], b[0:HG, 0:NT], RMS_EPS, None, ALU.add).then_inc(read, 1)
                    side_read(dve, ("ms", hg))
                    v.memset(told, 0.0).then_inc(h_ms, 1)
                    dve.wait_ge(h_sqrt, hg + 1)
                    v.reciprocal(rr[:, 1, :], rr[:, 1, :]).then_inc(h_rstd, 1)
                if p == 15:
                    for hh in range(HG):
                        b, read = side(("rb", hg, hh))
                        h = H0 + hh
                        v.scalar_tensor_tensor(out=O4[:, hh, :], in0=O4[:, hh, :], scalar=gnorm[:, 0:1],
                                               in1=b[:, 0:NT], op0=ALU.mult, op1=ALU.mult).then_inc(read, 1)
                        side_read(dve, ("rb", hg, hh))
                        link(v.tensor_tensor(G[:, h, :], G[:, h, :], O4[:, hh, :], ALU.mult))
                    settle()
                    if hg == 1:
                        v.memset(told, 0.0).then_inc(h_done, 1)

            low(0)
            for c in range(N_GLU):
                if c + 1 < 4 * SPLIT_IN:
                    low(c + 1)
                if c == 0:
                    dve.wait_ge(dt_exp, 1)
                    v.tensor_copy(parnat[:, 2, :].rearrange("t (g n) -> t g n", g=2),
                                  dtn[:, :].unsqueeze(2).to_broadcast([NST, 2, 64])).then_inc(dt_wide, 1)
                if c == 1:
                    params_1()
                    dve.wait_ge(s_vec, 48)
                    v.tensor_tensor(lbraw[:, :], lbraw[:, :], lbraw[:, :], ALU.subtract).then_inc(lb_diff, 1)
                if c == 2:
                    params_2()
                if c == 3:
                    dve.wait_ge(s_const, 16 * 5)
                    input_matrix()
                if c == 5:
                    output_matrix()
                if c == 8:
                    spread_u()
                if c == 9:
                    sample_states()
                if c in (7, 10):
                    last_powers((c - 7) // 3)
                for tau in s5_at.get(c, []):
                    s5(tau)
                    if tau % 4 == 1 and tau > 4:
                        s5_y(tau // 4 - 1)
                if c == S5_END:
                    s5_y(KW - 1)
                    b, read = side("fin")
                    v.tensor_copy(finT[:, :, :].rearrange("p r n -> p (r n)"), b[0:NST, 0:256]).then_inc(read, 1)
                    side_read(dve, "fin")
                    v.memset(told, 0.0).then_inc(outT, 1)
                    b, read = side("xso")
                    v.tensor_copy(xs[:, :, :].rearrange("p r n -> p (r n)"), b[:, :]).then_inc(read, 1)
                    side_read(dve, "xso")
                    v.memset(told, 0.0).then_inc(outT, 1)
                for hg, p in hg_at.get(c, []):
                    hgrn(hg, p)
                blk = c // 4
                if c % 4 == 3 and blk in (2, 3, 8, 9):
                    for m in range(4):
                        J = 4 * blk + m
                        n = (blk >= 8) * KW + J % KW
                        dve.wait_ge(sig_ready, n + 1)
                        v.tensor_tensor((Q, G)[blk >= 8][:, J % KW, :], bank[m][:, 0:NT], sigtmp[:, n % 2, :],
                                        ALU.mult).then_inc(acc_read[m], 1)

            low(N_GLU)
            for i in range(2):
                js = slice(4 * i, 4 * i + 4)
                dve.wait_ge(a_hi, 1 + i)
                v.tensor_tensor(YGL[:, js, :], U[:, js, :], YGH[:, js, :].bitcast(F32),
                                ALU.subtract).then_inc(a_lo, 1)
            dve.wait_ge(a_hi, 3)
            v.tensor_tensor(YBL[:, :, :], G[:, :, :], YBH[:, :, :].bitcast(F32), ALU.subtract).then_inc(a_lo, 1)

            def router(piece):
                if piece == 0:
                    b, read = side("log")
                    dve.wait_ge(r_ld, 64)
                    link(v.memset(lg8[:, :, :], -3.0e38))
                    link(v.memset(logit[:, :, :], 0.0))
                    settle()
                    for tt, (t0, tn) in enumerate(TOK):
                        last = v.tensor_tensor(logit[0:tn, tt, :], b[0:tn, tt * 36:(tt + 1) * 36],
                                               rbias[0:tn, :], ALU.add)
                        if tt < 2:
                            link(last)
                    last.then_inc(read, 1)
                    side_read(dve, "log")
                    settle()
                    link(v.tensor_copy(lg8[:, :, 0:4], logit[:, :, 0:4]))
                    settle()
                    for tt in range(3):
                        link(v.max(gmx[:, tt, :], lg8[:, tt, :]))
                    settle()
                    for tt in range(3):
                        link(v.max_index(gix[:, tt, :], gmx[:, tt, :], lg8[:, tt, :]))
                    v.tensor_tensor(gex[:, :, :], logit[:, :, 0:4], gmx[:, :, 0:1].to_broadcast([P, 3, 4]),
                                    ALU.subtract).then_inc(gm_neg, 1)
                    settle()
                    link(v.tensor_copy(gif[:, :, :], gix[:, :, :]))
                    settle()
                    last = v.tensor_tensor(oh[:, :, :], iota[:, 0:4].unsqueeze(1).to_broadcast([P, 3, 4]),
                                           gif[:, :, 0:1].to_broadcast([P, 3, 4]), ALU.is_equal)
                    last.then_inc(oh_ready, 1)
                    dve.wait_ge(oh_ready, 1)
                if piece == 1:
                    for g in range(GROUPS):
                        le = logit[:, :, 4 + 8 * g:12 + 8 * g]
                        w = oh[:, :, g:g + 1].to_broadcast([P, 3, 8])
                        dst = ing if g == 0 else ctmp
                        link(v.tensor_tensor(dst[:, :, :], le, w, ALU.mult))
                        settle()
                        if g:
                            link(v.tensor_tensor(ing[:, :, :], ing[:, :, :], ctmp[:, :, :], ALU.add))
                            settle()
                    for tt in range(3):
                        link(v.max(emx[:, tt, :], ing[:, tt, :]))
                    settle()
                    for tt in range(3):
                        link(v.max_index(eix[:, tt, :], emx[:, tt, :], ing[:, tt, :]))
                    v.tensor_tensor(rsm[:, :, 0], emx[:, :, 1], emx[:, :, 0], ALU.subtract).then_inc(e_diff, 1)
                    settle()
                    link(v.tensor_copy(eif[:, :, :], eix[:, :, :]))
                    settle()
                if piece == 2:
                    dve.wait_ge(r_exp, 1)
                    dve.wait_ge(r_exp2, 1)
                    link(v.tensor_reduce(rsm[:, :, 2:3], gex[:, :, :], AX_X, ALU.add))
                    link(v.tensor_scalar(rsm[:, :, 3], rsm[:, :, 1], 1.0, None, ALU.add))
                    settle()
                    link(v.tensor_tensor(rsm[:, :, 3], rsm[:, :, 3], rsm[:, :, 2], ALU.mult))
                    settle()
                    link(v.reciprocal(rsm[:, :, 3:4], rsm[:, :, 3:4]))
                    settle()
                    link(v.tensor_tensor(rsm[:, :, 4], rsm[:, :, 3], rsm[:, :, 1], ALU.mult))
                    settle()
                    for i in range(2):
                        dst = comb8 if i == 0 else ctmp
                        link(v.tensor_tensor(dst[:, :, :], iota[:, 0:8].unsqueeze(1).to_broadcast([P, 3, 8]),
                                             eif[:, :, i:i + 1].to_broadcast([P, 3, 8]), ALU.is_equal))
                        settle()
                        link(v.tensor_tensor(dst[:, :, :], dst[:, :, :],
                                             rsm[:, :, 3 + i:4 + i].to_broadcast([P, 3, 8]), ALU.mult))
                        settle()
                    link(v.tensor_tensor(comb8[:, :, :], comb8[:, :, :], ctmp[:, :, :], ALU.add))
                    settle()
                if piece == 3:
                    b, read = side("rank")
                    for tt, (t0, tn) in enumerate(TOK):
                        link(v.scalar_tensor_tensor(out=rank[0:tn, tt, :], in0=b[0:tn, 4 * tt:4 * tt + 4],
                                                    scalar=1.0, in1=oh[0:tn, tt, :], op0=ALU.add,
                                                    op1=ALU.mult))
                    link(v.tensor_reduce(flagf[:, 0:1], b[:, 16:20], AX_X, ALU.max))
                    settle()
                    v.memset(told, 0.0).then_inc(read, 1)
                    for tt, (t0, tn) in enumerate(TOK):
                        link(v.tensor_scalar(rank[0:tn, tt, :], rank[0:tn, tt, :], -1.0, None, ALU.add))
                    v.tensor_scalar(flag[:, :], flagf[:, 0:1], float(SLOTS), None, ALU.is_gt).then_inc(
                        flag_ready, 1)
                    settle()
                    select(0)

            def select(rnd):
                for g in range(GROUPS):
                    for tt, (t0, tn) in enumerate(TOK):
                        last = v.tensor_scalar(Sel[0:tn, tt, g, :], iota[0:tn, :], rank[0:tn, tt, g:g + 1],
                                               None, ALU.is_equal)
                        if (g, tt) != (GROUPS - 1, 2):
                            link(last)
                last.then_inc(sel_ready, 1)

            def statistics(j):
                for tt, (t0, tn) in enumerate(TOK):
                    b, read = side(("h", j, tt))
                    v.bn_stats(stats[0:tn, tt, j, :], b[0:tn, :]).then_inc(stat_done, 1)

            def deviations(tt, n):
                link(v.bn_aggr(mv[0:n, tt, :], stats[0:n, tt, :, :].rearrange("p a b -> p (a b)")))
                settle()
                link(v.tensor_scalar(rstd[0:n, tt:tt + 1], mv[0:n, tt, 1:2], LN_EPS, None, ALU.add))

            for n in range(N_GLU, N_END):
                for ahead in ahead_of(n):
                    if ahead != N_PP + 1:
                        low(ahead)
                if N_GLU < n <= N_BB and n % 2 == 0:
                    i = (n - N_GLU) // 2
                    js = slice(4 * i - 4, 4 * i)
                    dve.wait_ge(a_hi, 3 + i)
                    v.tensor_tensor(YAL[:, js, :], U[:, js, :], YAH[:, js, :].bitcast(F32),
                                    ALU.subtract).then_inc(a_lo, 1)
                if N_BA < n <= N_O and n % 2 == 0:
                    i = (n - N_BA) // 2
                    js = slice(4 * i - 4, 4 * i)
                    dve.wait_ge(a_hi, 5 + i)
                    v.tensor_tensor(ML[:, js, :], GA[:, js, :], MH[:, js, :].bitcast(F32),
                                    ALU.subtract).then_inc(a_lo, 1)
                if n < N_BB and n % 2 == 1:
                    blk = (n - N_GLU) // 2
                    for m in range(4):
                        J = 4 * blk + m
                        k = 2 * KW + J
                        dve.wait_ge(sig_ready, k + 1)
                        last = v.tensor_tensor(U[:, J, :], U[:, J, :], sigtmp[:, k % 2, :], ALU.mult)
                        last.then_inc(acc_read[m], 1)
                    dve.wait_ge(acc_read[3], BLK_GLU + blk + 1)
                    v.memset(told, 0.0).then_inc(a_raw, 1)
                if N_BB <= n < N_BA and n % 2 == 1:
                    for m in range(4):
                        J = 4 * ((n - N_BB) // 2) + m
                        summed(dve, BLK_BB + J // 4, m)
                        v.tensor_tensor(GB[:, J, :], bank[m][:, 0:NT], GB[:, J, :], ALU.mult).then_inc(
                            acc_read[m], 1)
                if N_BA <= n < N_O and n % 2 == 1:
                    blk = (n - N_BA) // 2
                    for m in range(4):
                        J = 4 * blk + m
                        summed(dve, BLK_BA + blk, m)
                        v.tensor_tensor(GA[:, J, :], bank[m][:, 0:NT], GA[:, J, :], ALU.mult).then_inc(
                            acc_read[m], 1)
                    js = slice(4 * blk, 4 * blk + 4)
                    for m in range(4):
                        dve.wait_ge(acc_read[m], BLK_BA + blk + 1)
                    v.tensor_tensor(GA[:, js, :], GA[:, js, :], GB[:, js, :], ALU.add).then_inc(a_raw, 1)
                if n == N_O:
                    for k in range(2):
                        b, read = side(f"p{k}")
                        dve.wait_ge(pt_hi, k + 1)
                        v.tensor_tensor(pTl[:, k, :], b[:, 0:NT], pTh[:, k, :].bitcast(F32),
                                        ALU.subtract).then_inc(read, 1)
                    dve.wait_ge(wr_hi, 1)
                    v.tensor_tensor(wrl[:, :, :], wrr[:, :, :], wrh[:, :, :].bitcast(F32),
                                    ALU.subtract).then_inc(wr_lo, 1)
                if N_O + 4 < n < N_PP and (n - N_O) % 4 == 1:
                    statistics((n - N_O) // 4 - 1)
                if N_O <= n < N_PP and (n - N_O) % 4 == 3:
                    for m in range(4):
                        J = n - N_O - 3 + m
                        summed(dve, BLK_O + J // 4, m)
                        v.scalar_tensor_tensor(out=XT[:, J, :], in0=XT[:, J, :], scalar=ALPHA,
                                               in1=bank[m][:, 0:NT], op0=ALU.mult, op1=ALU.add).then_inc(
                            acc_read[m], 1)
                    for m in range(4):
                        dve.wait_ge(acc_read[m], BLK_O + (n - N_O) // 4 + 1)
                    v.memset(told, 0.0).then_inc(hpre, 1)
                if n == N_PP - 1:
                    low(N_PP + 1)
                    statistics(3)
                    dve.wait_ge(stat_done, 12)
                    link(v.memset(mv[:, :, :], 0.0))
                    link(v.memset(rstd[:, :], 1.0))
                    settle()
                    for tt, (t0, tn) in enumerate(TOK):
                        deviations(tt, tn)
                    settle()
                    v.memset(told, 0.0).then_inc(ln_var, 1)
                    dve.wait_ge(ln_sq, 1)
                    link(v.reciprocal(rstd[:, :], rstd[:, :]))
                    settle()
                    v.scalar_tensor_tensor(out=nmr[:, :], in0=mv[:, :, 0], scalar=-1.0, in1=rstd[:, :],
                                           op0=ALU.mult, op1=ALU.mult).then_inc(ln_nmr, 1)
                    for m in range(4):
                        summed(dve, BLK_PP, m)
                        v.tensor_copy(PPT[:, m, :], bank[m][:, 0:NT]).then_inc(acc_read[m], 1)
                    dve.wait_ge(ln_ld, 32)
                    for i, tt in enumerate(NORM_ORDER):
                        if tt < 2:
                            dve.wait_ge(ln_norm, i + 1)
                            v.tensor_tensor(htok[:, tt, :], htok[:, tt, :], ln1[:, 0, :], ALU.mult).then_inc(
                                gained, 1)
                            dve.wait_ge(gained, tt + 1)
                            v.tensor_tensor(htok[:, tt, :], htok[:, tt, :], ln1[:, 1, :], ALU.add).then_inc(
                                h_ready, 1)
                if n == N_PG - 1:
                    for k in range(KD):
                        b, read = side(("ht", k))
                        dve.wait_ge(ht_hi, k + 1)
                        v.tensor_tensor(HTL[:, k, :], b[:, 0:NT], HTH[:, k, :].bitcast(F32),
                                        ALU.subtract).then_inc(read, 1)
                if n >= N_PG:
                    i = n - N_PG
                    if i % 4 == 3:
                        for m in range(4):
                            J = i - 3 + m
                            k = 3 * KW + J
                            dve.wait_ge(sig_ready, k + 1)
                            v.tensor_tensor(PPT[:, J, :], PPT[:, J, :], sigtmp[:, k % 2, :], ALU.mult).then_inc(
                                acc_read[m], 1)
                        for m in range(4):
                            dve.wait_ge(acc_read[m], BLK_PG + i // 4 + 1)
                        v.memset(told, 0.0).then_inc(ple_ready, 1)
                    if i in (4, 6, 12, 13):
                        router((4, 6, 12, 13).index(i))
                    if (i % 4 == 1 and i > 4) or i == 15:
                        j = 3 if i == 15 else i // 4 - 1
                        for tt, (t0, tn) in enumerate(TOK):
                            b, read = side(("ple", j, tt))
                            cs = slice(j * 512, (j + 1) * 512)
                            v.scalar_tensor_tensor(out=atok[0:tn, tt, cs], in0=htok[0:tn, tt, cs],
                                                   scalar=ALPHA, in1=b[0:tn, :], op0=ALU.mult,
                                                   op1=ALU.add).then_inc(read, 1)

            def gather_part(rnd, g, kq):
                b, read = side(("ga", rnd, g, kq))
                dve.wait_ge(hg_hi, 4 * (rnd * GROUPS + g) + kq + 1)
                ks = slice(4 * kq, 4 * kq + 4)
                v.tensor_tensor(hgl[:, g % 2, ks, :].rearrange("p k s -> p (k s)"), b[:, :],
                                hgh[:, g % 2, ks, :].rearrange("p k s -> p (k s)").bitcast(F32),
                                ALU.subtract).then_inc(read, 1)

            def scatter(rnd, g):
                for tt, (t0, tn) in enumerate(TOK):
                    for nb in range(4):
                        b, read = side(("sc", rnd, g, tt, nb))
                        cs = slice(nb * 512, (nb + 1) * 512)
                        v.tensor_tensor(atok[0:tn, tt, cs], atok[0:tn, tt, cs], b[0:tn, :],
                                        ALU.add).then_inc(read, 1)
                side_read(dve, ("sc", rnd, g, 2, 2))
                side_read(dve, ("sc", rnd, g, 2, 3))

            def store(gg):
                for nb in range(4):
                    dve.wait_ge(outg_done, 4 * gg + nb + 1)
                    cs = slice(nb * 512, (nb + 1) * 512)
                    v.tensor_tensor(outgl[:, cs], bank[nb][:, :], outgh[:, cs].bitcast(F32),
                                    ALU.subtract).then_inc(outg_low, 1)

            def lows(n, which):
                for s in which:
                    if s < 4:
                        dve.wait_ge(g_hi, 4 * n + s + 1)
                        v.tensor_tensor(mlo[s], mraw[s], mhi[s % 3].bitcast(F32), ALU.subtract).then_inc(g_lo, 1)
                    else:
                        dve.wait_ge(d_hi, 2 * n + s - 5)
                        v.tensor_tensor(mlo[s], mraw[s], mhi[s % 3].bitcast(F32), ALU.subtract).then_inc(d_lo, 1)

            def hidden(n, g, e):
                dve.wait_ge(silu_done, n)
                v.scalar_tensor_tensor(out=hid[:, :], in0=bank[4][:, FE:2 * FE], scalar=combg[:, g % 2, e],
                                       in1=gsil[:, :], op0=ALU.mult, op1=ALU.mult).then_inc(hid_done, 1)

            def hidden_low(n):
                dve.wait_ge(hidT_hi, n)
                v.tensor_tensor(hidL[:, :, :].rearrange("p j s -> p (j s)"), bank[5][:, 0:256],
                                hidH[:, :, :].rearrange("p j s -> p (j s)").bitcast(F32),
                                ALU.subtract).then_inc(hidT_lo, 1)

            def turn(n, g, e):
                hidden(n, g, e)
                lows(n, (0, 1, 2))
                hidden_low(n)
                lows(n, (3, 4, 5))

            def expert_round(rnd):
                if rnd:
                    for tt, (t0, tn) in enumerate(TOK):
                        link(v.tensor_scalar(rank[0:tn, tt, :], rank[0:tn, tt, :], -float(SLOTS), None, ALU.add))
                    settle()
                    dve.wait_ge(misc_ready, misc[("ga", rnd - 1, GROUPS - 1, 3)][0] + 1)
                    select(rnd)
                n0 = EPG * GROUPS * rnd
                lows(n0, (0,))
                for kq in range(4):
                    gather_part(rnd, 0, kq)
                    if kq < 2:
                        lows(n0, (kq + 1,))
                for g in range(GROUPS):
                    gg = rnd * GROUPS + g
                    n0 = EPG * gg
                    if g == 0:
                        lows(n0, (3,))
                    else:
                        turn(n0, g - 1, slice(EPG - 1, EPG))
                    side_read(dve, ("cg", rnd, g))
                    hidden(n0 + 1, g, slice(0, 1))
                    lows(n0 + 1, (0, 1))
                    if g:
                        store(gg - 1)
                    lows(n0 + 1, (2,))
                    hidden_low(n0 + 1)
                    lows(n0 + 1, (3, 4, 5))
                    hidden(n0 + 2, g, slice(1, 2))
                    hidden_low(n0 + 2)
                    if g:
                        scatter(rnd, g - 1)
                    lows(n0 + 2, (0,))
                    if g + 1 < GROUPS:
                        gather_part(rnd, g + 1, 0)
                    lows(n0 + 2, (1, 2, 3, 4, 5))
                    n1 = n0 + 3
                    if g + 1 < GROUPS:
                        for kq in range(1, 4):
                            e = n1 - 1 - n0
                            hidden(n1, g, slice(e, e + 1))
                            lows(n1, (0, 1, 2))
                            hidden_low(n1)
                            gather_part(rnd, g + 1, kq)
                            lows(n1, (3, 4, 5))
                            n1 += 1
                    with dve.Fori(n1, n0 + EPG) as n:
                        turn(n, g, bass.ds(n - (n0 + 1), 1))
                n1 = EPG * GROUPS * (rnd + 1)
                hidden(n1, GROUPS - 1, slice(EPG - 1, EPG))
                for j in range(2):
                    dve.wait_ge(d_hi, 2 * n1 - 1 + j)
                    v.tensor_tensor(mlo[j], mraw[j], mhi[(4 + j) % 3].bitcast(F32), ALU.subtract).then_inc(d_lo, 1)
                    if j == 0:
                        hidden_low(n1)
                store(GROUPS * (rnd + 1) - 1)
                scatter(rnd, GROUPS - 1)

            expert_round(0)
            dve.wait_ge(flag_ready, 1)
            more = dve.value_load(flag[0:1, 0:1], min_val=0, max_val=1)
            with dve.If(more > 0):
                for rnd in range(1, ROUNDS):
                    expert_round(rnd)
                dve.wait_ge(ln2_ld, 32 * ROUNDS)
            tail = sem("final_chain")
            done = [0]

            def final_link(ins):
                done[0] += 1
                ins.then_inc(tail, 1)

            def final_statistics(i):
                tt = NORM_ORDER[i]
                tn = TOK[tt][1]
                for j in range(4):
                    final_link(v.bn_stats(stats[0:tn, tt, j, :], atok[0:tn, tt, j * 512:(j + 1) * 512]))
                dve.wait_ge(tail, done[0])
                final_link(v.bn_aggr(mv[0:tn, tt, :], stats[0:tn, tt, :, :].rearrange("p a b -> p (a b)")))
                dve.wait_ge(tail, done[0])
                v.tensor_scalar(rstd[0:tn, tt:tt + 1], mv[0:tn, tt, 1:2], LN_EPS, None, ALU.add).then_inc(f_var, 1)

            def final_scalars(i):
                tt = NORM_ORDER[i]
                tn = TOK[tt][1]
                dve.wait_ge(f_sq, i + 1)
                final_link(v.reciprocal(rstd[0:tn, tt:tt + 1], rstd[0:tn, tt:tt + 1]))
                dve.wait_ge(tail, done[0])
                v.scalar_tensor_tensor(out=nmr[0:tn, tt:tt + 1], in0=mv[0:tn, tt, 0:1], scalar=-1.0,
                                       in1=rstd[0:tn, tt:tt + 1], op0=ALU.mult, op1=ALU.mult).then_inc(f_nmr, 1)

            def final_gain_bias(i):
                tt = NORM_ORDER[i]
                dve.wait_ge(f_norm, i + 1)
                v.tensor_tensor(atok[:, tt, :], atok[:, tt, :], ln2[:, 0, :], ALU.mult).then_inc(gained, 1)
                dve.wait_ge(gained, 2 + i)
                v.tensor_tensor(atok[:, tt, :], atok[:, tt, :], ln2[:, 1, :], ALU.add).then_inc(f_out, 1)

            dve.wait_ge(ln2_ld, 32)
            v.memset(told, 0.0).then_inc(final_vectors, 1)
            final_statistics(0)
            final_scalars(0)
            final_statistics(1)
            final_scalars(1)
            final_statistics(2)
            final_scalars(2)
            final_gain_bias(1)
            final_gain_bias(2)


_INS = ["x_prompt", "x_sample", "p_prompt", "p_sample", "state_s5_re", "state_s5_im", "state_hgrn", "w_in",
        "s5_lambda_re", "s5_lambda_im", "s5_log_dt", "s5_b_re", "s5_b_im", "s5_c_re", "s5_c_im", "s5_d",
        "s5_w_glu", "hg_lower_bounds", "hg_norm_gain", "w_branch_a", "w_branch_b", "w_out", "ln1_gain",
        "ln1_bias", "w_group_router", "b_group_router", "w_expert_router", "b_expert_router", "w_exp_gate",
        "w_exp_up", "w_exp_down", "w_ple_proj", "w_ple_gate", "ln2_gain", "ln2_bias"]
_OUTS = [(1, T, D), (NB, 1, D), (1, 1, 64, 64), (1, 1, 64, 64), (1, 1, HEADS, 128, 128),
         (1, NB, 64, 64), (1, NB, 64, 64), (1, NB, HEADS, 128, 128)]


def kernel(**inputs):
    import concourse.bacc as _bacc
    from concourse.bass_utils import run_bass_kernel_spmd as _run

    nc = _bacc.Bacc("TRN2", target_bir_lowering=False, num_devices=1, dynamic_dma_scratch_size=8192)
    arrays, args = {}, {}
    for name in _INS + ["consts"]:
        a = shape_constants() if name == "consts" else np.ascontiguousarray(inputs[name])
        arrays[f"in_{name}"] = a
        args[name] = nc.dram_tensor(f"in_{name}", a.shape, mybir.dt.from_np(a.dtype), kind="ExternalInput").ap()
    outs = [nc.dram_tensor(f"out_{i}", shape, F32, kind="ExternalOutput").ap() for i, shape in enumerate(_OUTS)]
    build(nc, args, outs)
    r = _run(nc, [arrays], core_ids=[0])
    return tuple(r.results[0][f"out_{i}"] for i in range(len(_OUTS)))
```
